# Optimizing a Trainium2 kernel written in Bass

```python
import jax
import jax.numpy as jnp
from jax import lax
import numpy as np

D_MODEL = 1024
BATCH = 1
SEQ = 1024
DEPTH = 1

MIX_W = D_MODEL
M_HEADS = 4
M_HEAD_DIM = MIX_W // (2 * M_HEADS)
M_W = M_HEADS * M_HEAD_DIM
M_CHUNK = 128
CONV_K = 5
N_GATE = 4 * M_HEADS
A_HEADS = 4
A_V_DIM = (MIX_W - M_W) // A_HEADS
A_NOPE = A_V_DIM
A_ROPE = A_NOPE // 2
A_W = A_HEADS * A_V_DIM
Q_LORA = 3 * D_MODEL // 8
KV_LORA = D_MODEL // 4
ROPE_BASE = 10000.0
Q_BLOCK = 128
N_GROUPS = 4
EXP_PER_GROUP = 8
N_EXPERTS = N_GROUPS * EXP_PER_GROUP
TOP_K = 2
D_EXPERT = D_MODEL // 2
MOE_BLOCK = 128
POS_OFFSET_MAX = 1024
LN_EPS = 1e-5
RMS_EPS = 1e-6
IN_SIZES = (M_W, M_W, M_W, M_W, N_GATE, Q_LORA, KV_LORA, A_ROPE)
N_IN = 4 * M_W + N_GATE + Q_LORA + KV_LORA + A_ROPE

kernel_name = 'hymba_mlstm_mla_hmoe_deepnorm_encoder'

def _split_points(sizes):
    pts, acc = [], 0
    for s in sizes[:-1]:
        acc += s
        pts.append(acc)
    return pts

def _layernorm(x):
    xf = x.astype(jnp.float32)
    mu = jnp.mean(xf, -1, keepdims=True)
    var = jnp.mean(jnp.square(xf - mu), -1, keepdims=True)
    return (xf - mu) * lax.rsqrt(var + LN_EPS)

def _post_ln(z, g, b):
    return (_layernorm(z) * g.astype(jnp.float32) + b.astype(jnp.float32)).astype(z.dtype)

def _rmsnorm(x, g):
    xf = x.astype(jnp.float32)
    y = xf * lax.rsqrt(jnp.mean(jnp.square(xf), -1, keepdims=True) + RMS_EPS)
    return (y * g.astype(jnp.float32)).astype(x.dtype)

def _rope_tables(positions):
    half = A_ROPE // 2
    inv = ROPE_BASE ** (-jnp.arange(half, dtype=jnp.float32) / half)
    ang = positions.astype(jnp.float32)[..., None] * inv
    return jnp.cos(ang), jnp.sin(ang)

def _rope(x, cos, sin):
    xf = x.astype(jnp.float32)
    x1, x2 = jnp.split(xf, 2, axis=-1)
    return jnp.concatenate([x1 * cos - x2 * sin, x2 * cos + x1 * sin], -1).astype(x.dtype)

def _mlstm_scan(q, k, v, i_pre, f_pre):
    B, H, S, dk = q.shape
    dv = v.shape[-1]
    L = M_CHUNK
    nc = S // L
    f32 = jnp.float32

    def chunks(t):
        return jnp.moveaxis(t.reshape((B, H, nc, L) + t.shape[3:]), 2, 0)

    qc, kc, vc = chunks(q.astype(f32)), chunks(k.astype(f32)), chunks(v.astype(f32))
    ic = chunks(i_pre.astype(f32))
    lfc = chunks(jax.nn.log_sigmoid(f_pre.astype(f32)))
    past_mask = jnp.tril(jnp.ones((L, L), dtype=bool))

    def step(carry, inp):
        c_mat, n_vec, m_prev = carry
        qb, kb, vb, ib, lfb = inp
        b = jnp.cumsum(lfb, axis=-1)
        d_log = b[..., :, None] - b[..., None, :] + ib[..., None, :]
        d_log = jnp.where(past_mask, d_log, -jnp.inf)
        inter = b + m_prev[..., None]
        m_t = jnp.maximum(inter, jnp.max(d_log, -1))
        w = jnp.exp(d_log - m_t[..., None])
        s = jnp.einsum('bhtd,bhsd->bhts', qb, kb) * w
        a = jnp.exp(inter - m_t)
        num = a[..., None] * jnp.einsum('bhtd,bhde->bhte', qb, c_mat) + jnp.einsum('bhts,bhse->bhte', s, vb)
        den = a * jnp.einsum('bhtd,bhd->bht', qb, n_vec) + jnp.sum(s, -1)
        h = num / jnp.maximum(jnp.abs(den), jnp.exp(-m_t))[..., None]
        b_end = b[..., -1]
        g = b_end[..., None] - b + ib
        m_new = jnp.maximum(b_end + m_prev, jnp.max(g, -1))
        wg = jnp.exp(g - m_new[..., None])
        decay = jnp.exp(b_end + m_prev - m_new)
        kw = kb * wg[..., None]
        c_new = decay[..., None, None] * c_mat + jnp.einsum('bhsd,bhse->bhde', kw, vb)
        n_new = decay[..., None] * n_vec + jnp.sum(kw, axis=2)
        return (c_new, n_new, m_new), h

    init = (jnp.zeros((B, H, dk, dv), f32), jnp.zeros((B, H, dk), f32), jnp.zeros((B, H), f32))
    _, h = lax.scan(step, init, (qc, kc, vc, ic, lfc))
    return jnp.moveaxis(h, 0, 2).reshape(B, H, S, dv)

def _block_attention(q_nope, q_rope, k_nope, k_rope, v):
    B, S, H, _ = q_nope.shape
    dv = v.shape[-1]
    nb = S // Q_BLOCK
    scale = (A_NOPE + A_ROPE) ** -0.5

    def to_blocks(t):
        return jnp.swapaxes(t.reshape((B, nb, Q_BLOCK) + t.shape[2:]), 0, 1)

    def attend(blk):
        qn, qr = blk
        s = jnp.einsum('bqhd,bkhd->bhqk', qn, k_nope) + jnp.einsum('bqhr,bkr->bhqk', qr, k_rope)
        p = jax.nn.softmax(s.astype(jnp.float32) * scale, axis=-1)
        return jnp.einsum('bhqk,bkhd->bqhd', p.astype(v.dtype), v)

    out = lax.map(attend, (to_blocks(q_nope), to_blocks(q_rope)))
    return jnp.swapaxes(out, 0, 1).reshape(B, S, H * dv)

def _mixer(u, cos, sin, w_in, conv_w, conv_b, gate_b, mh_norm_g, q_norm_g, kv_norm_g,
           w_uq, w_ukv, attn_norm_g, w_out):
    B, S, _ = u.shape
    dt = u.dtype
    proj = u @ w_in
    qm, km, vm, om, gates, cq, ckv, kr = jnp.split(proj, _split_points(IN_SIZES), axis=-1)

    qk = jnp.concatenate([qm, km], -1)
    qk = lax.conv_general_dilated(qk, conv_w[:, None, :], window_strides=(1,),
                                  padding=[(CONV_K // 2, CONV_K // 2)],
                                  dimension_numbers=('NWC', 'WIO', 'NWC'),
                                  feature_group_count=2 * M_W) + conv_b
    qm, km = jnp.split(jax.nn.silu(qk), 2, axis=-1)

    def heads(t):
        return t.reshape(B, S, M_HEADS, M_HEAD_DIM).transpose(0, 2, 1, 3)

    q = heads(qm) * (M_HEAD_DIM ** -0.5)
    k = heads(km)
    v = heads(vm)
    g = gates.astype(jnp.float32).reshape(B, S, 4, M_HEADS) + gate_b.astype(jnp.float32)
    i_fw, f_fw, i_bw, f_bw = g.transpose(2, 0, 3, 1)
    h_fw = _mlstm_scan(q, k, v, i_fw, f_fw)
    flip = lambda t: jnp.flip(t, axis=2)
    h_bw = flip(_mlstm_scan(flip(q), flip(k), flip(v), flip(i_bw), flip(f_bw)))
    h = (h_fw + h_bw).transpose(0, 2, 1, 3)
    mu = jnp.mean(h, -1, keepdims=True)
    var = jnp.mean(jnp.square(h - mu), -1, keepdims=True)
    h = (h - mu) * lax.rsqrt(var + LN_EPS) * mh_norm_g.astype(jnp.float32).reshape(M_HEADS, M_HEAD_DIM)
    h_m = (jax.nn.sigmoid(om.astype(jnp.float32)) * h.reshape(B, S, M_W)).astype(dt)

    cq = _rmsnorm(cq, q_norm_g)
    qa = (cq @ w_uq).reshape(B, S, A_HEADS, A_NOPE + A_ROPE)
    q_nope, q_rope = qa[..., :A_NOPE], qa[..., A_NOPE:]
    q_rope = _rope(q_rope, cos[:, :, None, :], sin[:, :, None, :])
    ckv = _rmsnorm(ckv, kv_norm_g)
    kv = (ckv @ w_ukv).reshape(B, S, A_HEADS, A_NOPE + A_V_DIM)
    k_nope, v_a = kv[..., :A_NOPE], kv[..., A_NOPE:]
    k_rope = _rope(kr, cos, sin)
    o_a = _block_attention(q_nope, q_rope, k_nope, k_rope, v_a)
    h_a = _rmsnorm(o_a, attn_norm_g)

    return jnp.concatenate([h_m, h_a], -1) @ w_out

def _hier_moe(u, w_rg, b_rg, w_re, b_re, w_gate, w_up, w_down):
    B, S, D = u.shape
    dt = u.dtype
    T = B * S
    A = T * TOP_K
    f32 = jnp.float32
    xt = u.reshape(T, D)
    g_logits = (xt @ w_rg).astype(f32) + b_rg.astype(f32)
    g_prob = jax.nn.softmax(g_logits, -1)
    _, g_idx = lax.top_k(g_logits, 1)
    g_w = jnp.take_along_axis(g_prob, g_idx, axis=1)
    e_logits = ((xt @ w_re).astype(f32) + b_re.astype(f32)).reshape(T, N_GROUPS, EXP_PER_GROUP)
    e_in = jnp.take_along_axis(e_logits, g_idx[:, :, None], axis=1)[:, 0]
    top_v, top_i = lax.top_k(e_in, TOP_K)
    w_pair = jax.nn.softmax(top_v, -1) * g_w
    eid = (g_idx * EXP_PER_GROUP + top_i).reshape(A)
    tok = jnp.repeat(jnp.arange(T, dtype=jnp.int32), TOP_K)
    wts = w_pair.reshape(A)
    order = jnp.argsort(eid)
    se, stok, sw = eid[order], tok[order], wts[order]
    counts = jnp.bincount(eid, length=N_EXPERTS)
    starts = jnp.cumsum(counts) - counts
    pcounts = (counts + MOE_BLOCK - 1) // MOE_BLOCK * MOE_BLOCK
    pends = jnp.cumsum(pcounts)
    pstarts = pends - pcounts
    dest = pstarts[se] + (jnp.arange(A) - starts[se])
    n_slots = A + N_EXPERTS * MOE_BLOCK
    n_blocks = n_slots // MOE_BLOCK
    slot_tok = jnp.full((n_slots,), T, jnp.int32).at[dest].set(stok)
    slot_w = jnp.zeros((n_slots,), f32).at[dest].set(sw)
    x_pad = jnp.concatenate([xt, jnp.zeros((1, D), dt)], 0)
    xbuf = x_pad[slot_tok].reshape(n_blocks, MOE_BLOCK, D)
    block_e = jnp.minimum(jnp.searchsorted(pends, jnp.arange(n_blocks) * MOE_BLOCK, side='right'),
                          N_EXPERTS - 1)

    def run_block(args):
        xb, e = args
        hdn = jax.nn.silu(xb @ w_gate[e]) * (xb @ w_up[e])
        return hdn @ w_down[e]

    out = lax.map(run_block, (xbuf, block_e)).reshape(n_slots, D)
    y = jnp.zeros((T + 1, D), dt).at[slot_tok].add(out * slot_w[:, None].astype(dt))[:T]
    return y.reshape(B, S, D)

def setup_inputs(seed: int = 0) -> dict:
    key = jax.random.key(seed)
    ks = iter(jax.random.split(key, 48))
    f32 = jnp.float32
    L, D = DEPTH, D_MODEL
    beta = (8.0 * DEPTH) ** -0.25

    def nrm(shape, scale):
        return scale * jax.random.normal(next(ks), shape, f32)

    x = nrm((BATCH, SEQ, D), 1.0)
    c = nrm((BATCH, D), 1.0)
    positions = (jnp.arange(SEQ, dtype=jnp.int32)[None, :]
                 + jax.random.randint(next(ks), (BATCH, 1), 0, POS_OFFSET_MAX, dtype=jnp.int32))
    fb = jnp.linspace(3.0, 6.0, M_HEADS, dtype=f32)
    zb = jnp.zeros((M_HEADS,), f32)
    gate_base = jnp.stack([zb, fb, zb, fb])
    return {
        'x': x,
        'c': c,
        'positions': positions,
        'w_ada': nrm((L, D, 6 * D), 0.5 * D ** -0.5),
        'b_ada': nrm((L, 6 * D), 0.02),
        'w_in': nrm((L, D, N_IN), D ** -0.5),
        'conv_w': nrm((L, CONV_K, 2 * M_W), CONV_K ** -0.5),
        'conv_b': nrm((L, 2 * M_W), 0.02),
        'gate_b': gate_base[None] + nrm((L, 4, M_HEADS), 0.1),
        'mh_norm_g': 1.0 + nrm((L, M_W), 0.02),
        'q_norm_g': 1.0 + nrm((L, Q_LORA), 0.02),
        'kv_norm_g': 1.0 + nrm((L, KV_LORA), 0.02),
        'w_uq': nrm((L, Q_LORA, A_HEADS * (A_NOPE + A_ROPE)), Q_LORA ** -0.5),
        'w_ukv': nrm((L, KV_LORA, A_HEADS * (A_NOPE + A_V_DIM)), KV_LORA ** -0.5),
        'attn_norm_g': 1.0 + nrm((L, A_W), 0.02),
        'w_out': nrm((L, MIX_W, D), beta * MIX_W ** -0.5),
        'ln1_g': 1.0 + nrm((L, D), 0.02),
        'ln1_b': nrm((L, D), 0.02),
        'w_rg': nrm((L, D, N_GROUPS), D ** -0.5),
        'b_rg': nrm((L, N_GROUPS), 0.01),
        'w_re': nrm((L, D, N_EXPERTS), D ** -0.5),
        'b_re': nrm((L, N_EXPERTS), 0.01),
        'w_gate': nrm((L, N_EXPERTS, D, D_EXPERT), D ** -0.5),
        'w_up': nrm((L, N_EXPERTS, D, D_EXPERT), D ** -0.5),
        'w_down': nrm((L, N_EXPERTS, D_EXPERT, D), beta * D_EXPERT ** -0.5),
        'ln2_g': 1.0 + nrm((L, D), 0.02),
        'ln2_b': nrm((L, D), 0.02),
    }

def reference(x, c, positions, w_ada, b_ada, w_in, conv_w, conv_b, gate_b, mh_norm_g,
              q_norm_g, kv_norm_g, w_uq, w_ukv, attn_norm_g, w_out, ln1_g, ln1_b,
              w_rg, b_rg, w_re, b_re, w_gate, w_up, w_down, ln2_g, ln2_b):
    dt = x.dtype
    alpha = (2.0 * DEPTH) ** 0.25
    cos, sin = _rope_tables(positions)
    c_act = jax.nn.silu(c)
    for l in range(DEPTH):
        mod = c_act @ w_ada[l] + b_ada[l]
        sh1, sc1, g1, sh2, sc2, g2 = jnp.split(mod, 6, axis=-1)
        u = (_layernorm(x) * (1.0 + sc1[:, None, :]) + sh1[:, None, :]).astype(dt)
        y = _mixer(u, cos, sin, w_in[l], conv_w[l], conv_b[l], gate_b[l], mh_norm_g[l],
                   q_norm_g[l], kv_norm_g[l], w_uq[l], w_ukv[l], attn_norm_g[l], w_out[l])
        x = _post_ln(alpha * x + (1.0 + g1[:, None, :]) * y, ln1_g[l], ln1_b[l])
        u = (_layernorm(x) * (1.0 + sc2[:, None, :]) + sh2[:, None, :]).astype(dt)
        y = _hier_moe(u, w_rg[l], b_rg[l], w_re[l], b_re[l], w_gate[l], w_up[l], w_down[l])
        x = _post_ln(alpha * x + (1.0 + g2[:, None, :]) * y, ln2_g[l], ln2_b[l])
    return x


_drawn_inputs = setup_inputs


def setup_inputs(seed=0):
    import zlib

    import numpy as np

    out = dict(_drawn_inputs(seed))
    spreads = {}
    factors = {'conv_b': 8.0,
     'mh_norm_g': 22.0,
     'q_norm_g': 8.0,
     'kv_norm_g': 4.097,
     'attn_norm_g': 14.253,
     'b_rg': 8.0,
     'b_re': 5.828,
     'ln2_g': 7.73,
     'ln2_b': 7.83}
    for name, (base, spread) in spreads.items():
        noise = np.random.default_rng([zlib.crc32(name.encode()), seed]).standard_normal(out[name].shape)
        drawn = base * np.exp(spread * noise) if base else spread * noise
        out[name] = jnp.asarray(drawn.astype(out[name].dtype))
    for name, factor in factors.items():
        out[name] = (out[name] * factor).astype(out[name].dtype)
    return out
```

```python
from contextlib import ExitStack

import numpy as np
import concourse.bass as bass
from concourse import mybir

F32 = mybir.dt.float32
I32 = mybir.dt.int32
ALU = mybir.AluOpType
ACT = mybir.ActivationFunctionType
AX = mybir.AxisListType.X

P = 128
D = 1024
T = 1024
TT = T // P
KD = D // P
H = 4
HD = 128
QL, KVL, RO = 384, 256, 64
NTOK = 1744
E, EG, NG = 32, 8, 4
FE = 512
KF = FE // P
NB = (2 * T + E * (P - 1)) // P + 1
LN_EPS, RMS_EPS = 1e-5, 1e-6
ALPHA = 2.0 ** 0.25
QSCALE = HD ** -0.5
ASCALE = (HD + RO) ** -0.5
BIG = 1e30
OOB = 4096

C_ID, C_UFW, C_UBW, C_E127, C_E0, C_ONE, C_MFW, C_MBW, C_US = (i * P for i in range(9))
C_SEL = 9 * P
C_IM99 = C_SEL + H * P
C_INV = C_IM99 + 32
C_IOTA = C_INV + 32
C_END = C_IOTA + NB


def constants():
    c = np.zeros((P, C_END), np.float32)
    s, t = np.arange(P)[:, None], np.arange(P)[None, :]
    c[:, C_ID:C_ID + P] = s == t
    c[:, C_UFW:C_UFW + P] = s <= t
    c[:, C_UBW:C_UBW + P] = s >= t
    c[P - 1, C_E127:C_E127 + P] = 1
    c[0, C_E0:C_E0 + P] = 1
    c[:, C_ONE:C_ONE + P] = 1
    c[:, C_MFW:C_MFW + P] = np.where(s <= t, 0, BIG)
    c[:, C_MBW:C_MBW + P] = np.where(s >= t, 0, BIG)
    c[:, C_US:C_US + P] = s < t
    for h in range(H):
        c[h, C_SEL + h * P:C_SEL + (h + 1) * P] = 1
    c[:, C_IM99:C_IM99 + 32] = np.arange(32) - 99
    c[:, C_INV:C_INV + 32] = np.float32(10000.0) ** (-np.arange(32, dtype=np.float32) / np.float32(32))
    c[:, C_IOTA:C_IOTA + NB] = np.arange(NB)
    return c


class Chain:

    def __init__(self, eng, sem):
        self.eng, self.sem, self.n, self.off = eng, sem, 0, 0

    def link(self, ins):
        ins.then_inc(self.sem, 1)
        self.n += 1
        self.eng.wait_ge(self.sem, self.off + self.n if self.n else self.off)

    def enter(self, i, per):
        self.base, self.per = self.n, per
        self.off = i * per

    def leave(self, count):
        assert self.n - self.base == self.per, (self.n - self.base, self.per)
        self.n = self.base + self.per * count
        self.off = 0


class Kernel:
    def __init__(self, nc, ins, out):
        self.nc, self.i, self.out = nc, ins, out
        self.ctx = ExitStack()
        self.live = []
        self.scratch_dram()

    def sb(self, name, shape, dt=F32, ctx=None):
        return (ctx or self.ctx).enter_context(self.nc.sbuf_tensor(name, shape, dt))

    def sem(self, name):
        self.live.append(self.nc.alloc_semaphore(name=name))
        return self.live[-1]

    def clear_semaphores(self):
        self.nc.clear_and_free_semaphores(self.live)
        self.nc.all_engine_barrier()
        self.live = []

    def scratch_dram(self):
        d = lambda n, s, dt=F32: self.nc.dram_tensor(n, s, dt, kind="Internal").ap()
        self.u2d = d("u2_rows", (T, D))
        self.x1d = d("x1_rows", (T, D))
        self.slotmap = d("slot_to_assignment", (NB * P, 1), I32)
        self.ybuf = d("expert_rows", (2 * T, D))

    def build(self):
        nc = self.nc
        with self.ctx:
            self.ps = self.ctx.enter_context(nc.psum_tensor("ps", [P, 8, 512], F32))
            self.cst = self.sb("cst", [P, C_END])
            self.mod = self.sb("mod", [P, 6, D])
            self.lg = self.sb("logits", [P, TT, NG + E])
            with ExitStack() as mix:
                self.rlat = self.sb("lat_rstd", [P, 2, TT], ctx=mix)
                self.tab = self.sb("sin_cos", [P, 2, TT, 32], ctx=mix)
                self.kr2 = self.sb("kr_rotated", [P, TT, 2, RO], ctx=mix)
                self.hm = self.sb("mlstm_rows", [P, TT, H * HD], ctx=mix)
                self.cq = self.sb("cq", [P, TT, QL], ctx=mix)
                self.ckv = self.sb("ckv", [P, TT, KVL], ctx=mix)
                self.kr = self.sb("kr", [P, TT, RO], ctx=mix)
                self.gt = self.sb("gates", [P, TT, 16], ctx=mix)
                with ExitStack() as up:
                    self.vaug = self.sb("vaug", [P, TT, H, HD + 1], ctx=up)
                    self.uT = self.sb("uT", [P, KD, T], ctx=up)
                    with ExitStack() as first:
                        self.s_wt = self.sem("w_in_tokens_loaded")
                        self.wt = self.sb("w_in_tok", [P, KD, NTOK], ctx=first)
                        self.modulation()
                        self.project_tokens()
                    self.qkT = self.sb("qkT", [P, 8, T], ctx=up)
                    self.project_channels()
                    self.mlstm_gates(up)
                    self.mlstm(up)
                    self.mlstm_norm()
                self.clear_semaphores()
                self.s_wo = self.sem("w_out_loaded")
                self.wo = self.sb("w_out", [P, KD, D], ctx=mix)
                self.oa = self.sb("attn_rows", [P, TT, H * HD], ctx=mix)
                self.attention()
                self.output_projection()
            self.clear_semaphores()
            self.routing(self.ctx)
            self.experts()
            self.combine()

    def c(self, at, n=P, parts=P):
        return self.cst[0:parts, at:at + n]

    def modulation(self):
        nc, cst, mod, ps = self.nc, self.cst, self.mod, self.ps
        s_const, s_c, s_cact = self.sem("const_loaded"), self.sem("c_loaded"), self.sem("c_activated")
        s_bias = self.sem("b_ada_loaded")
        s_w = [self.sem(f"w_ada_loaded{j}") for j in range(2)]
        s_mm = [self.sem(f"mod_product_ready{j}") for j in range(2)]
        s_add = [self.sem(f"mod_added{j}") for j in range(2)]
        s_v = self.sem("mod_dve")
        modf = mod[:].rearrange("p a d -> p (a d)")
        w_ada = self.i["w_ada"].rearrange("(p k) n -> p k n", k=KD)
        with ExitStack() as x, nc.Block() as block:
            cc = self.sb("c_cols", [P, KD], ctx=x)
            ca = self.sb("c_act", [P, KD], ctx=x)
            w = self.uT[:].rearrange("p k t -> p (k t)").rearrange("p (j k n) -> p j k n", j=2, k=KD)

            @block.sync
            def _(sp):
                sp.dma_start(cc[:], self.i["c"].rearrange("(p k) -> p k", k=KD)).then_inc(s_c, 16)
                with sp.Fori(0, 6) as i:
                    for j in range(2):
                        sp.wait_ge(s_mm[j], i + 1)
                        sp.dma_start(w[:, j], w_ada[:, :, bass.ds((i * 2 + j) * 512, 512)]).then_inc(s_w[j], 16)
                w_t = self.i["w_in"].rearrange("(k p) n -> p k n", p=P)[:, :, 1024:]
                for k in range(KD):
                    sp.dma_start(self.wt[:, k], w_t[:, k]).then_inc(self.s_wt, 16)

            @block.scalar
            def _(act):
                act.dma_start(cst[:], self.i["consts"]).then_inc(s_const, 16)
                act.dma_start(modf, self.i["b_ada"].partition_broadcast(P)).then_inc(s_bias, 16)
                act.wait_ge(s_c, 16)
                nc.scalar.activation(ca[:], cc[:], ACT.Silu).then_inc(s_cact, 1)
                act.wait_ge(s_const, 16)

            @block.tensor
            def _(pe):
                for j in range(2):
                    pe.sem_inc(s_mm[j], 1)
                pe.wait_ge(s_cact, 1)
                with pe.Fori(0, 6) as i:
                    for j in range(2):
                        pe.wait_ge(s_w[j], i * 16 + 16)
                        pe.wait_ge(s_add[j], i + 1)
                        for k in range(KD):
                            mm = nc.tensor.matmul(ps[:, j, :], ca[:, k:k + 1].to_broadcast([P, P]), w[:, j, k, :],
                                                  start=k == 0, stop=k == KD - 1)
                        mm.then_inc(s_mm[j], 1)

            @block.vector
            def _(dve):
                ch = Chain(dve, s_v)
                for j in range(2):
                    dve.sem_inc(s_add[j], 1)
                dve.wait_ge(s_bias, 16)
                with dve.Fori(0, 6) as i:
                    for j in range(2):
                        dve.wait_ge(s_mm[j], i + 2)
                        piece = modf[:, bass.ds((i * 2 + j) * 512, 512)]
                        nc.vector.tensor_tensor(piece, piece, ps[:, j, :], ALU.add).then_inc(s_add[j], 1)
                for j in range(2):
                    dve.wait_ge(s_add[j], 7)
                ch.link(nc.vector.tensor_scalar_add(mod[:, 1:3, :], mod[:, 1:3, :], 1.0))
                ch.link(nc.vector.tensor_scalar_add(mod[:, 4:6, :], mod[:, 4:6, :], 1.0))

    def project_tokens(self):
        nc, ps, mod = self.nc, self.ps, self.mod
        s_x = [self.sem(f"x_loaded{j}") for j in range(2)]
        s_xfree = [self.sem(f"x_used{j}") for j in range(2)]
        s_wt, wt = self.s_wt, self.wt
        s_var, s_std = self.sem("var1_ready"), self.sem("std1_ready")
        s_u = [self.sem(f"u_ready{j}") for j in range(2)]
        s_tr, s_uT, s_uTf = self.sem("u_transposed"), self.sem("uT_tile_ready"), self.sem("uT_full_copied")
        s_g = [self.sem(f"proj_group{g}") for g in range(4)]
        s_e = [self.sem(f"proj_evacuated{g}") for g in range(4)]
        s_v, s_one = self.sem("proj_dve"), self.sem("ones_col")
        x_t = self.i["x"].rearrange("(t p) d -> t p d", p=P)
        cols = [(0, 512), (512, 512), (1024, 400), (1424, 320)]
        with ExitStack() as x, nc.Block() as block:
            xs = self.sb("x_tiles", [P, 2, D], ctx=x)
            un = self.sb("u_tiles", [P, 2, D], ctx=x)
            uTt = self.sb("uT_tiles", [P, 2, KD, P], ctx=x)
            st = self.sb("st1", [P, 2, 6], ctx=x)
            mv = self.sb("mv1", [P, 2], ctx=x)
            ve = self.sb("ve1", [P, 2], ctx=x)
            one = self.sb("one1", [P, 1], ctx=x)
            ident = self.c(C_ID)

            @block.sync
            def _(sp):
                with sp.Fori(0, TT // 2) as i:
                    for j in range(2):
                        sp.wait_ge(s_xfree[j], i + 1)
                        sp.dma_start(xs[:, j], x_t[bass.ds(i * 2 + j, 1)].rearrange("a p d -> p (a d)")).then_inc(s_x[j], 16)

            @block.gpsimd
            def _(pool):
                nc.gpsimd.memset(self.vaug[:, :, :, HD:HD + 1], 1.0).then_inc(s_one, 1)

            @block.vector
            def _(dve):
                ch = Chain(dve, s_v)
                for j in range(2):
                    dve.sem_inc(s_xfree[j], 1)
                for g in (0, 2):
                    dve.sem_inc(s_e[g], 1)

                def front(t, j, i):
                    dve.wait_ge(s_x[j], i * 16 + 16)
                    ch.link(nc.vector.bn_stats(st[:, 0, :], xs[:, j, 0:512]))
                    ch.link(nc.vector.bn_stats(st[:, 1, :], xs[:, j, 512:1024]))
                    nc.vector.tensor_copy(one[:], ident[:, 0:1])
                    ch.link(nc.vector.bn_aggr(mv[:], st[:].rearrange("p a b -> p (a b)")))
                    nc.vector.tensor_scalar_add(ve[:, 0:1], mv[:, 1:2], LN_EPS).then_inc(s_var, 1)
                    dve.wait_ge(s_std, t + 1)
                    ch.link(nc.vector.reciprocal(ve[:, 1:2], ve[:, 1:2]))
                    dve.wait_ge(s_uTf, t + 1)
                    nc.vector.tensor_scalar(un[:, j], xs[:, j], mv[:, 0:1], ve[:, 1:2], ALU.subtract, ALU.mult).then_inc(s_xfree[j], 1)
                    dve.wait_ge(s_xfree[j], i + 2)
                    ch.link(nc.vector.tensor_tensor(un[:, j], un[:, j], mod[:, 1, :], ALU.mult))
                    nc.vector.tensor_tensor(un[:, j], un[:, j], mod[:, 0, :], ALU.add).then_inc(s_u[j], 1)

                def back(t):
                    dve.wait_ge(s_g[0], t + 1)
                    nc.vector.tensor_copy(self.vaug[:, bass.ds(t, 1), :, 0:HD],
                                          ps[:, 2, :].rearrange("p (a h d) -> p a h d", a=1, h=H)).then_inc(s_e[0], 1)
                    dve.wait_ge(s_g[2], t + 1)
                    nc.vector.tensor_copy(self.gt[:, bass.ds(t, 1), :],
                                          ps[:, 4, 0:16].rearrange("p (a d) -> p a d", a=1))
                    nc.vector.tensor_copy(self.cq[:, bass.ds(t, 1), :],
                                          ps[:, 4, 16:400].rearrange("p (a d) -> p a d", a=1)).then_inc(s_e[2], 1)

                front(0, 0, 0)
                with dve.Fori(0, TT // 2 - 1) as i:
                    ch.enter(i, 10)
                    front(i * 2 + 1, 1, i)
                    back(i * 2)
                    front(i * 2 + 2, 0, i + 1)
                    back(i * 2 + 1)
                    ch.leave(TT // 2 - 1)
                front(TT - 1, 1, TT // 2 - 1)
                back(TT - 2)
                back(TT - 1)

            @block.scalar
            def _(act):
                act.sem_inc(s_uTf, 2)
                act.sem_inc(s_uT, 1)
                for g in (1, 3):
                    act.sem_inc(s_e[g], 1)

                def std(t):
                    act.wait_ge(s_var, t + 1)
                    nc.scalar.activation(ve[:, 1:2], ve[:, 0:1], ACT.Sqrt).then_inc(s_std, 1)

                def turned(t, j):
                    act.wait_ge(s_tr, t + 1)
                    act.wait_ge(s_g[3], t + 1)
                    nc.scalar.copy(uTt[:, j].rearrange("p k t -> p (k t)"), ps[:, 0:2, :].rearrange("p a b -> p (a b)")).then_inc(s_uT, 1)
                    nc.scalar.copy(self.uT[:, :, bass.ds(t * P, P)],
                                   ps[:, 0:2, :].rearrange("p a (b t) -> p (a b) t", t=P)).then_inc(s_uTf, 1)

                def evacuate1(t):
                    act.wait_ge(s_g[1], t + 1)
                    nc.scalar.copy(self.hm[:, bass.ds(t, 1), :],
                                   ps[:, 3, :].rearrange("p (a d) -> p a d", a=1)).then_inc(s_e[1], 1)

                def evacuate3(t):
                    act.wait_ge(s_g[3], t + 3)
                    nc.scalar.copy(self.ckv[:, bass.ds(t, 1), :],
                                   ps[:, 5, 0:256].rearrange("p (a d) -> p a d", a=1))
                    nc.scalar.copy(self.kr[:, bass.ds(t, 1), :],
                                   ps[:, 5, 256:320].rearrange("p (a d) -> p a d", a=1)).then_inc(s_e[3], 1)

                def step(t, j):
                    std(t + 1)
                    evacuate1(t)
                    turned(t + 1, 1 - j)
                    evacuate3(t)

                std(0)
                turned(0, 0)
                with act.Fori(0, TT // 2 - 1) as i:
                    step(i * 2, 0)
                    step(i * 2 + 1, 1)
                step(TT - 2, 0)
                evacuate1(TT - 1)
                evacuate3(TT - 1)
                act.wait_ge(s_e[3], TT + 1)

            @block.tensor
            def _(pe):
                pe.sem_inc(s_g[3], 2)
                pe.wait_ge(s_wt, 16 * KD)

                def turn(t, j, i):
                    pe.wait_ge(s_u[j], i + 1)
                    pe.wait_ge(s_uTf, t + 2)
                    for k in range(KD):
                        mm = nc.tensor.transpose(ps[:, k // 4, (k % 4) * P:(k % 4 + 1) * P], un[:, j, k * P:(k + 1) * P], ident)
                    mm.then_inc(s_tr, 1)

                def products(t, j, groups):
                    if 0 in groups:
                        pe.wait_ge(s_uT, t + 2)
                    for g in groups:
                        c0, n = cols[g]
                        pe.wait_ge(s_e[g], t + 1)
                        for k in range(KD):
                            mm = nc.tensor.matmul(ps[:, 2 + g, 0:n], uTt[:, j, k, :], wt[:, k, c0:c0 + n],
                                                  start=k == 0, stop=k == KD - 1)
                        mm.then_inc(s_g[g], 1)

                def step(t, j, i):
                    products(t, j, (0, 1))
                    turn(t + 1, 1 - j, i)
                    products(t, j, (2, 3))

                turn(0, 0, 0)
                with pe.Fori(0, TT // 2 - 1) as i:
                    step(i * 2, 0, i)
                    step(i * 2 + 1, 1, i + 1)
                step(TT - 2, 0, TT // 2 - 1)
                products(TT - 1, 1, (0, 1, 2, 3))

    def project_channels(self):
        nc, ps = self.nc, self.ps
        s_w = [self.sem(f"w_qk_loaded{j}") for j in range(2)]
        s_mm = [self.sem(f"qk_product{j}") for j in range(2)]
        s_raw = [self.sem(f"qk_raw{j}") for j in range(2)]
        s_cv = [self.sem(f"qk_conv{j}") for j in range(2)]
        s_act = [self.sem(f"qk_silu{j}") for j in range(2)]
        s_cw, s_v, s_pad = self.sem("conv_w_loaded"), self.sem("conv_dve"), self.sem("conv_pad")
        s_pos, s_sq, s_ms, s_std, s_tr, s_sin = (self.sem(n) for n in ("pos_loaded", "lat_squared", "lat_var", "lat_std", "angles_reduced", "sines"))
        w_q = self.i["w_in"].rearrange("(k p) n -> p k n", p=P)
        with ExitStack() as x, nc.Block() as block:
            w = self.sb("w_qk", [P, 2, KD, P], ctx=x)
            raw = self.sb("qk_raw", [P, 2, T + 4], ctx=x)
            acc = self.sb("qk_acc", [P, 2, T], ctx=x)
            cw = self.sb("conv_w", [P, 8, 6], ctx=x)
            cwt = self.sb("conv_w_tile", [P, 6], ctx=x)

            pi_ = self.sb("pos_i", [P, TT], I32, ctx=x)
            pf = self.sb("pos_f", [P, TT], ctx=x)
            qkf = self.qkT[:].rearrange("p k t -> p (k t)")
            sq = qkf[:, 0:TT * QL].rearrange("p (t n) -> p t n", t=TT)
            sq2 = qkf[:, TT * QL:TT * (QL + KVL)].rearrange("p (t n) -> p t n", t=TT)
            rest = qkf[:, TT * (QL + KVL):].rearrange("p (a t n) -> p a t n", t=TT, n=32)
            ang, kk, tmp = rest[:, 0], rest[:, 1:3], rest[:, 3]
            MAGIC = 12582912.0
            TWO_PI_HI = 6.28125
            TWO_PI_LO = float(2 * np.pi - 6.28125)

            @block.sync
            def _(sp):
                with nc.allow_non_contiguous_dma("one position to a partition"):
                    sp.dma_start(pi_[:], self.i["positions"].rearrange("(t p) -> p t", p=P)).then_inc(s_pos, 16)
                with nc.allow_non_contiguous_dma("small convolution weights"):
                    for tap in range(5):
                        sp.dma_start(cw[:, :, tap], self.i["conv_w"][tap].rearrange("(c p) -> p c", p=P)).then_inc(s_cw, 16)
                    sp.dma_start(cw[:, :, 5], self.i["conv_b"].rearrange("(c p) -> p c", p=P)).then_inc(s_cw, 16)
                with sp.Fori(0, 4) as i:
                    for j in range(2):
                        sp.wait_ge(s_mm[j], i + 1)
                        sp.dma_start(w[:, j], w_q[:, :, bass.ds((i * 2 + j) * P, P)]).then_inc(s_w[j], 16)

            @block.tensor
            def _(pe):
                for j in range(2):
                    pe.sem_inc(s_mm[j], 1)
                with pe.Fori(0, 4) as i:
                    for j in range(2):
                        pe.wait_ge(s_w[j], i * 16 + 16)
                        pe.wait_ge(s_raw[j], i + 1)
                        for half in range(2):
                            for k in range(KD):
                                mm = nc.tensor.matmul(ps[:, 2 * j + half, :], w[:, j, k, :], self.uT[:, k, half * 512:half * 512 + 512],
                                                      start=k == 0, stop=k == KD - 1)
                        mm.then_inc(s_mm[j], 1)

            @block.scalar
            def _(act):
                for j in range(2):
                    act.sem_inc(s_raw[j], 1)
                    act.sem_inc(s_act[j], 1)
                nc.scalar.activation(sq, self.cq[:], ACT.Square).then_inc(s_sq, 1)
                nc.scalar.activation(sq2, self.ckv[:], ACT.Square).then_inc(s_sq, 1)
                act.wait_ge(s_ms, 1)
                nc.scalar.activation(self.rlat[:], self.rlat[:], ACT.Sqrt).then_inc(s_std, 1)
                act.wait_ge(s_tr, 1)
                nc.scalar.activation(self.tab[:], self.tab[:], ACT.Sin).then_inc(s_sin, 1)
                act.wait_ge(s_pad, 2)
                with act.Fori(0, 4) as i:
                    for j in range(2):
                        act.wait_ge(s_mm[j], i + 2)
                        act.wait_ge(s_cv[j], i + 1)
                        nc.scalar.copy(raw[:, j, 2:T + 2], ps[:, 2 * j:2 * j + 2, :].rearrange("p a b -> p (a b)")).then_inc(s_raw[j], 1)
                        act.wait_ge(s_cv[j], i + 2)
                        nc.scalar.activation(self.qkT[:, bass.ds(i * 2 + j, 1), :], acc[:, j:j + 1, :], ACT.Silu).then_inc(s_act[j], 1)

            @block.vector
            def _(dve):
                ch = Chain(dve, s_v)
                for j in range(2):
                    dve.sem_inc(s_cv[j], 1)
                nc.vector.memset(raw[:, :, 0:2], 0.0).then_inc(s_pad, 1)
                nc.vector.memset(raw[:, :, T + 2:T + 4], 0.0).then_inc(s_pad, 1)
                v = nc.vector
                dve.wait_ge(s_pos, 16)
                ch.link(v.tensor_copy(pf[:], pi_[:]))
                ch.link(v.tensor_tensor(ang, pf[:].unsqueeze(2).to_broadcast([P, TT, 32]),
                                        self.c(C_INV, 32).unsqueeze(1).to_broadcast([P, TT, 32]), ALU.mult))
                ch.link(v.tensor_scalar(kk[:, 0], ang, float(1 / (2 * np.pi)), MAGIC, ALU.mult, ALU.add))
                ch.link(v.tensor_scalar(kk[:, 1], ang, float(1 / (2 * np.pi)), 0.25, ALU.mult, ALU.add))
                ch.link(v.tensor_scalar_add(kk[:, 1], kk[:, 1], MAGIC))
                ch.link(v.tensor_scalar_add(kk, kk, -MAGIC))
                for y in range(2):
                    ch.link(v.scalar_tensor_tensor(out=self.tab[:, y], in0=kk[:, y], scalar=-TWO_PI_HI, in1=ang[:], op0=ALU.mult, op1=ALU.add))
                    ch.link(v.scalar_tensor_tensor(out=self.tab[:, y], in0=kk[:, y], scalar=-TWO_PI_LO, in1=self.tab[:, y], op0=ALU.mult, op1=ALU.add))
                ch.link(v.tensor_scalar_add(self.tab[:, 1], self.tab[:, 1], float(np.pi / 2)))
                v.tensor_scalar(self.tab[:], self.tab[:], 3.1415925, -3.1415925, ALU.min, ALU.max).then_inc(s_tr, 1)
                dve.wait_ge(s_sq, 2)
                ch.link(v.tensor_reduce(self.rlat[:, 0], sq, AX, ALU.add))
                ch.link(v.tensor_reduce(self.rlat[:, 1], sq2, AX, ALU.add))
                ch.link(v.tensor_scalar(self.rlat[:, 0], self.rlat[:, 0], 1.0 / QL, RMS_EPS, ALU.mult, ALU.add))
                v.tensor_scalar(self.rlat[:, 1], self.rlat[:, 1], 1.0 / KVL, RMS_EPS, ALU.mult, ALU.add).then_inc(s_ms, 1)
                dve.wait_ge(s_std, 1)
                ch.link(v.reciprocal(self.rlat[:], self.rlat[:]))
                dve.wait_ge(s_sin, 1)
                x1, x2, sn, cs = self.kr[:, :, 0:32], self.kr[:, :, 32:64], self.tab[:, 0], self.tab[:, 1]
                ch.link(v.tensor_tensor(self.kr2[:, :, 0, 0:32], x1, cs, ALU.mult))
                ch.link(v.tensor_tensor(tmp, x2, sn, ALU.mult))
                ch.link(v.tensor_tensor(self.kr2[:, :, 0, 0:32], self.kr2[:, :, 0, 0:32], tmp, ALU.subtract))
                ch.link(v.tensor_tensor(self.kr2[:, :, 0, 32:64], x2, cs, ALU.mult))
                ch.link(v.tensor_tensor(tmp, x1, sn, ALU.mult))
                ch.link(v.tensor_tensor(self.kr2[:, :, 0, 32:64], self.kr2[:, :, 0, 32:64], tmp, ALU.add))
                ch.link(v.tensor_copy(self.kr2[:, :, 1, :], self.kr2[:, :, 0, :]))
                dve.wait_ge(s_cw, 96)
                with dve.Fori(0, 4) as i:
                    ch.enter(i, 10)
                    for j in range(2):
                        ch.link(nc.vector.tensor_copy(cwt[:].rearrange("p (a b) -> p a b", a=1), cw[:, bass.ds(i * 2 + j, 1), :]))
                        dve.wait_ge(s_raw[j], i + 2)
                        dve.wait_ge(s_act[j], i + 1)
                        ch.link(nc.vector.tensor_scalar(acc[:, j], raw[:, j, 0:T], cwt[:, 0:1], cwt[:, 5:6], ALU.mult, ALU.add))
                        for tap in range(1, 5):
                            op = nc.vector.scalar_tensor_tensor(out=acc[:, j], in0=raw[:, j, tap:tap + T], scalar=cwt[:, tap:tap + 1],
                                                                in1=acc[:, j], op0=ALU.mult, op1=ALU.add)
                            if tap < 4:
                                ch.link(op)
                        op.then_inc(s_cv[j], 1)
                        dve.wait_ge(s_cv[j], i + 2)
                    ch.leave(4)

    def mlstm_gates(self, up):
        nc, ps = self.nc, self.ps
        s_gb, s_v, s_nf, s_e, s_l = (self.sem(n) for n in ("gate_b_loaded", "gates_dve", "neg_abs_f", "exp_f", "ln_f"))
        s_lf, s_b, s_bc = self.sem("log_f_ready"), self.sem("b_product"), self.sem("b_copied")
        s_rows, s_rowc, s_m, s_mc = self.sem("rows_turned"), self.sem("rows_copied"), self.sem("m_rows_ready"), self.sem("m_columns_turned")
        s_mb, s_mb2, s_f, s_fin = self.sem("m_copied"), self.sem("m_end_spread"), self.sem("factors_in"), self.sem("factors_out")
        s_rdy = self.sem("M_rows_ready")
        self.acol = self.sb("a_col", [P, 2, TT, H], ctx=up)
        self.mext = self.sb("m_prev", [P, 2, TT + 2, H], ctx=up)
        self.wg = self.sb("wg", [P, 2, TT, H], ctx=up)
        self.dec = self.sb("decay", [P, 2, TT, H], ctx=up)
        self.emm = self.sb("exp_neg_m", [P, 2, TT, H], ctx=up)
        self.Mrow = self.sb("M_rows", [H, 2, T], ctx=up)
        with ExitStack() as x, nc.Block() as block:
            gb = self.sb("gate_b", [P, 16], ctx=x)
            g2 = self.sb("g_if", [P, 2, 2, TT, H], ctx=x)
            nf = self.sb("nf", [P, 2, TT, H], ctx=x)
            lf = self.sb("lf", [P, 2, TT, H], ctx=x)
            bcol = self.sb("b_col", [P, 2, TT, H], ctx=x)
            mcol = self.sb("m_col", [P, 2, 2, TT, H], ctx=x)
            mend = self.sb("m_end", [P, 2, 2, TT, H], ctx=x)
            rows = self.sb("rows", [H, 3, T], ctx=x)
            mrow = self.sb("m_rows", [H, 2, T], ctx=x)
            flat = lambda a: a.rearrange("p d c h -> p (d c h)")
            gt5 = self.gt[:].rearrange("p c (d y h) -> p y d c h", d=2, y=2)

            @block.sync
            def _(sp):
                sp.dma_start(gb[:], self.i["gate_b"].partition_broadcast(P)).then_inc(s_gb, 16)

            @block.vector
            def _(dve):
                ch = Chain(dve, s_v)
                v = nc.vector
                dve.wait_ge(s_gb, 16)
                gb5 = gb[:].rearrange("p (d y h) -> p y d h", d=2, y=2)
                for y in range(2):
                    for d in range(2):
                        ch.link(v.tensor_tensor(g2[:, y, d], gt5[:, y, d], gb5[:, y, d].unsqueeze(1).to_broadcast([P, TT, H]), ALU.add))
                f = flat(g2[:, 1])
                v.scalar_tensor_tensor(out=flat(nf[:]), in0=f, scalar=-1.0, in1=f, op0=ALU.mult, op1=ALU.min).then_inc(s_nf, 1)
                dve.wait_ge(s_l, 1)
                v.scalar_tensor_tensor(out=flat(lf[:]), in0=f, scalar=0.0, in1=flat(nf[:]), op0=ALU.min, op1=ALU.subtract).then_inc(s_lf, 1)
                dve.wait_ge(s_b, 1)
                v.tensor_copy(flat(bcol[:]), ps[:, 0, 0:64]).then_inc(s_bc, 1)
                dve.wait_ge(s_bc, 1)
                ch.link(v.tensor_tensor(flat(self.acol[:]), flat(g2[:, 0]), flat(bcol[:]), ALU.subtract))
                for d in range(2):
                    dve.wait_ge(s_rows, d + 1)
                    v.tensor_copy(rows[:], ps[0:H, 1:7, :].rearrange("p (q a) n -> p q (a n)", q=3)).then_inc(s_rowc, 1)
                    dve.wait_ge(s_rowc, d + 1)
                    if d == 0:
                        op = v.tensor_tensor_scan(mrow[:, 0, :], rows[:, 0, :], rows[:, 1, :], 0.0, ALU.add, ALU.max)
                    else:
                        op = v.tensor_tensor_scan(mrow[:, 1, :][:, ::-1], rows[:, 0, :][:, ::-1], rows[:, 1, :][:, ::-1], 0.0, ALU.add, ALU.max)
                    op.then_inc(s_m, 1)
                    dve.wait_ge(s_m, d + 1)
                    v.tensor_tensor(self.Mrow[:, d, :], mrow[:, d, :], rows[:, 2, :], ALU.subtract).then_inc(s_rdy, 1)
                    dve.wait_ge(s_rdy, d + 1)
                dve.wait_ge(s_mc, 1)
                ch.link(v.tensor_copy(flat(mcol[:, 0]), ps[:, 0, 0:64]))
                v.tensor_tensor(flat(mcol[:, 1]), flat(mcol[:, 0]), flat(bcol[:]), ALU.subtract).then_inc(s_mb, 1)
                dve.wait_ge(s_mb2, 1)
                ch.link(v.tensor_copy(mend[:].rearrange("p d q c h -> p (d q c h)"), ps[:, 1, 0:128]))
                ch.link(v.memset(self.mext[:], 0.0))
                ch.link(v.tensor_copy(self.mext[:, 0, 2:TT + 1, :], mend[:, 0, 0, 0:TT - 1, :]))
                ch.link(v.tensor_copy(self.mext[:, 1, 1:TT, :], mend[:, 1, 0, 1:TT, :]))
                for d in range(2):
                    ch.link(v.tensor_tensor(self.wg[:, d], self.acol[:, d], mend[:, d, 1], ALU.subtract))
                    op = v.tensor_tensor(self.dec[:, d], self.mext[:, d, 1:TT + 1, :], mend[:, d, 1], ALU.subtract)
                    if d == 0:
                        ch.link(op)
                op.then_inc(s_f, 1)

            @block.scalar
            def _(act):
                act.wait_ge(s_nf, 1)
                nc.scalar.activation(flat(nf[:]), flat(nf[:]), ACT.Exp).then_inc(s_e, 1)
                act.wait_ge(s_e, 1)
                nc.scalar.activation(flat(nf[:]), flat(nf[:]), ACT.Ln, bias=1.0).then_inc(s_l, 1)
                act.wait_ge(s_mb, 1)
                nc.scalar.activation(flat(self.emm[:]), flat(mcol[:, 0]), ACT.Exp, scale=-1.0).then_inc(s_fin, 1)
                act.wait_ge(s_f, 1)
                nc.scalar.activation(flat(self.wg[:]), flat(self.wg[:]), ACT.Exp).then_inc(s_fin, 1)
                nc.scalar.activation(flat(self.dec[:]), flat(self.dec[:]), ACT.Exp).then_inc(s_fin, 1)

            @block.tensor
            def _(pe):
                pe.wait_ge(s_lf, 1)
                for d, u in enumerate((C_UFW, C_UBW)):
                    mm = nc.tensor.matmul(ps[:, 0, d * 32:d * 32 + 32], self.c(u), lf[:, d].rearrange("p c h -> p (c h)"), start=True, stop=True)
                mm.then_inc(s_b, 1)
                pe.wait_ge(s_bc, 1)
                for d in range(2):
                    if d:
                        pe.wait_ge(s_rowc, d)
                    for q, src in enumerate((lf, g2[:, 0], bcol)):
                        for c in range(TT):
                            mm = nc.tensor.matmul(ps[0:H, 1 + 2 * q + c // 4, (c % 4) * P:(c % 4 + 1) * P], src[:, d, c, :], self.c(C_ID),
                                                  start=True, stop=True)
                    mm.then_inc(s_rows, 1)
                pe.wait_ge(s_m, 2)
                for d in range(2):
                    for c in range(TT):
                        mm = nc.tensor.matmul(ps[:, 0, (d * TT + c) * H:(d * TT + c + 1) * H], mrow[:, d, c * P:(c + 1) * P], self.cst[0:H, C_ID:C_ID + H],
                                              start=True, stop=True)
                mm.then_inc(s_mc, 1)
                pe.wait_ge(s_mb, 1)
                pe.wait_ge(s_rowc, 2)
                for d, e in enumerate((C_E127, C_E0)):
                    mm = nc.tensor.matmul(ps[:, 1, d * 64:d * 64 + 64], self.c(e), mcol[:, :, d].rearrange("p q c h -> p q (c h)"), start=True, stop=True)
                mm.then_inc(s_mb2, 1)

    def mlstm(self, up):
        nc, ps = self.nc, self.ps
        N = ("kc", "mb", "sc", "kt", "mask", "z", "w", "y", "a", "p", "q", "kw", "o", "cm", "cn", "h")
        S = {n: [self.sem(f"ml_{n}{d}") for d in range(2)] for n in N}
        s_v, s_c0 = self.sem("ml_dve"), self.sem("ml_state0")
        self.hdir = self.uT[:].rearrange("p (d a) (c n) -> p d (a c) n", d=2, c=2)
        with ExitStack() as x, nc.Block() as block:
            sb = lambda n, s: self.sb(n, s, ctx=x)
            kc, mm_, w, ab, p, q, kw = (sb(n, [P, 2, H, P]) for n in ("kc", "Mm", "W", "ab", "pT", "qs", "kw"))
            cst8 = sb("Caug", [P, 2, H, HD + 1])
            den = sb("den", [P, 2, H])
            hn = HD + 1
            chunk = lambda i, d: i if d == 0 else i * -1 + (TT - 1)

            @block.scalar
            def _(act):
                a = nc.scalar
                with act.Fori(0, TT) as i:
                    for d in range(2):
                        c = chunk(i, d)
                        act.wait_ge(S["kt"][d], i + 1)
                        a.copy(kc[:, d], self.qkT[:, 4:8, bass.ds(c * P, P)]).then_inc(S["kc"][d], 1)
                    for d in range(2):
                        act.wait_ge(S["z"][d], i + 1)
                        act.wait_ge(S["p"][d], i + 1)
                        a.activation(w[:, d], mm_[:, d], ACT.Exp).then_inc(S["w"][d], 1)
                        act.wait_ge(S["y"][d], i + 2)
                        a.activation(ab[:, d], ab[:, d], ACT.Exp).then_inc(S["a"][d], 1)

            @block.tensor
            def _(pe):
                t = nc.tensor
                for n in ("kt", "o", "cm"):
                    for d in range(2):
                        pe.sem_inc(S[n][d], 1)
                pe.wait_ge(s_c0, 1)
                with pe.Fori(0, TT) as i:
                    for d in range(2):
                        c = chunk(i, d)
                        other = i + 1 if d == 0 else i + 2
                        pe.wait_ge(S["y"][1 - d], other)
                        for h in range(H):
                            m = t.matmul(ps[:, 0, h * P:(h + 1) * P], self.cst[0:H, C_SEL + h * P:C_SEL + (h + 1) * P],
                                         self.Mrow[0:H, d, bass.ds(c * P, P)], start=True, stop=True)
                        m.then_inc(S["mb"][d], 1)
                        pe.wait_ge(S["kc"][d], i + 1)
                        pe.wait_ge(S["p"][1 - d], other)
                        for h in range(H):
                            m = t.matmul(ps[:, 1, h * P:(h + 1) * P], kc[:, d, h, :], self.qkT[:, h, bass.ds(c * P, P)], start=True, stop=True)
                        m.then_inc(S["sc"][d], 1)
                        pe.wait_ge(S["kw"][1 - d], other)
                        for h in range(H):
                            m = t.transpose(ps[:, 2, h * P:(h + 1) * P], kc[:, d, h, :], self.c(C_ID))
                        m.then_inc(S["kt"][d], 1)
                    for d in range(2):
                        c = chunk(i, d)
                        other = i + 1 if d == 0 else i + 2
                        pe.wait_ge(S["p"][d], i + 2)
                        pe.wait_ge(S["q"][d], i + 2)
                        pe.wait_ge(S["cn"][d], i + 1)
                        pe.wait_ge(S["h"][1 - d], other)
                        for h in range(H):
                            o = ps[:, 3 + h // 2, (h % 2) * hn:(h % 2 + 1) * hn]
                            t.matmul(o, p[:, d, h, :], self.vaug[:, bass.ds(c, 1), h, :].rearrange("p a e -> p (a e)"), start=True, stop=False)
                            m = t.matmul(o, q[:, d, h, :], cst8[:, d, h, :], start=False, stop=True)
                        m.then_inc(S["o"][d], 1)
                        pe.wait_ge(S["kw"][d], i + 2)
                        pe.wait_ge(S["cn"][1 - d], other)
                        for h in range(H):
                            m = t.matmul(ps[:, 5 + h // 2, (h % 2) * hn:(h % 2 + 1) * hn], kw[:, d, h, :],
                                         self.vaug[:, bass.ds(c, 1), h, :].rearrange("p a e -> p (a e)"), start=True, stop=True)
                        m.then_inc(S["cm"][d], 1)

            @block.vector
            def _(dve):
                v = nc.vector
                ch = Chain(dve, s_v)
                for d in range(2):
                    for n in ("p", "kw", "y", "q", "cn", "h"):
                        dve.sem_inc(S[n][d], 1)
                v.memset(cst8[:], 0.0).then_inc(s_c0, 1)
                dve.wait_ge(s_c0, 1)
                bc = lambda ap: ap.unsqueeze(2).to_broadcast([P, H, P])
                sq = lambda ap: ap.rearrange("p a h -> p (a h)")
                psM = ps[:, 0, :].rearrange("p (h t) -> p h t", h=H)
                psS = ps[:, 1, :].rearrange("p (h t) -> p h t", h=H)
                psK = ps[:, 2, :].rearrange("p (h t) -> p h t", h=H)
                with dve.Fori(0, TT) as i:
                    ch.enter(i, 10)
                    for d in range(2):
                        c = chunk(i, d)
                        mask = self.c((C_MFW, C_MBW)[d]).unsqueeze(1).to_broadcast([P, H, P])
                        dve.wait_ge(S["mb"][d], i + 1)
                        ch.link(v.tensor_tensor(mm_[:, d], psM, mask, ALU.add))
                        v.tensor_tensor(mm_[:, d], bc(sq(self.acol[:, d, bass.ds(c, 1), :])), mm_[:, d], ALU.subtract).then_inc(S["z"][d], 1)
                        v.tensor_tensor(ab[:, d], bc(sq(self.mext[:, d, bass.ds(c + 1, 1), :])), psM, ALU.subtract).then_inc(S["y"][d], 1)
                        dve.wait_ge(S["sc"][d], i + 1)
                        dve.wait_ge(S["w"][d], i + 1)
                        dve.wait_ge(S["o"][d], i + 1)
                        v.scalar_tensor_tensor(out=p[:, d], in0=psS, scalar=QSCALE, in1=w[:, d], op0=ALU.mult, op1=ALU.mult).then_inc(S["p"][d], 1)
                        dve.wait_ge(S["kt"][d], i + 2)
                        dve.wait_ge(S["cm"][d], i + 1)
                        v.tensor_tensor(kw[:, d], psK, bc(sq(self.wg[:, d, bass.ds(c, 1), :])), ALU.mult).then_inc(S["kw"][d], 1)
                        dve.wait_ge(S["a"][d], i + 1)
                        v.scalar_tensor_tensor(out=q[:, d], in0=self.qkT[:, 0:H, bass.ds(c * P, P)], scalar=QSCALE, in1=ab[:, d],
                                               op0=ALU.mult, op1=ALU.mult).then_inc(S["q"][d], 1)
                    for d in range(2):
                        c = chunk(i, d)
                        dve.wait_ge(S["o"][d], i + 2)
                        po = ps[:, 3:5, 0:2 * hn].rearrange("p b (h e) -> p b h e", h=2)
                        den4 = den[:, d].rearrange("p (b h a) -> p b h a", b=2, a=1)
                        em4 = self.emm[:, d, bass.ds(c, 1), :].rearrange("p a (b h) -> p b h a", b=2)
                        ch.link(v.scalar_tensor_tensor(out=den4, in0=po[:, :, :, HD:hn], scalar=-1.0, in1=em4, op0=ALU.mult, op1=ALU.max))
                        ch.link(v.tensor_tensor(den4, den4, po[:, :, :, HD:hn], ALU.max))
                        ch.link(v.reciprocal(den[:, d], den[:, d]))
                        v.tensor_tensor(self.hdir[:, d, bass.ds(c, 1), :].rearrange("p a (b h e) -> p (a b) h e", b=2, h=2),
                                        po[:, :, :, 0:HD], den4.to_broadcast([P, 2, 2, HD]), ALU.mult).then_inc(S["h"][d], 1)
                        dve.wait_ge(S["cm"][d], i + 2)
                        pc = ps[:, 5:7, 0:2 * hn].rearrange("p b (h e) -> p b h e", h=2)
                        dc = self.dec[:, d, bass.ds(c, 1), :].rearrange("p a (b h) -> p b h a", b=2)
                        c4 = cst8[:, d].rearrange("p (b h) e -> p b h e", b=2)
                        ch.link(v.tensor_tensor(c4, c4, dc.to_broadcast([P, 2, 2, hn]), ALU.mult))
                        v.tensor_tensor(c4, c4, pc, ALU.add).then_inc(S["cn"][d], 1)
                    ch.leave(TT)

    def mlstm_norm(self):
        nc = self.nc
        s_g, s_v, s_var, s_std, s_sig, s_sq, s_cen = (self.sem(n) for n in ("mh_g_loaded", "mln_dve", "mln_var", "mln_std", "o_sigmoid", "mln_squared", "mln_centred"))
        G = TT * H
        with ExitStack() as x, nc.Block() as block:
            g = self.sb("mh_g", [P, H * HD], ctx=x)
            sq = self.qkT
            sm = self.sb("mln_sum", [P, G], ctx=x)
            grp = lambda ap: ap.rearrange("p t (h e) -> p (t h) e", h=H)
            hf, hb = grp(self.hdir[:, 0]), grp(self.hdir[:, 1])
            sqv = sq[:, 0:4].rearrange("p k (g e) -> p (k g) e", e=HD)
            bc = lambda ap: ap.unsqueeze(2).to_broadcast([P, G, HD])

            @block.sync
            def _(sp):
                sp.dma_start(g[:], self.i["mh_norm_g"].partition_broadcast(P)).then_inc(s_g, 16)

            @block.scalar
            def _(act):
                nc.scalar.activation(self.hm[:], self.hm[:], ACT.Sigmoid).then_inc(s_sig, 1)
                act.wait_ge(s_cen, 1)
                nc.scalar.activation(sqv, hf, ACT.Square).then_inc(s_sq, 1)
                act.wait_ge(s_var, 1)
                nc.scalar.activation(sm[:], sm[:], ACT.Sqrt).then_inc(s_std, 1)

            @block.vector
            def _(dve):
                v = nc.vector
                ch = Chain(dve, s_v)
                ch.link(v.tensor_tensor(hf, hf, hb, ALU.add))
                ch.link(v.tensor_reduce(sm[:], hf, AX, ALU.add))
                ch.link(v.tensor_scalar_mul(sm[:], sm[:], 1.0 / HD))
                v.tensor_tensor(hf, hf, bc(sm[:]), ALU.subtract).then_inc(s_cen, 1)
                dve.wait_ge(s_g, 16)
                dve.wait_ge(s_sig, 1)
                ch.link(v.tensor_tensor(self.hm[:], self.hm[:], g[:].unsqueeze(1).to_broadcast([P, TT, H * HD]), ALU.mult))
                dve.wait_ge(s_sq, 1)
                ch.link(v.tensor_reduce(sm[:], sqv, AX, ALU.add))
                v.tensor_scalar(sm[:], sm[:], 1.0 / HD, LN_EPS, ALU.mult, ALU.add).then_inc(s_var, 1)
                dve.wait_ge(s_std, 1)
                ch.link(v.reciprocal(sm[:], sm[:]))
                dve.wait_ge(s_cen, 1)
                ch.link(v.tensor_tensor(hf, hf, bc(sm[:]), ALU.mult))
                ch.link(v.tensor_tensor(grp(self.hm[:]), grp(self.hm[:]), hf, ALU.mult))

    def attention(self):
        with ExitStack() as at:
            self.latent_projections(at)
            self.attend()

    def latent_projections(self, at):
        nc, ps = self.nc, self.ps
        s_w, s_gg, s_v = self.sem("w_lat_loaded"), self.sem("lat_g_loaded"), self.sem("lat_dve")
        s_n, s_kr, s_tr, s_cT, s_tre = (self.sem(n) for n in ("lat_normed", "kr_tile", "lat_transposed", "latT_ready", "krT_copied"))
        s_qn, s_kn, s_qr, s_va = (self.sem(n) for n in ("qn_product", "kn_product", "qr_product", "va_product"))
        s_qne, s_kne, s_qrot, s_vae, s_qrt, s_qrte = (self.sem(n) for n in ("qn_copied", "kn_copied", "qr_rotated", "va_copied", "qr_transposed", "qrT_copied"))
        self.qnT = self.sb("qnT", [P, TT + 1, H, P], ctx=at)
        self.qrT = self.sb("qrT", [P, TT + 1, 2, P], ctx=at)
        self.knT = self.sb("knT", [P, H, T], ctx=at)
        self.krT = self.sb("krT", [P, T], ctx=at)
        self.va = self.sb("va", [P, TT, H * HD], ctx=at)
        NL = QL // P + KVL // P
        with ExitStack() as x, nc.Block() as block:
            wof, nq, nkv = self.wo[:].rearrange("p k n -> p (k n)"), QL // P * H * (HD + RO), KVL // P * H * 2 * HD
            wq = wof[:, 0:nq].rearrange("p (k n) -> p k n", k=QL // P)
            wkv = wof[:, nq:nq + nkv].rearrange("p (k n) -> p k n", k=KVL // P)
            gg = self.sb("lat_g", [P, NL], ctx=x)
            tn = self.sb("lat_tile", [P, QL + KVL + 2 * RO], ctx=x)
            cT = self.sb("latT", [P, NL, P], ctx=x)
            qr = self.sb("qr_tile", [P, H, RO], ctx=x)
            tmp = self.sb("qr_tmp", [P, H, 32], ctx=x)

            @block.sync
            def _(sp):
                sp.dma_start(wq, self.i["w_uq"].rearrange("(k p) n -> p k n", p=P)).then_inc(s_w, 16)
                sp.dma_start(wkv, self.i["w_ukv"].rearrange("(k p) n -> p k n", p=P)).then_inc(s_w, 16)
                with nc.allow_non_contiguous_dma("gains with a channel to a partition"):
                    sp.dma_start(gg[:, 0:QL // P], self.i["q_norm_g"].rearrange("(k p) -> p k", p=P)).then_inc(s_gg, 16)
                    sp.dma_start(gg[:, QL // P:NL], self.i["kv_norm_g"].rearrange("(k p) -> p k", p=P)).then_inc(s_gg, 16)

            @block.gpsimd
            def _(pool):
                nc.gpsimd.memset(self.qnT[:, TT:TT + 1], 0.0)
                nc.gpsimd.memset(self.qrT[:, TT:TT + 1], 0.0)

            @block.vector
            def _(dve):
                v = nc.vector
                ch = Chain(dve, s_v)
                for s in (s_kne, s_qrot):
                    dve.sem_inc(s, 1)
                with dve.Fori(0, TT) as t:
                    ch.enter(t, 6)
                    dve.wait_ge(s_tr, t + 1)
                    ch.link(v.tensor_tensor(tn[:, 0:QL].unsqueeze(1), self.cq[:, bass.ds(t, 1), :],
                                            self.rlat[:, 0, bass.ds(t, 1)].unsqueeze(2).to_broadcast([P, 1, QL]), ALU.mult))
                    v.tensor_tensor(tn[:, QL:QL + KVL].unsqueeze(1), self.ckv[:, bass.ds(t, 1), :],
                                    self.rlat[:, 1, bass.ds(t, 1)].unsqueeze(2).to_broadcast([P, 1, KVL]), ALU.mult).then_inc(s_n, 1)
                    dve.wait_ge(s_kn, t + 1)
                    v.tensor_copy(self.knT[:, :, bass.ds(t * P, P)], ps[:, 3, :].rearrange("p (h t) -> p h t", h=H)).then_inc(s_kne, 1)
                    dve.wait_ge(s_qr, t + 1)
                    dve.wait_ge(s_qrt, t + 1)
                    pq = ps[:, 4, 0:H * RO].rearrange("p (h e) -> p h e", h=H)
                    x1, x2 = pq[:, :, 0:32], pq[:, :, 32:64]
                    sn = self.tab[:, 0, bass.ds(t, 1), :].to_broadcast([P, H, 32])
                    cs = self.tab[:, 1, bass.ds(t, 1), :].to_broadcast([P, H, 32])
                    ch.link(v.tensor_tensor(qr[:, :, 0:32], x1, cs, ALU.mult))
                    ch.link(v.tensor_tensor(tmp[:], x2, sn, ALU.mult))
                    ch.link(v.tensor_tensor(qr[:, :, 0:32], qr[:, :, 0:32], tmp[:], ALU.subtract))
                    ch.link(v.tensor_tensor(qr[:, :, 32:64], x2, cs, ALU.mult))
                    ch.link(v.tensor_tensor(tmp[:], x1, sn, ALU.mult))
                    v.tensor_tensor(qr[:, :, 32:64], qr[:, :, 32:64], tmp[:], ALU.add).then_inc(s_qrot, 1)
                    ch.leave(TT)

            @block.scalar
            def _(act):
                a = nc.scalar
                for s in (s_qne, s_vae, s_tre, s_qrte):
                    act.sem_inc(s, 1)
                act.wait_ge(s_gg, 32)
                with act.Fori(0, TT) as t:
                    act.wait_ge(s_tr, t + 1)
                    a.copy(tn[:, QL + KVL:].rearrange("p (a b c) -> p a b c", a=1, b=2), self.kr2[:, bass.ds(t, 1)]).then_inc(s_kr, 1)
                    act.wait_ge(s_tr, t + 2)
                    for j in range(NL):
                        op = a.mul(cT[:, j, :], ps[:, j // 4, (j % 4) * P:(j % 4 + 1) * P], gg[:, j:j + 1])
                    op.then_inc(s_cT, 1)
                    a.copy(self.krT[:, bass.ds(t * P, P)], ps[:, NL // 4, (NL % 4) * P:(NL % 4 + 1) * P]).then_inc(s_tre, 1)
                    act.wait_ge(s_qn, t + 1)
                    a.copy(self.qnT[:, bass.ds(t, 1)], ps[:, 2, :].rearrange("p (a h t) -> p a h t", a=1, h=H)).then_inc(s_qne, 1)
                    act.wait_ge(s_va, t + 1)
                    a.copy(self.va[:, bass.ds(t, 1), :], ps[:, 5, :].rearrange("p (a n) -> p a n", a=1)).then_inc(s_vae, 1)
                    act.wait_ge(s_qrt, t + 2)
                    a.copy(self.qrT[:, bass.ds(t, 1)], ps[:, 6, 0:2 * P].rearrange("p (a b t) -> p a b t", a=1, b=2)).then_inc(s_qrte, 1)

            @block.tensor
            def _(pe):
                m_ = nc.tensor
                ident = self.c(C_ID)
                pe.sem_inc(s_tr, 1)
                pe.sem_inc(s_qrt, 1)
                pe.wait_ge(s_w, 32)
                with pe.Fori(0, TT) as t:
                    pe.wait_ge(s_n, t + 1)
                    pe.wait_ge(s_kr, t + 1)
                    pe.wait_ge(s_tre, t + 1)
                    for j in range(NL + 1):
                        m = m_.transpose(ps[:, j // 4, (j % 4) * P:(j % 4 + 1) * P], tn[:, j * P:(j + 1) * P], ident)
                    m.then_inc(s_tr, 1)
                    pe.wait_ge(s_cT, t + 1)
                    nq = QL // P
                    pe.wait_ge(s_qrot, t + 1)
                    for k in range(nq):
                        m = m_.matmul(ps[:, 4, 0:H * RO], cT[:, k, :], wq[:, k, :].rearrange("p (h e) -> p h e", h=H)[:, :, HD:],
                                      start=k == 0, stop=k == nq - 1)
                    m.then_inc(s_qr, 1)
                    pe.wait_ge(s_kne, t + 1)
                    for h in range(H):
                        for k in range(KVL // P):
                            m = m_.matmul(ps[:, 3, h * P:(h + 1) * P], wkv[:, k, h * 256:h * 256 + P], cT[:, nq + k, :],
                                          start=k == 0, stop=k == KVL // P - 1)
                    m.then_inc(s_kn, 1)
                    pe.wait_ge(s_qne, t + 1)
                    for h in range(H):
                        for k in range(nq):
                            m = m_.matmul(ps[:, 2, h * P:(h + 1) * P], wq[:, k, h * 192:h * 192 + P], cT[:, k, :],
                                          start=k == 0, stop=k == nq - 1)
                    m.then_inc(s_qn, 1)
                    pe.wait_ge(s_vae, t + 1)
                    for k in range(KVL // P):
                        m = m_.matmul(ps[:, 5, :], cT[:, nq + k, :], wkv[:, k, :].rearrange("p (h e) -> p h e", h=H)[:, :, HD:],
                                      start=k == 0, stop=k == KVL // P - 1)
                    m.then_inc(s_va, 1)
                    pe.wait_ge(s_qrot, t + 2)
                    pe.wait_ge(s_qrte, t + 1)
                    for pair in range(2):
                        m = m_.transpose(ps[:, 6, pair * P:(pair + 1) * P], qr[:, 2 * pair:2 * pair + 2, :].rearrange("p h e -> p (h e)"), ident)
                    m.then_inc(s_qrt, 1)

    def attend(self):
        nc, ps = self.nc, self.ps
        s_q, s_S, s_nm, s_p, s_t, s_td, s_ta, s_o, s_oe, s_v, s_mx = (self.sem(n) for n in (
            "q_tile", "scores", "neg_max", "probs", "probs_turned", "pT_dve", "pT_act", "attn_out", "attn_copied", "att_dve", "maxed"))
        with ExitStack() as x, nc.Block() as block:
            qs = self.sb("qs_tile", [P, H, P], ctx=x)
            qrs = self.sb("qrs_tile", [P, 2, P], ctx=x)
            pb = self.sb("probs", [P, 2, T], ctx=x)
            pT = self.sb("probsT", [P, TT, P], ctx=x)
            mx = self.sb("mx", [P, 2], ctx=x)
            nm = self.sb("nm", [P, 2], ctx=x)
            rs = self.sb("rs", [P, 2], ctx=x)
            ri = self.sb("ri", [P, 2], ctx=x)

            @block.sync
            def _(sp):
                sp.dma_start(self.wo[:], self.i["w_out"].rearrange("(k p) n -> p k n", p=P)).then_inc(self.s_wo, 16)

            @block.tensor
            def _(pe):
                m_ = nc.tensor

                def scores(n, h):
                    pe.wait_ge(s_p, n)
                    b = 2 * (h % 2)
                    lo = RO * (h % 2)
                    for half in range(2):
                        sl = slice(half * 512, half * 512 + 512)
                        m_.matmul(ps[:, b + half, :], qs[:, h, :], self.knT[:, h, sl], start=True, stop=False)
                        m = m_.matmul(ps[:, b + half, :], qrs[lo:lo + RO, h // 2, :], self.krT[lo:lo + RO, sl], start=False, stop=True)
                    m.then_inc(s_S, 1)

                pe.wait_ge(s_q, 1)
                for half in range(2):
                    sl = slice(half * 512, half * 512 + 512)
                    m_.matmul(ps[:, half, :], qs[:, 0, :], self.knT[:, 0, sl], start=True, stop=False)
                    m = m_.matmul(ps[:, half, :], qrs[0:RO, 0, :], self.krT[0:RO, sl], start=False, stop=True)
                m.then_inc(s_S, 1)
                with pe.Fori(0, TT) as t:
                    for h in range(H):
                        n = t * H + h
                        if h == H - 1:
                            pe.wait_ge(s_q, t + 2)
                        scores(n + 1, (h + 1) % H)
                        pe.wait_ge(s_p, n + 2)
                        pe.wait_ge(s_td, n + 1)
                        pe.wait_ge(s_ta, n + 1)
                        for k in range(TT):
                            m = m_.transpose(ps[:, 4 + k // 4, (k % 4) * P:(k % 4 + 1) * P], pb[:, h % 2, k * P:(k + 1) * P], self.c(C_ID))
                        m.then_inc(s_t, 1)
                        pe.wait_ge(s_td, n + 2)
                        pe.wait_ge(s_ta, n + 2)
                        pe.wait_ge(s_oe, n + 1)
                        for k in range(TT):
                            m = m_.matmul(ps[:, 6, 0:HD], pT[:, k, :], self.va[:, k, h * HD:(h + 1) * HD], start=k == 0, stop=k == TT - 1)
                        m.then_inc(s_o, 1)

            @block.scalar
            def _(act):
                a = nc.scalar
                act.sem_inc(s_p, 1)
                act.sem_inc(s_ta, 1)
                a.copy(qs[:], self.qnT[:, 0])
                a.copy(qrs[:], self.qrT[:, 0]).then_inc(s_q, 1)
                with act.Fori(0, TT) as t:
                    for h in range(H):
                        n = t * H + h
                        if h == H - 1:
                            act.wait_ge(s_S, n + 1)
                            a.copy(qs[:], self.qnT[:, bass.ds(t + 1, 1)].rearrange("p a h t -> p (a h) t"))
                            a.copy(qrs[:], self.qrT[:, bass.ds(t + 1, 1)].rearrange("p a h t -> p (a h) t")).then_inc(s_q, 1)
                        act.wait_ge(s_nm, n + 1)
                        a.activation(pb[:, h % 2, :], ps[:, 2 * (h % 2):2 * (h % 2) + 2, :].rearrange("p a b -> p (a b)"), ACT.Exp,
                                     bias=nm[:, h % 2:h % 2 + 1], scale=ASCALE, accum_out=rs[:, h % 2:h % 2 + 1]).then_inc(s_p, 1)
                        act.wait_ge(s_t, n + 1)
                        a.copy(pT[:, 4:8, :], ps[:, 5, :].rearrange("p (k t) -> p k t", k=4)).then_inc(s_ta, 1)

            @block.vector
            def _(dve):
                v = nc.vector
                ch = Chain(dve, s_v)
                dve.sem_inc(s_td, 1)
                dve.sem_inc(s_oe, 1)
                with dve.Fori(0, TT) as t:
                    ch.enter(t, 2 * H)
                    for h in range(H):
                        n = t * H + h
                        j = h % 2
                        dve.wait_ge(s_S, n + 1)
                        ch.link(v.tensor_reduce(mx[:, j:j + 1], ps[:, 2 * j:2 * j + 2, :].rearrange("p a b -> p (a b)"), AX, ALU.max))
                        v.tensor_scalar_mul(nm[:, j:j + 1], mx[:, j:j + 1], -ASCALE).then_inc(s_nm, 1)
                        dve.wait_ge(s_t, n + 1)
                        v.tensor_copy(pT[:, 0:4, :], ps[:, 4, :].rearrange("p (k t) -> p k t", k=4)).then_inc(s_td, 1)
                        ch.link(v.reciprocal(ri[:, j:j + 1], rs[:, j:j + 1]))
                        dve.wait_ge(s_o, n + 1)
                        v.tensor_scalar(self.oa[:, bass.ds(t, 1), h * HD:(h + 1) * HD], ps[:, 6, 0:HD].unsqueeze(1), ri[:, j:j + 1], None,
                                        ALU.mult).then_inc(s_oe, 1)
                    ch.leave(TT)

    def output_projection(self):
        nc, ps, mod = self.nc, self.ps, self.mod
        s_x, s_w, s_row, s_v, s_osq, s_oms, s_ostd, s_oan = (self.sem(n) for n in (
            "x_all_loaded", "w_router_loaded", "rows_loaded", "op_dve", "oa_squared", "oa_var", "oa_std", "oa_normed"))
        s_hc, s_ht, s_hT, s_y, s_ye = (self.sem(n) for n in ("h_tile", "h_turned", "hT_ready", "y_product", "y_read"))
        s_v1, s_s1, s_v2, s_s2, s_u, s_ut, s_uT, s_l, s_le, s_st = (self.sem(n) for n in (
            "varA", "stdA", "varB", "stdB", "u2_ready", "u2_turned", "u2T_ready", "logits_product", "logits_copied", "u2_stored"))
        s_x1, s_x1st = self.sem("x1_ready"), self.sem("x1_stored")
        with ExitStack() as x, nc.Block() as block:
            sb = lambda n, s: self.sb(n, s, ctx=x)
            x1 = sb("x1", [P, TT, D])
            wo = self.wo
            wr = sb("w_router", [P, KD, NG + E])
            ag = sb("attn_g", [P, H * HD])
            g1 = sb("ln1_g", [P, D])
            b1 = sb("ln1_b", [P, D])
            ro = sb("oa_rstd", [P, TT])
            hT = sb("hT", [P, KD, P])
            z = sb("z", [P, D])
            u2 = sb("u2", [P, D])
            uT = sb("u2T", [P, KD, P])
            oc = sb("oc", [P, 1])
            st, mv, ve = sb("stB", [P, 2, 6]), sb("mvB", [P, 2]), sb("veB", [P, 2])
            hc = sb("h_cat", [P, D])
            sqh = sb("oa_sq", [P, H * HD])

            @block.sync
            def _(sp):
                sp.dma_start(ag[:], self.i["attn_norm_g"].partition_broadcast(P)).then_inc(s_row, 16)
                sp.dma_start(g1[:], self.i["ln1_g"].partition_broadcast(P)).then_inc(s_row, 16)
                sp.dma_start(b1[:], self.i["ln1_b"].partition_broadcast(P)).then_inc(s_row, 16)
                sp.dma_start(x1[:], self.i["x"].rearrange("(t p) d -> p t d", p=P)).then_inc(s_x, 16)
                with nc.allow_non_contiguous_dma("narrow router weights"):
                    sp.dma_start(wr[:, :, 0:NG], self.i["w_rg"].rearrange("(k p) n -> p k n", p=P)).then_inc(s_w, 16)
                    sp.dma_start(wr[:, :, NG:], self.i["w_re"].rearrange("(k p) n -> p k n", p=P)).then_inc(s_w, 16)
                sp.sem_inc(s_st, 16)
                with sp.Fori(0, TT) as t:
                    sp.wait_ge(s_x1, t + 1)
                    sp.dma_start(self.x1d.rearrange("(t p) d -> t p d", p=P)[bass.ds(t, 1)].rearrange("a p d -> p (a d)"),
                                 x1[:, bass.ds(t, 1), :].rearrange("p a d -> p (a d)")).then_inc(s_x1st, 16)
                    sp.wait_ge(s_u, t + 1)
                    sp.dma_start(self.u2d.rearrange("(t p) d -> t p d", p=P)[bass.ds(t, 1)].rearrange("a p d -> p (a d)"), u2[:]).then_inc(s_st, 16)
                sp.wait_ge(s_st, 16 * TT + 16)
                sp.wait_ge(s_x1st, 16 * TT)

            @block.scalar
            def _(act):
                a = nc.scalar
                for t in range(TT):
                    a.activation(sqh[:], self.oa[:, t, :], ACT.Square, accum_out=ro[:, t:t + 1]).then_inc(s_osq, 1)
                    act.wait_ge(s_osq, t + 1)
                act.wait_ge(s_oms, 1)
                a.activation(ro[:], ro[:], ACT.Sqrt).then_inc(s_ostd, 1)
                act.wait_ge(s_oan, 1)

                def front(t, first=False):
                    if not first:
                        act.wait_ge(s_ht, t)
                    a.copy(hc[:, 0:512].rearrange("p (a n) -> p a n", a=1), self.hm[:, bass.ds(t, 1), :])
                    a.copy(hc[:, 512:].rearrange("p (a n) -> p a n", a=1), self.oa[:, bass.ds(t, 1), :]).then_inc(s_hc, 1)
                    act.wait_ge(s_ht, t + 1)
                    a.copy(hT[:].rearrange("p k t -> p (k t)"), ps[:, 0:2, :].rearrange("p a b -> p (a b)")).then_inc(s_hT, 1)

                def back(t):
                    act.wait_ge(s_v1, t + 1)
                    a.activation(ve[:, 1:2], ve[:, 0:1], ACT.Sqrt).then_inc(s_s1, 1)
                    act.wait_ge(s_v2, t + 1)
                    a.activation(ve[:, 1:2], ve[:, 0:1], ACT.Sqrt).then_inc(s_s2, 1)
                    act.wait_ge(s_ut, t + 1)
                    a.copy(uT[:].rearrange("p k t -> p (k t)"), ps[:, 4:6, :].rearrange("p a b -> p (a b)")).then_inc(s_uT, 1)
                    act.wait_ge(s_l, t + 1)
                    a.copy(self.lg[:, bass.ds(t, 1), :], ps[:, 6, 0:NG + E].rearrange("p (a n) -> p a n", a=1)).then_inc(s_le, 1)

                front(0, first=True)
                with act.Fori(0, TT - 1) as t:
                    front(t + 1)
                    back(t)
                back(TT - 1)

            @block.tensor
            def _(pe):
                m_ = nc.tensor
                ident = self.c(C_ID)

                def front(t, first=False):
                    pe.wait_ge(s_hc, t + 1)
                    if not first:
                        pe.wait_ge(s_hT, t)
                    for k in range(KD):
                        m = m_.transpose(ps[:, k // 4, (k % 4) * P:(k % 4 + 1) * P], hc[:, k * P:(k + 1) * P], ident)
                    m.then_inc(s_ht, 1)
                    pe.wait_ge(s_hT, t + 1)
                    if not first:
                        pe.wait_ge(s_ye, t)
                    for half in range(2):
                        for k in range(KD):
                            m = m_.matmul(ps[:, 2 + half, :], hT[:, k, :], wo[:, k, half * 512:half * 512 + 512], start=k == 0, stop=k == KD - 1)
                    m.then_inc(s_y, 1)

                def back(t):
                    pe.wait_ge(s_u, t + 1)
                    pe.wait_ge(s_le, t + 1)
                    for k in range(KD):
                        m = m_.transpose(ps[:, 4 + k // 4, (k % 4) * P:(k % 4 + 1) * P], u2[:, k * P:(k + 1) * P], ident)
                    m.then_inc(s_ut, 1)
                    pe.wait_ge(s_uT, t + 1)
                    for k in range(KD):
                        m = m_.matmul(ps[:, 6, 0:NG + E], uT[:, k, :], wr[:, k, :], start=k == 0, stop=k == KD - 1)
                    m.then_inc(s_l, 1)

                pe.sem_inc(s_le, 1)
                pe.wait_ge(self.s_wo, 16)
                front(0, first=True)
                pe.wait_ge(s_w, 32)
                with pe.Fori(0, TT - 1) as t:
                    front(t + 1)
                    back(t)
                back(TT - 1)

            @block.vector
            def _(dve):
                v = nc.vector
                ch = Chain(dve, s_v)
                dve.wait_ge(s_osq, TT)
                v.tensor_scalar(ro[:], ro[:], 1.0 / (H * HD), RMS_EPS, ALU.mult, ALU.add).then_inc(s_oms, 1)
                dve.wait_ge(s_ostd, 1)
                ch.link(v.reciprocal(ro[:], ro[:]))
                ch.link(v.tensor_tensor(self.oa[:], self.oa[:], ro[:].unsqueeze(2).to_broadcast([P, TT, H * HD]), ALU.mult))
                dve.wait_ge(s_row, 48)
                v.tensor_tensor(self.oa[:], self.oa[:], ag[:].unsqueeze(1).to_broadcast([P, TT, H * HD]), ALU.mult).then_inc(s_oan, 1)
                dve.wait_ge(s_x, 16)
                one = lambda ap: ap.unsqueeze(1)

                def normed(src, s_var, s_std, t, out):
                    ch.link(v.bn_stats(st[:, 0, :], src[:, 0:512]))
                    ch.link(v.bn_stats(st[:, 1, :], src[:, 512:1024]))
                    v.tensor_copy(oc[:], self.cst[:, 0:1])
                    ch.link(v.bn_aggr(mv[:], st[:].rearrange("p a b -> p (a b)")))
                    v.tensor_scalar_add(ve[:, 0:1], mv[:, 1:2], LN_EPS).then_inc(s_var, 1)
                    dve.wait_ge(s_std, t + 1)
                    ch.link(v.reciprocal(ve[:, 1:2], ve[:, 1:2]))
                    ch.link(v.tensor_scalar(out, src, mv[:, 0:1], ve[:, 1:2], ALU.subtract, ALU.mult))

                with dve.Fori(0, TT) as t:
                    ch.enter(t, 14)
                    dve.wait_ge(s_y, t + 1)
                    v.tensor_tensor(z[:], ps[:, 2:4, :].rearrange("p a b -> p (a b)"), mod[:, 2, :], ALU.mult).then_inc(s_ye, 1)
                    dve.wait_ge(s_ye, t + 1)
                    ch.link(v.scalar_tensor_tensor(out=one(z[:]), in0=x1[:, bass.ds(t, 1), :], scalar=ALPHA, in1=one(z[:]), op0=ALU.mult, op1=ALU.add))
                    normed(z[:], s_v1, s_s1, t, z[:])
                    ch.link(v.tensor_tensor(z[:], z[:], g1[:], ALU.mult))
                    ch.link(v.tensor_tensor(z[:], z[:], b1[:], ALU.add))
                    v.tensor_scalar_mul(x1[:, bass.ds(t, 1), :], one(z[:]), 1.0).then_inc(s_x1, 1)
                    normed(z[:], s_v2, s_s2, t, z[:])
                    dve.wait_ge(s_le, t + 1)
                    dve.wait_ge(s_st, t * 16 + 16)
                    ch.link(v.tensor_tensor(u2[:], z[:], mod[:, 4, :], ALU.mult))
                    v.tensor_tensor(u2[:], u2[:], mod[:, 3, :], ALU.add).then_inc(s_u, 1)
                    ch.leave(TT)

    def routing(self, ctx):
        nc, ps = self.nc, self.ps
        s_b, s_v, s_d, s_e, s_d2, s_e2, s_A, s_rank, s_pos, s_fill, s_init, s_ids, s_sc, s_asg = (self.sem(n) for n in (
            "router_b", "rt_dve", "g_shifted", "g_exp", "e_gap", "e_exp", "assigned", "ranked", "positions_ready", "fill_ready",
            "slotmap_cleared", "ids_ready", "scattered", "asg_loaded"))
        self.wts = self.sb("pair_weights", [P, 2, TT], ctx=ctx)
        self.asg = self.sb("block_asg", [P, NB], I32, ctx=ctx)
        self.tok = self.sb("block_tok", [P, NB], I32, ctx=ctx)
        self.tbl = self.sb("block_table", [1, 6, NB], I32, ctx=ctx)
        with ExitStack() as x, nc.Block() as block:
            sb = lambda n, s, dt=F32: self.sb(n, s, dt, ctx=x)
            br = sb("b_router", [P, NG + E])
            gx = sb("g_work", [P, 3, TT, NG])
            gm, gs, gw = sb("g_max", [P, TT]), sb("g_sel", [P, TT]), sb("g_w", [P, TT])
            em, eq = sb("e_masked", [P, TT, E]), sb("e_eq", [P, TT, E])
            oh = sb("one_hot", [P, 2, TT, E])
            A = sb("assigned", [P, TT, E])
            mk = sb("e_top", [P, 2, TT])
            sel = sb("e_sel", [P, TT])
            eg = sb("e_gap", [P, TT])
            cnt, nbk, bend, bst = sb("cnt", [P, E]), sb("nbk", [P, E]), sb("bend", [P, E]), sb("bst", [P, E])
            ci = sb("cnt_i", [P, E], I32)
            zero = sb("zero_e", [P, E])
            pos = sb("pos", [P, 2, TT])
            posi = sb("pos_i32", [P, 2, TT], I32)
            ids = sb("ids", [P, 2, TT], I32)
            fill = sb("fill", [P, NB], I32)
            cmp_ = sb("cmp", [1, NB, NB])
            tf = sb("table_f", [1, 6, NB])
            zn = sb("zero_n", [1, NB])

            @block.sync
            def _(sp):
                sp.dma_start(br[:, 0:NG], self.i["b_rg"].partition_broadcast(P)).then_inc(s_b, 16)
                sp.dma_start(br[:, NG:], self.i["b_re"].partition_broadcast(P)).then_inc(s_b, 16)
                sp.wait_ge(s_fill, 1)
                sp.dma_start(self.slotmap.rearrange("(p b) a -> p (b a)", p=P), fill[:]).then_inc(s_init, 16)
                sp.wait_ge(s_sc, 16 * 2 * TT)
                with nc.allow_non_contiguous_dma("slots of a block to the partitions"):
                    sp.dma_start(self.asg[:], self.slotmap.rearrange("(b p) a -> p (b a)", p=P)).then_inc(s_asg, 16)

            @block.gpsimd
            def _(pool):
                g = nc.gpsimd
                g.memset(fill[:], OOB).then_inc(s_fill, 1)
                g.iota(ids[:], pattern=[[1, 2], [2 * P, TT]], base=0, channel_multiplier=2).then_inc(s_ids, 1)
                pool.wait_ge(s_ids, 1)
                pool.wait_ge(s_init, 16)
                pool.wait_ge(s_pos, 1)
                for k in range(2):
                    for t in range(TT):
                        g.indirect_dma_start(out=self.slotmap, out_offset=bass.IndirectOffsetOnAxis(ap=posi[:, k, t:t + 1], axis=0),
                                             in_=ids[:, k, t:t + 1], in_offset=None).then_inc(s_sc, 16)

            @block.scalar
            def _(act):
                act.wait_ge(s_d, 1)
                nc.scalar.activation(gx[:, 1], gx[:, 1], ACT.Exp).then_inc(s_e, 1)
                act.wait_ge(s_d2, 1)
                nc.scalar.activation(eg[:], eg[:], ACT.Exp).then_inc(s_e2, 1)

            @block.tensor
            def _(pe):
                pe.wait_ge(s_A, 1)
                for t in range(TT):
                    for j in range(t + 1):
                        m = nc.tensor.matmul(ps[:, 0, t * E:(t + 1) * E], self.c(C_ONE if j < t else C_US), A[:, j, :], start=j == 0, stop=j == t)
                for j in range(TT):
                    m = nc.tensor.matmul(ps[:, 1, 0:E], self.c(C_ONE), A[:, j, :], start=j == 0, stop=j == TT - 1)
                m.then_inc(s_rank, 1)

            @block.vector
            def _(dve):
                v = nc.vector
                ch = Chain(dve, s_v)
                lk = ch.link
                b3 = lambda ap, n: ap.unsqueeze(2).to_broadcast([P, TT, n])
                im4 = self.c(C_IM99, NG).unsqueeze(1).to_broadcast([P, TT, NG])
                im32 = self.c(C_IM99, E).unsqueeze(1).to_broadcast([P, TT, E])
                dve.wait_ge(s_b, 32)
                lk(v.tensor_tensor(self.lg[:], self.lg[:], br[:].unsqueeze(1).to_broadcast([P, TT, NG + E]), ALU.add))
                g4, e32 = self.lg[:, :, 0:NG], self.lg[:, :, NG:]
                lk(v.tensor_reduce(gm[:], g4, AX, ALU.max))
                lk(v.tensor_tensor(gx[:, 0], g4, b3(gm[:], NG), ALU.is_equal))
                lk(v.tensor_tensor(gx[:, 0], gx[:, 0], im4, ALU.mult))
                lk(v.tensor_reduce(gs[:], gx[:, 0], AX, ALU.min))
                lk(v.tensor_tensor(gx[:, 0], im4, b3(gs[:], NG), ALU.is_equal))
                v.tensor_tensor(gx[:, 1], g4, b3(gm[:], NG), ALU.subtract).then_inc(s_d, 1)
                dve.wait_ge(s_e, 1)
                lk(v.tensor_reduce(gw[:], gx[:, 1], AX, ALU.add))
                lk(v.reciprocal(gw[:], gw[:]))
                lk(v.tensor_scalar(gx[:, 2], gx[:, 0], BIG, -BIG, ALU.mult, ALU.add))
                lk(v.tensor_tensor(em[:].rearrange("p t (g e) -> p t g e", g=NG), e32.rearrange("p t (g e) -> p t g e", g=NG),
                                   gx[:, 2].unsqueeze(3).to_broadcast([P, TT, NG, EG]), ALU.add))
                for k in range(2):
                    lk(v.tensor_reduce(mk[:, k], em[:], AX, ALU.max))
                    lk(v.tensor_tensor(eq[:], em[:], b3(mk[:, k], E), ALU.is_equal))
                    lk(v.tensor_tensor(eq[:], eq[:], im32, ALU.mult))
                    lk(v.tensor_reduce(sel[:], eq[:], AX, ALU.min))
                    lk(v.tensor_tensor(oh[:, k], im32, b3(sel[:], E), ALU.is_equal))
                    if k == 0:
                        lk(v.scalar_tensor_tensor(out=em[:], in0=oh[:, 0], scalar=-100 * BIG, in1=em[:], op0=ALU.mult, op1=ALU.add))
                v.tensor_tensor(A[:], oh[:, 0], oh[:, 1], ALU.add).then_inc(s_A, 1)
                v.tensor_tensor(eg[:], mk[:, 1], mk[:, 0], ALU.subtract).then_inc(s_d2, 1)
                lk(v.memset(zero[:], 0.0))
                lk(v.memset(zn[:], 0.0))
                dve.wait_ge(s_e2, 1)
                lk(v.tensor_scalar_add(sel[:], eg[:], 1.0))
                lk(v.reciprocal(sel[:], sel[:]))
                lk(v.tensor_tensor(self.wts[:, 0], sel[:], gw[:], ALU.mult))
                lk(v.tensor_tensor(self.wts[:, 1], eg[:], self.wts[:, 0], ALU.mult))
                dve.wait_ge(s_rank, 1)
                lk(v.tensor_scalar_add(ci[:], ps[:, 1, 0:E], float(P - 1)))
                lk(v.tensor_scalar(ci[:], ci[:], 7, None, ALU.arith_shift_right))
                lk(v.tensor_copy(nbk[:], ci[:]))
                lk(v.tensor_tensor_scan(bend[:], nbk[:], zero[:], 0.0, ALU.add, ALU.add))
                lk(v.tensor_tensor(bst[:], bend[:], nbk[:], ALU.subtract))
                lk(v.tensor_scalar_mul(bst[:], bst[:], float(P)))
                lk(v.tensor_tensor(em[:], ps[:, 0, 0:TT * E].rearrange("p (t e) -> p t e", e=E), bst[:].unsqueeze(1).to_broadcast([P, TT, E]), ALU.add))
                for k in range(2):
                    lk(v.tensor_tensor(oh[:, k], oh[:, k], em[:], ALU.mult))
                    lk(v.tensor_reduce(pos[:, k], oh[:, k], AX, ALU.add))
                v.tensor_copy(posi[:], pos[:]).then_inc(s_pos, 1)
                io = self.cst[0:1, C_IOTA:C_IOTA + NB]
                lk(v.tensor_tensor(cmp_[:, :, 0:E], bend[0:1, :].unsqueeze(1).to_broadcast([1, NB, E]), io.unsqueeze(2).to_broadcast([1, NB, E]), ALU.is_le))
                lk(v.tensor_reduce(tf[:, 0], cmp_[:, :, 0:E], AX, ALU.add))
                lk(v.tensor_tensor(tf[:, 3, 1:NB], tf[:, 0, 1:NB], tf[:, 0, 0:NB - 1], ALU.not_equal))
                lk(v.memset(tf[:, 3, 0:1], 1.0))
                lk(v.tensor_tensor_scan(tf[:, 1], tf[:, 3], zn[:], 0.0, ALU.add, ALU.add))
                lk(v.tensor_scalar_add(zn[:], tf[:, 1], -2.0))
                lk(v.tensor_tensor(cmp_[:], tf[:, 1].unsqueeze(1).to_broadcast([1, NB, NB]), zn[:].unsqueeze(2).to_broadcast([1, NB, NB]), ALU.is_le))
                lk(v.tensor_reduce(tf[:, 2], cmp_[:], AX, ALU.add))
                lk(v.tensor_scalar_add(tf[:, 2], tf[:, 2], 1.0))
                lk(v.tensor_scalar_mul(tf[:, 5], tf[:, 1], 16.0))
                lk(v.tensor_scalar_min(tf[:, 0], tf[:, 0], float(E - 1)))
                lk(v.tensor_scalar_add(tf[:, 4], zn[:], 0.0))
                lk(v.tensor_copy(tf[:, 4, 0:1], bend[0:1, E - 1:E]))
                lk(v.tensor_copy(self.tbl[:], tf[:]))
                dve.wait_ge(s_asg, 16)
                lk(v.tensor_scalar(self.tok[:], self.asg[:], 1, None, ALU.arith_shift_right))

    def experts(self):
        nc, ps = self.nc, self.ps
        s_w = [self.sem(f"{n}_loaded") for n in ("w_gate", "w_up", "w_down")]
        s_x0, s_xg, s_xt, s_xT, s_G, s_U, s_sg, s_h, s_ht, s_hT, s_Y, s_yd, s_ya, s_out = (self.sem(n) for n in (
            "slots_cleared", "slots_gathered", "x_turned", "xT_copied", "gate_product", "up_product", "gate_silu", "h_ready", "hid_turned", "hidT_ready",
            "down_product", "y_copied_dve", "y_copied_act", "y_scattered"))
        s_yfree = self.sem("y_slots_free")
        wg_d = self.i["w_gate"].rearrange("e (k p) f -> e p k f", p=P)
        wu_d = self.i["w_up"].rearrange("e (k p) f -> e p k f", p=P)
        wd_d = self.i["w_down"].rearrange("e (k p) f -> e p k f", p=P)
        with ExitStack() as x, nc.Block() as block:
            sb = lambda n, s, dt=F32: self.sb(n, s, dt, ctx=x)
            wg, wu = sb("w_gate_sb", [P, 2, KD, FE]), sb("w_up_sb", [P, 2, KD, FE])
            wd = sb("w_down_sb", [P, 2, KF, D])
            xg = sb("x_slots", [P, D])
            xT = sb("x_slotsT", [P, KD, P])
            sg, h = sb("silu_g", [P, FE]), sb("hid", [P, FE])
            hT = sb("hidT", [P, KF, P])
            ys = sb("y_slots", [P, D])
            s_used = (s_G, s_U, s_Y)
            count = lambda eng: eng.value_load(self.tbl[0:1, 4, 0:1], min_val=1, max_val=NB - 1)
            entry = lambda eng, row, b, hi: eng.value_load(self.tbl[0:1, row, bass.ds(b, 1)], min_val=0, max_val=hi)

            @block.sync
            def _(sp):
                n = count(sp)
                with sp.Fori(0, NB) as b:
                    with sp.If(b < n):
                        new = entry(sp, 3, b, 1)
                        with sp.If(new > 0):
                            e = entry(sp, 0, b, E - 1)
                            w = entry(sp, 1, b, E)
                            landed = entry(sp, 5, b, 16 * E)
                            through = entry(sp, 2, b, NB + 1)
                            for j, (src, dst) in enumerate(((wg_d, wg), (wu_d, wu), (wd_d, wd))):
                                sp.wait_ge(s_w[j], landed)
                                sp.wait_ge(s_used[j], through)
                                buf = (w + 2 * (j + 1)) % 2
                                sp.dma_start(dst[:, bass.ds(buf, 1)].rearrange("p a k f -> p (a k) f"),
                                             src[bass.ds(e, 1)].rearrange("a p k f -> p (a k) f")).then_inc(s_w[j], 16)

            @block.gpsimd
            def _(pool):
                g = nc.gpsimd
                n = count(pool)
                tok_end, asg_end = pool.to_reg(T - 1), pool.to_reg(2 * T - 1)

                def gather(b):
                    g.indirect_dma_start(out=xg[:], out_offset=None, in_=self.u2d,
                                         in_offset=bass.IndirectOffsetOnAxis(ap=self.tok[:, b:b + 1], axis=0),
                                         bounds_check=tok_end, oob_is_err=False).then_inc(s_xg, 16)

                def scatter(b):
                    pool.wait_ge(s_yd, b + 2)
                    pool.wait_ge(s_ya, b + 2)
                    g.indirect_dma_start(out=self.ybuf, out_offset=bass.IndirectOffsetOnAxis(ap=self.asg[:, b:b + 1], axis=0),
                                         in_=ys[:], in_offset=None, bounds_check=asg_end, oob_is_err=False).then_inc(s_out, 16)
                    pool.wait_ge(s_out, 16 * (b + 1))
                    pool.sem_inc(s_yfree, 1)

                pool.sem_inc(s_yfree, 1)
                g.memset(xg[:], 0.0).then_inc(s_x0, 1)
                pool.wait_ge(s_x0, 1)
                gather(0)
                for b in range(NB):
                    with pool.If(n > b):
                        pool.wait_ge(s_xt, b + 1)
                        gather(b + 1 if b + 1 < NB else b)
                    if b > 0:
                        with pool.If(n > b - 1):
                            scatter(b - 1)

            @block.tensor
            def _(pe):
                m_ = nc.tensor
                ident = self.c(C_ID)

                def turn():
                    for k in range(KD):
                        m = m_.transpose(ps[:, k // 4, (k % 4) * P:(k % 4 + 1) * P], xg[:, k * P:(k + 1) * P], ident)
                    m.then_inc(s_xt, 1)

                n = count(pe)
                for s in (s_G, s_U, s_Y, s_ht):
                    pe.sem_inc(s, 1)
                for s in s_w:
                    pe.sem_inc(s, 16)
                pe.wait_ge(s_xg, 16)
                turn()
                with pe.Fori(0, NB) as b:
                    with pe.If(b < n):
                        w = entry(pe, 1, b, E)
                        buf = w % 2
                        pe.wait_ge(s_xT, b + 1)
                        for dst, wt, s, s_done, bank in ((s_sg, wg, s_w[0], s_G, 2), (s_h, wu, s_w[1], s_U, 3)):
                            pe.wait_ge(dst, b + 1)
                            pe.wait_ge(s, w * 16 + 16)
                            for k in range(KD):
                                m = m_.matmul(ps[:, bank, :], xT[:, k, :], wt[:, bass.ds(buf, 1), k, :].rearrange("p a f -> p (a f)"),
                                              start=k == 0, stop=k == KD - 1)
                            m.then_inc(s_done, 1)
                        pe.wait_ge(s_xg, b * 16 + 32)
                        turn()
                        pe.wait_ge(s_h, b + 2)
                        for k in range(KF):
                            m = m_.transpose(ps[:, 4, k * P:(k + 1) * P], h[:, k * P:(k + 1) * P], ident)
                        m.then_inc(s_ht, 1)
                        pe.wait_ge(s_hT, b + 1)
                        pe.wait_ge(s_yd, b + 1)
                        pe.wait_ge(s_ya, b + 1)
                        pe.wait_ge(s_w[2], w * 16 + 16)
                        for half in range(2):
                            for k in range(KF):
                                m = m_.matmul(ps[:, 5 + half, :], hT[:, k, :],
                                              wd[:, bass.ds(buf, 1), k, half * 512:half * 512 + 512].rearrange("p a f -> p (a f)"),
                                              start=k == 0, stop=k == KF - 1)
                        m.then_inc(s_Y, 1)

            @block.scalar
            def _(act):
                a = nc.scalar
                n = count(act)
                act.sem_inc(s_sg, 1)
                act.sem_inc(s_ya, 1)
                act.wait_ge(s_xt, 1)
                a.copy(xT[:].rearrange("p k t -> p (k t)"), ps[:, 0:2, :].rearrange("p a b -> p (a b)")).then_inc(s_xT, 1)
                with act.Fori(0, NB) as b:
                    with act.If(b < n):
                        act.wait_ge(s_G, b + 2)
                        act.wait_ge(s_h, b + 1)
                        a.activation(sg[:], ps[:, 2, :], ACT.Silu).then_inc(s_sg, 1)
                        act.wait_ge(s_xt, b + 2)
                        a.copy(xT[:].rearrange("p k t -> p (k t)"), ps[:, 0:2, :].rearrange("p a b -> p (a b)")).then_inc(s_xT, 1)
                        act.wait_ge(s_Y, b + 2)
                        act.wait_ge(s_yfree, b + 1)
                        a.copy(ys[:, 512:], ps[:, 6, :]).then_inc(s_ya, 1)
                act.wait_ge(s_yfree, n + 1)
                a.copy(sg[:, 0:1], ys[:, 0:1])

            @block.vector
            def _(dve):
                v = nc.vector
                n = count(dve)
                dve.sem_inc(s_h, 1)
                dve.sem_inc(s_yd, 1)
                with dve.Fori(0, NB) as b:
                    with dve.If(b < n):
                        dve.wait_ge(s_U, b + 2)
                        dve.wait_ge(s_sg, b + 2)
                        dve.wait_ge(s_ht, b + 1)
                        v.tensor_tensor(h[:], sg[:], ps[:, 3, :], ALU.mult).then_inc(s_h, 1)
                        dve.wait_ge(s_ht, b + 2)
                        v.tensor_copy(hT[:].rearrange("p k t -> p (k t)"), ps[:, 4, :]).then_inc(s_hT, 1)
                        dve.wait_ge(s_Y, b + 2)
                        dve.wait_ge(s_yfree, b + 1)
                        v.tensor_copy(ys[:, 0:512], ps[:, 5, :]).then_inc(s_yd, 1)

    def combine(self):
        nc, mod = self.nc, self.mod
        s_x1 = self.sem("x1_loaded")
        s_y = [self.sem(f"pair_loaded{j}") for j in range(2)]
        s_yf = [self.sem(f"pair_used{j}") for j in range(2)]
        s_row, s_v, s_var, s_std, s_o = (self.sem(n) for n in ("ln2_rows", "cb_dve", "varC", "stdC", "out_ready"))
        s_st = [self.sem(f"out_stored{j}") for j in range(2)]
        yb = self.ybuf.rearrange("(t p k) d -> t p k d", p=P, k=2)
        with ExitStack() as x, nc.Block() as block:
            sb = lambda n, s: self.sb(n, s, ctx=x)
            yt = sb("y_pair", [P, 2, 2, D])
            x1 = sb("x1_again", [P, TT, D])
            g2, b2 = sb("ln2_g", [P, D]), sb("ln2_b", [P, D])
            z = sb("z2", [P, 2, D])
            st, mv, ve = sb("stC", [P, 2, 6]), sb("mvC", [P, 2]), sb("veC", [P, 2])

            @block.sync
            def _(sp):
                sp.dma_start(x1[:], self.x1d.rearrange("(t p) d -> p t d", p=P)).then_inc(s_x1, 16)
                sp.dma_start(g2[:], self.i["ln2_g"].partition_broadcast(P)).then_inc(s_row, 16)
                sp.dma_start(b2[:], self.i["ln2_b"].partition_broadcast(P)).then_inc(s_row, 16)
                with sp.Fori(0, TT // 2) as i:
                    for j in range(2):
                        sp.wait_ge(s_yf[j], i + 1)
                        sp.dma_start(yt[:, j], yb[bass.ds(i * 2 + j, 1)].rearrange("a p k d -> p (a k) d")).then_inc(s_y[j], 16)

            @block.gpsimd
            def _(pool):
                for t in range(TT):
                    pool.wait_ge(s_o, t + 1)
                    pool.dma_start(self.out[t * P:(t + 1) * P, :], z[:, t % 2, :]).then_inc(s_st[t % 2], 16)
                for j in range(2):
                    pool.wait_ge(s_st[j], 8 * TT)

            @block.scalar
            def _(act):
                with act.Fori(0, TT) as t:
                    act.wait_ge(s_var, t + 1)
                    nc.scalar.activation(ve[:, 1:2], ve[:, 0:1], ACT.Sqrt).then_inc(s_std, 1)

            @block.vector
            def _(dve):
                v = nc.vector
                ch = Chain(dve, s_v)
                for j in range(2):
                    dve.sem_inc(s_yf[j], 1)
                dve.wait_ge(s_row, 32)
                dve.wait_ge(s_x1, 16)
                for t in range(TT):
                    i, j = t // 2, t % 2
                    zt = z[:, j]
                    dve.wait_ge(s_y[j], 16 * i + 16)
                    if t > 1:
                        dve.wait_ge(s_st[j], 16 * i)
                    ch.link(v.tensor_scalar(zt, yt[:, j, 0, :], self.wts[:, 0, t:t + 1], None, ALU.mult))
                    v.scalar_tensor_tensor(out=zt, in0=yt[:, j, 1, :], scalar=self.wts[:, 1, t:t + 1], in1=zt, op0=ALU.mult, op1=ALU.add).then_inc(s_yf[j], 1)
                    dve.wait_ge(s_yf[j], i + 2)
                    ch.link(v.tensor_tensor(zt, zt, mod[:, 5, :], ALU.mult))
                    ch.link(v.scalar_tensor_tensor(out=zt, in0=x1[:, t, :], scalar=ALPHA, in1=zt, op0=ALU.mult, op1=ALU.add))
                    ch.link(v.bn_stats(st[:, 0, :], zt[:, 0:512]))
                    ch.link(v.bn_stats(st[:, 1, :], zt[:, 512:1024]))
                    ch.link(v.bn_aggr(mv[:], st[:].rearrange("p a b -> p (a b)")))
                    v.tensor_scalar_add(ve[:, 0:1], mv[:, 1:2], LN_EPS).then_inc(s_var, 1)
                    dve.wait_ge(s_std, t + 1)
                    ch.link(v.reciprocal(ve[:, 1:2], ve[:, 1:2]))
                    ch.link(v.tensor_scalar(zt, zt, mv[:, 0:1], ve[:, 1:2], ALU.subtract, ALU.mult))
                    ch.link(v.tensor_tensor(zt, zt, g2[:], ALU.mult))
                    v.tensor_tensor(zt, zt, b2[:], ALU.add).then_inc(s_o, 1)


SHAPES = {
    "x": (T, D), "c": (D,), "positions": (T,), "w_ada": (D, 6 * D), "b_ada": (6 * D,), "w_in": (D, 2768), "conv_w": (5, D), "conv_b": (D,),
    "gate_b": (16,), "mh_norm_g": (512,), "q_norm_g": (QL,), "kv_norm_g": (KVL,), "w_uq": (QL, 768), "w_ukv": (KVL, 1024), "attn_norm_g": (512,),
    "w_out": (D, D), "ln1_g": (D,), "ln1_b": (D,), "w_rg": (D, NG), "b_rg": (NG,), "w_re": (D, E), "b_re": (E,),
    "w_gate": (E, D, FE), "w_up": (E, D, FE), "w_down": (E, FE, D), "ln2_g": (D,), "ln2_b": (D,),
}


def kernel(**inputs):
    import concourse.bacc as bacc
    from concourse.bass_utils import run_bass_kernel_spmd

    nc = bacc.Bacc("TRN2", target_bir_lowering=False, num_devices=1)
    arrays = {f"in_{n}": np.ascontiguousarray(inputs[n]).reshape(s) for n, s in SHAPES.items()}
    arrays["in_consts"] = constants()
    ins = {n[3:]: nc.dram_tensor(n, a.shape, mybir.dt.from_np(a.dtype), kind="ExternalInput").ap() for n, a in arrays.items()}
    out = nc.dram_tensor("out_rows", (T, D), F32, kind="ExternalOutput").ap()
    Kernel(nc, ins, out).build()
    r = run_bass_kernel_spmd(nc, [arrays], core_ids=[0])
    return r.results[0]["out_rows"].reshape(1, T, D)
```

```python
from contextlib import ExitStack

import numpy as np
import concourse.bass as bass
from concourse import mybir

F32 = mybir.dt.float32
I32 = mybir.dt.int32
ALU = mybir.AluOpType
ACT = mybir.ActivationFunctionType
AX = mybir.AxisListType.X

P = 128
D = 1024
T = 1024
TT = T // P
KD = D // P
H = 4
HD = 128
QL, KVL, RO = 384, 256, 64
NTOK = 1744
E, EG, NG = 32, 8, 4
FE = 512
KF = FE // P
NB = (2 * T + E * (P - 1)) // P + 1
LN_EPS, RMS_EPS = 1e-5, 1e-6
ALPHA = 2.0 ** 0.25
QSCALE = HD ** -0.5
ASCALE = (HD + RO) ** -0.5
BIG = 1e30
EARLY = 2 * D // 512
GATED = 4
LATE = 4 * D // 512 - GATED
OOB = 4096

C_ID, C_UFW, C_UBW, C_E127, C_E0, C_ONE, C_MFW, C_MBW, C_US = (i * P for i in range(9))
C_SEL = 9 * P
C_IM99 = C_SEL + H * P
C_INV = C_IM99 + 32
C_IOTA = C_INV + 32
C_END = C_IOTA + NB


def constants():
    c = np.zeros((P, C_END), np.float32)
    s, t = np.arange(P)[:, None], np.arange(P)[None, :]
    c[:, C_ID:C_ID + P] = s == t
    c[:, C_UFW:C_UFW + P] = s <= t
    c[:, C_UBW:C_UBW + P] = s >= t
    c[P - 1, C_E127:C_E127 + P] = 1
    c[0, C_E0:C_E0 + P] = 1
    c[:, C_ONE:C_ONE + P] = 1
    c[:, C_MFW:C_MFW + P] = np.where(s <= t, 0, BIG)
    c[:, C_MBW:C_MBW + P] = np.where(s >= t, 0, BIG)
    c[:, C_US:C_US + P] = s < t
    for h in range(H):
        c[h, C_SEL + h * P:C_SEL + (h + 1) * P] = 1
    c[:, C_IM99:C_IM99 + 32] = np.arange(32) - 99
    c[:, C_INV:C_INV + 32] = np.float32(10000.0) ** (-np.arange(32, dtype=np.float32) / np.float32(32))
    c[:, C_IOTA:C_IOTA + NB] = np.arange(NB)
    return c


class Chain:

    def __init__(self, eng, sem):
        self.eng, self.sem, self.n, self.off = eng, sem, 0, 0

    def link(self, ins):
        ins.then_inc(self.sem, 1)
        self.n += 1
        self.eng.wait_ge(self.sem, self.off + self.n if self.n else self.off)

    def enter(self, i, per):
        self.base, self.per = self.n, per
        self.off = i * per

    def leave(self, count):
        assert self.n - self.base == self.per, (self.n - self.base, self.per)
        self.n = self.base + self.per * count
        self.off = 0


class Kernel:
    def __init__(self, nc, ins, out):
        self.nc, self.i, self.out = nc, ins, out
        self.ctx = ExitStack()
        self.live = []
        self.scratch_dram()

    def sb(self, name, shape, dt=F32, ctx=None):
        return (ctx or self.ctx).enter_context(self.nc.sbuf_tensor(name, shape, dt))

    def sem(self, name):
        self.live.append(self.nc.alloc_semaphore(name=name))
        return self.live[-1]

    def clear_semaphores(self):
        self.nc.clear_and_free_semaphores(self.live)
        self.nc.all_engine_barrier()
        self.live = []

    def scratch_dram(self):
        d = lambda n, s, dt=F32: self.nc.dram_tensor(n, s, dt, kind="Internal").ap()
        self.u2d = d("u2_rows", (T, D))
        self.x1d = d("x1_rows", (T, D))
        self.slotmap = d("slot_to_assignment", (NB * P, 1), I32)
        self.ybuf = d("expert_rows", (2 * T, D))

    def build(self):
        nc = self.nc
        with self.ctx:
            self.ps = self.ctx.enter_context(nc.psum_tensor("ps", [P, 8, 512], F32))
            self.cst = self.sb("cst", [P, C_END])
            self.mod = self.sb("mod", [P, 6, D])
            self.lg = self.sb("logits", [P, TT, NG + E])
            with ExitStack() as mix:
                self.rlat = self.sb("lat_rstd", [P, 2, TT], ctx=mix)
                self.tab = self.sb("sin_cos", [P, 2, TT, 32], ctx=mix)
                self.kr2 = self.sb("kr_rotated", [P, TT, 2, RO], ctx=mix)
                self.hm = self.sb("mlstm_rows", [P, TT, H * HD], ctx=mix)
                self.cq = self.sb("cq", [P, TT, QL], ctx=mix)
                self.ckv = self.sb("ckv", [P, TT, KVL], ctx=mix)
                self.kr = self.sb("kr", [P, TT, RO], ctx=mix)
                self.gt = self.sb("gates", [P, TT, 16], ctx=mix)
                with ExitStack() as up:
                    self.vaug = self.sb("vaug", [P, TT, H, HD + 1], ctx=up)
                    self.uT = self.sb("uT", [P, KD, T], ctx=up)
                    with ExitStack() as first:
                        self.ca = self.sb("c_act", [P, KD], ctx=up)
                        self.s_wt = self.sem("w_in_tokens_loaded")
                        self.wt = self.sb("w_in_tok", [P, KD, NTOK], ctx=first)
                        self.modulation()
                        self.project_tokens()
                    self.qkT = self.sb("qkT", [P, 8, T], ctx=up)
                    self.project_channels()
                    self.mlstm_gates(up)
                    self.mlstm(up)
                    self.mlstm_norm()
                self.clear_semaphores()
                self.s_wo = self.sem("w_out_loaded")
                self.wo = self.sb("w_out", [P, KD, D], ctx=mix)
                self.oa = self.sb("attn_rows", [P, TT, H * HD], ctx=mix)
                self.attention()
                self.output_projection()
            self.clear_semaphores()
            self.routing(self.ctx)
            self.s_again = self.sem("x1_and_rows_loaded")
            self.x1b = self.sb("x1_again", [P, TT, D])
            self.g2, self.b2 = self.sb("ln2_g", [P, D]), self.sb("ln2_b", [P, D])
            self.experts()
            self.combine()

    def c(self, at, n=P, parts=P):
        return self.cst[0:parts, at:at + n]

    def modulation(self):
        nc, cst, mod, ps = self.nc, self.cst, self.mod, self.ps
        s_const, s_c, s_cact = self.sem("const_loaded"), self.sem("c_loaded"), self.sem("c_activated")
        s_bias = self.sem("b_ada_loaded")
        s_w = [self.sem(f"w_ada_loaded{n}") for n in range(EARLY)]
        s_mm = self.sem("mod_product_ready")
        s_v = self.sem("mod_dve")
        modf = mod[:].rearrange("p a d -> p (a d)")
        w_ada = self.i["w_ada"].rearrange("(p k) n -> p k n", k=KD)
        w_t = self.i["w_in"].rearrange("(k p) n -> p k n", p=P)[:, :, 1024:]
        self.w_ada_sb = self.uT[:].rearrange("p k t -> p (k t)").rearrange("p (j k n) -> p j k n", j=2, k=KD)
        w, ca = self.w_ada_sb, self.ca
        with ExitStack() as x, nc.Block() as block:
            cc = self.sb("c_cols", [P, KD], ctx=x)

            @block.sync
            def _(sp):
                sp.dma_start(cc[:], self.i["c"].rearrange("(p k) -> p k", k=KD)).then_inc(s_c, 16)
                for n in range(EARLY):
                    if n > 1:
                        sp.wait_ge(s_mm, n - 1)
                    sp.dma_start(w[:, n % 2], w_ada[:, :, n * 512:n * 512 + 512]).then_inc(s_w[n], 16)
                    if n > 0:
                        for k in range(KD)[(n - 1) * 3:n * 3]:
                            sp.dma_start(self.wt[:, k], w_t[:, k]).then_inc(self.s_wt, 16)

            @block.scalar
            def _(act):
                act.dma_start(cst[:], self.i["consts"]).then_inc(s_const, 16)
                act.dma_start(modf[:, 0:EARLY * 512], self.i["b_ada"][0:EARLY * 512].partition_broadcast(P)).then_inc(s_bias, 16)
                act.wait_ge(s_c, 16)
                nc.scalar.activation(ca[:], cc[:], ACT.Silu).then_inc(s_cact, 1)
                act.wait_ge(s_const, 16)

            @block.tensor
            def _(pe):
                pe.wait_ge(s_cact, 1)
                for n in range(EARLY):
                    pe.wait_ge(s_w[n], 16)
                    for k in range(KD):
                        mm = nc.tensor.matmul(ps[:, n, :], ca[:, k:k + 1].to_broadcast([P, P]), w[:, n % 2, k, :],
                                              start=k == 0, stop=k == KD - 1)
                    mm.then_inc(s_mm, 1)

            @block.vector
            def _(dve):
                ch = Chain(dve, s_v)
                dve.wait_ge(s_bias, 16)
                for n in range(EARLY):
                    dve.wait_ge(s_mm, n + 1)
                    piece = modf[:, n * 512:n * 512 + 512]
                    ch.link(nc.vector.tensor_tensor(piece, piece, ps[:, n, :], ALU.add))
                ch.link(nc.vector.tensor_scalar_add(mod[:, 1, :], mod[:, 1, :], 1.0))

    def project_tokens(self):
        nc, ps, mod = self.nc, self.ps, self.mod
        s_x = [self.sem(f"x_loaded{j}") for j in range(2)]
        s_xfree = [self.sem(f"x_used{j}") for j in range(2)]
        s_wt, wt = self.s_wt, self.wt
        s_var, s_std = self.sem("var1_ready"), self.sem("std1_ready")
        s_u = [self.sem(f"u_ready{j}") for j in range(2)]
        s_tr, s_uT, s_uTf = self.sem("u_transposed"), self.sem("uT_tile_ready"), self.sem("uT_full_copied")
        s_g = [self.sem(f"proj_group{g}") for g in range(4)]
        s_e = [self.sem(f"proj_evacuated{g}") for g in range(4)]
        s_v, s_one = self.sem("proj_dve"), self.sem("ones_col")
        x_t = self.i["x"].rearrange("(t p) d -> t p d", p=P)
        cols = [(0, 512), (512, 512), (1024, 400), (1424, 320)]
        with ExitStack() as x, nc.Block() as block:
            xs = self.sb("x_tiles", [P, 2, D], ctx=x)
            un = self.sb("u_tiles", [P, 2, D], ctx=x)
            uTt = self.sb("uT_tiles", [P, 2, KD, P], ctx=x)
            st = self.sb("st1", [P, 2, 6], ctx=x)
            mv = self.sb("mv1", [P, 2], ctx=x)
            ve = self.sb("ve1", [P, 2], ctx=x)
            one = self.sb("one1", [P, 1], ctx=x)
            ident = self.c(C_ID)

            @block.sync
            def _(sp):
                with sp.Fori(0, TT // 2) as i:
                    for j in range(2):
                        sp.wait_ge(s_xfree[j], i + 1)
                        sp.dma_start(xs[:, j], x_t[bass.ds(i * 2 + j, 1)].rearrange("a p d -> p (a d)")).then_inc(s_x[j], 16)

            @block.gpsimd
            def _(pool):
                nc.gpsimd.memset(self.vaug[:, :, :, HD:HD + 1], 1.0).then_inc(s_one, 1)

            @block.vector
            def _(dve):
                ch = Chain(dve, s_v)
                for j in range(2):
                    dve.sem_inc(s_xfree[j], 1)
                for g in (0, 2):
                    dve.sem_inc(s_e[g], 1)

                def front(t, j, i):
                    dve.wait_ge(s_x[j], i * 16 + 16)
                    ch.link(nc.vector.bn_stats(st[:, 0, :], xs[:, j, 0:512]))
                    ch.link(nc.vector.bn_stats(st[:, 1, :], xs[:, j, 512:1024]))
                    nc.vector.tensor_copy(one[:], ident[:, 0:1])
                    ch.link(nc.vector.bn_aggr(mv[:], st[:].rearrange("p a b -> p (a b)")))
                    nc.vector.tensor_scalar_add(ve[:, 0:1], mv[:, 1:2], LN_EPS).then_inc(s_var, 1)
                    dve.wait_ge(s_std, t + 1)
                    ch.link(nc.vector.reciprocal(ve[:, 1:2], ve[:, 1:2]))
                    dve.wait_ge(s_uTf, t + 1)
                    nc.vector.tensor_scalar(un[:, j], xs[:, j], mv[:, 0:1], ve[:, 1:2], ALU.subtract, ALU.mult).then_inc(s_xfree[j], 1)
                    dve.wait_ge(s_xfree[j], i + 2)
                    ch.link(nc.vector.tensor_tensor(un[:, j], un[:, j], mod[:, 1, :], ALU.mult))
                    nc.vector.tensor_tensor(un[:, j], un[:, j], mod[:, 0, :], ALU.add).then_inc(s_u[j], 1)

                def back(t):
                    dve.wait_ge(s_g[0], t + 1)
                    nc.vector.tensor_copy(self.vaug[:, bass.ds(t, 1), :, 0:HD],
                                          ps[:, 2, :].rearrange("p (a h d) -> p a h d", a=1, h=H)).then_inc(s_e[0], 1)
                    dve.wait_ge(s_g[2], t + 1)
                    nc.vector.tensor_copy(self.gt[:, bass.ds(t, 1), :],
                                          ps[:, 4, 0:16].rearrange("p (a d) -> p a d", a=1))
                    nc.vector.tensor_copy(self.cq[:, bass.ds(t, 1), :],
                                          ps[:, 4, 16:400].rearrange("p (a d) -> p a d", a=1)).then_inc(s_e[2], 1)

                front(0, 0, 0)
                with dve.Fori(0, TT // 2 - 1) as i:
                    ch.enter(i, 10)
                    front(i * 2 + 1, 1, i)
                    back(i * 2)
                    front(i * 2 + 2, 0, i + 1)
                    back(i * 2 + 1)
                    ch.leave(TT // 2 - 1)
                front(TT - 1, 1, TT // 2 - 1)
                back(TT - 2)
                back(TT - 1)

            @block.scalar
            def _(act):
                act.sem_inc(s_uTf, 2)
                act.sem_inc(s_uT, 1)
                for g in (1, 3):
                    act.sem_inc(s_e[g], 1)

                def std(t):
                    act.wait_ge(s_var, t + 1)
                    nc.scalar.activation(ve[:, 1:2], ve[:, 0:1], ACT.Sqrt).then_inc(s_std, 1)

                def turned(t, j):
                    act.wait_ge(s_tr, t + 1)
                    act.wait_ge(s_g[3], t + 1)
                    nc.scalar.copy(uTt[:, j].rearrange("p k t -> p (k t)"), ps[:, 0:2, :].rearrange("p a b -> p (a b)")).then_inc(s_uT, 1)
                    nc.scalar.copy(self.uT[:, :, bass.ds(t * P, P)],
                                   ps[:, 0:2, :].rearrange("p a (b t) -> p (a b) t", t=P)).then_inc(s_uTf, 1)

                def evacuate1(t):
                    act.wait_ge(s_g[1], t + 1)
                    nc.scalar.copy(self.hm[:, bass.ds(t, 1), :],
                                   ps[:, 3, :].rearrange("p (a d) -> p a d", a=1)).then_inc(s_e[1], 1)

                def evacuate3(t):
                    act.wait_ge(s_g[3], t + 3)
                    nc.scalar.copy(self.ckv[:, bass.ds(t, 1), :],
                                   ps[:, 5, 0:256].rearrange("p (a d) -> p a d", a=1))
                    nc.scalar.copy(self.kr[:, bass.ds(t, 1), :],
                                   ps[:, 5, 256:320].rearrange("p (a d) -> p a d", a=1)).then_inc(s_e[3], 1)

                def step(t, j):
                    std(t + 1)
                    evacuate1(t)
                    turned(t + 1, 1 - j)
                    evacuate3(t)

                std(0)
                turned(0, 0)
                with act.Fori(0, TT // 2 - 1) as i:
                    step(i * 2, 0)
                    step(i * 2 + 1, 1)
                step(TT - 2, 0)
                evacuate1(TT - 1)
                evacuate3(TT - 1)
                act.wait_ge(s_e[3], TT + 1)

            @block.tensor
            def _(pe):
                pe.sem_inc(s_g[3], 2)
                pe.wait_ge(s_wt, 16 * KD)

                def turn(t, j, i):
                    pe.wait_ge(s_u[j], i + 1)
                    pe.wait_ge(s_uTf, t + 2)
                    for k in range(KD):
                        mm = nc.tensor.transpose(ps[:, k // 4, (k % 4) * P:(k % 4 + 1) * P], un[:, j, k * P:(k + 1) * P], ident)
                    mm.then_inc(s_tr, 1)

                def products(t, j, groups):
                    if 0 in groups:
                        pe.wait_ge(s_uT, t + 2)
                    for g in groups:
                        c0, n = cols[g]
                        pe.wait_ge(s_e[g], t + 1)
                        for k in range(KD):
                            mm = nc.tensor.matmul(ps[:, 2 + g, 0:n], uTt[:, j, k, :], wt[:, k, c0:c0 + n],
                                                  start=k == 0, stop=k == KD - 1)
                        mm.then_inc(s_g[g], 1)

                def step(t, j, i):
                    products(t, j, (0, 1))
                    turn(t + 1, 1 - j, i)
                    products(t, j, (2, 3))

                turn(0, 0, 0)
                with pe.Fori(0, TT // 2 - 1) as i:
                    step(i * 2, 0, i)
                    step(i * 2 + 1, 1, i + 1)
                step(TT - 2, 0, TT // 2 - 1)
                products(TT - 1, 1, (0, 1, 2, 3))

    def project_channels(self):
        nc, ps = self.nc, self.ps
        s_w = [self.sem(f"w_qk_loaded{j}") for j in range(2)]
        s_mm = [self.sem(f"qk_product{j}") for j in range(2)]
        s_raw = [self.sem(f"qk_raw{j}") for j in range(2)]
        s_cv = [self.sem(f"qk_conv{j}") for j in range(2)]
        s_act = [self.sem(f"qk_silu{j}") for j in range(2)]
        s_cw, s_v, s_pad = self.sem("conv_w_loaded"), self.sem("conv_dve"), self.sem("conv_pad")
        s_pos, s_sq, s_ms, s_std, s_tr, s_sin = (self.sem(n) for n in ("pos_loaded", "lat_squared", "lat_var", "lat_std", "angles_reduced", "sines"))
        w_q = self.i["w_in"].rearrange("(k p) n -> p k n", p=P)
        with ExitStack() as x, nc.Block() as block:
            w = self.sb("w_qk", [P, 2, KD, P], ctx=x)
            raw = self.sb("qk_raw", [P, 2, T + 4], ctx=x)
            acc = self.sb("qk_acc", [P, 2, T], ctx=x)
            cw = self.sb("conv_w", [P, 8, 6], ctx=x)
            cwt = self.sb("conv_w_tile", [P, 6], ctx=x)

            pi_ = self.sb("pos_i", [P, TT], I32, ctx=x)
            pf = self.sb("pos_f", [P, TT], ctx=x)
            qkf = self.qkT[:].rearrange("p k t -> p (k t)")
            sq = qkf[:, 0:TT * QL].rearrange("p (t n) -> p t n", t=TT)
            sq2 = qkf[:, TT * QL:TT * (QL + KVL)].rearrange("p (t n) -> p t n", t=TT)
            rest = qkf[:, TT * (QL + KVL):].rearrange("p (a t n) -> p a t n", t=TT, n=32)
            ang, kk, tmp = rest[:, 0], rest[:, 1:3], rest[:, 3]
            MAGIC = 12582912.0
            TWO_PI_HI = 6.28125
            TWO_PI_LO = float(2 * np.pi - 6.28125)

            @block.sync
            def _(sp):
                with nc.allow_non_contiguous_dma("one position to a partition"):
                    sp.dma_start(pi_[:], self.i["positions"].rearrange("(t p) -> p t", p=P)).then_inc(s_pos, 16)
                with nc.allow_non_contiguous_dma("small convolution weights"):
                    for tap in range(5):
                        sp.dma_start(cw[:, :, tap], self.i["conv_w"][tap].rearrange("(c p) -> p c", p=P)).then_inc(s_cw, 16)
                    sp.dma_start(cw[:, :, 5], self.i["conv_b"].rearrange("(c p) -> p c", p=P)).then_inc(s_cw, 16)
                with sp.Fori(0, 4) as i:
                    for j in range(2):
                        sp.wait_ge(s_mm[j], i + 1)
                        sp.dma_start(w[:, j], w_q[:, :, bass.ds((i * 2 + j) * P, P)]).then_inc(s_w[j], 16)

            @block.tensor
            def _(pe):
                for j in range(2):
                    pe.sem_inc(s_mm[j], 1)
                with pe.Fori(0, 4) as i:
                    for j in range(2):
                        pe.wait_ge(s_w[j], i * 16 + 16)
                        pe.wait_ge(s_raw[j], i + 1)
                        for half in range(2):
                            for k in range(KD):
                                mm = nc.tensor.matmul(ps[:, 2 * j + half, :], w[:, j, k, :], self.uT[:, k, half * 512:half * 512 + 512],
                                                      start=k == 0, stop=k == KD - 1)
                        mm.then_inc(s_mm[j], 1)

            @block.scalar
            def _(act):
                for j in range(2):
                    act.sem_inc(s_raw[j], 1)
                    act.sem_inc(s_act[j], 1)
                nc.scalar.activation(sq, self.cq[:], ACT.Square).then_inc(s_sq, 1)
                nc.scalar.activation(sq2, self.ckv[:], ACT.Square).then_inc(s_sq, 1)
                act.wait_ge(s_ms, 1)
                nc.scalar.activation(self.rlat[:], self.rlat[:], ACT.Sqrt).then_inc(s_std, 1)
                act.wait_ge(s_tr, 1)
                nc.scalar.activation(self.tab[:], self.tab[:], ACT.Sin).then_inc(s_sin, 1)
                act.wait_ge(s_pad, 2)
                with act.Fori(0, 4) as i:
                    for j in range(2):
                        act.wait_ge(s_mm[j], i + 2)
                        act.wait_ge(s_cv[j], i + 1)
                        nc.scalar.copy(raw[:, j, 2:T + 2], ps[:, 2 * j:2 * j + 2, :].rearrange("p a b -> p (a b)")).then_inc(s_raw[j], 1)
                        act.wait_ge(s_cv[j], i + 2)
                        nc.scalar.activation(self.qkT[:, bass.ds(i * 2 + j, 1), :], acc[:, j:j + 1, :], ACT.Silu).then_inc(s_act[j], 1)

            @block.vector
            def _(dve):
                ch = Chain(dve, s_v)
                for j in range(2):
                    dve.sem_inc(s_cv[j], 1)
                nc.vector.memset(raw[:, :, 0:2], 0.0).then_inc(s_pad, 1)
                nc.vector.memset(raw[:, :, T + 2:T + 4], 0.0).then_inc(s_pad, 1)
                v = nc.vector
                dve.wait_ge(s_pos, 16)
                ch.link(v.tensor_copy(pf[:], pi_[:]))
                ch.link(v.tensor_tensor(ang, pf[:].unsqueeze(2).to_broadcast([P, TT, 32]),
                                        self.c(C_INV, 32).unsqueeze(1).to_broadcast([P, TT, 32]), ALU.mult))
                ch.link(v.tensor_scalar(kk[:, 0], ang, float(1 / (2 * np.pi)), MAGIC, ALU.mult, ALU.add))
                ch.link(v.tensor_scalar(kk[:, 1], ang, float(1 / (2 * np.pi)), 0.25, ALU.mult, ALU.add))
                ch.link(v.tensor_scalar_add(kk[:, 1], kk[:, 1], MAGIC))
                ch.link(v.tensor_scalar_add(kk, kk, -MAGIC))
                for y in range(2):
                    ch.link(v.scalar_tensor_tensor(out=self.tab[:, y], in0=kk[:, y], scalar=-TWO_PI_HI, in1=ang[:], op0=ALU.mult, op1=ALU.add))
                    ch.link(v.scalar_tensor_tensor(out=self.tab[:, y], in0=kk[:, y], scalar=-TWO_PI_LO, in1=self.tab[:, y], op0=ALU.mult, op1=ALU.add))
                ch.link(v.tensor_scalar_add(self.tab[:, 1], self.tab[:, 1], float(np.pi / 2)))
                v.tensor_scalar(self.tab[:], self.tab[:], 3.1415925, -3.1415925, ALU.min, ALU.max).then_inc(s_tr, 1)
                dve.wait_ge(s_sq, 2)
                ch.link(v.tensor_reduce(self.rlat[:, 0], sq, AX, ALU.add))
                ch.link(v.tensor_reduce(self.rlat[:, 1], sq2, AX, ALU.add))
                ch.link(v.tensor_scalar(self.rlat[:, 0], self.rlat[:, 0], 1.0 / QL, RMS_EPS, ALU.mult, ALU.add))
                v.tensor_scalar(self.rlat[:, 1], self.rlat[:, 1], 1.0 / KVL, RMS_EPS, ALU.mult, ALU.add).then_inc(s_ms, 1)
                dve.wait_ge(s_std, 1)
                ch.link(v.reciprocal(self.rlat[:], self.rlat[:]))
                dve.wait_ge(s_sin, 1)
                x1, x2, sn, cs = self.kr[:, :, 0:32], self.kr[:, :, 32:64], self.tab[:, 0], self.tab[:, 1]
                ch.link(v.tensor_tensor(self.kr2[:, :, 0, 0:32], x1, cs, ALU.mult))
                ch.link(v.tensor_tensor(tmp, x2, sn, ALU.mult))
                ch.link(v.tensor_tensor(self.kr2[:, :, 0, 0:32], self.kr2[:, :, 0, 0:32], tmp, ALU.subtract))
                ch.link(v.tensor_tensor(self.kr2[:, :, 0, 32:64], x2, cs, ALU.mult))
                ch.link(v.tensor_tensor(tmp, x1, sn, ALU.mult))
                ch.link(v.tensor_tensor(self.kr2[:, :, 0, 32:64], self.kr2[:, :, 0, 32:64], tmp, ALU.add))
                ch.link(v.tensor_copy(self.kr2[:, :, 1, :], self.kr2[:, :, 0, :]))
                dve.wait_ge(s_cw, 96)
                with dve.Fori(0, 4) as i:
                    ch.enter(i, 10)
                    for j in range(2):
                        ch.link(nc.vector.tensor_copy(cwt[:].rearrange("p (a b) -> p a b", a=1), cw[:, bass.ds(i * 2 + j, 1), :]))
                        dve.wait_ge(s_raw[j], i + 2)
                        dve.wait_ge(s_act[j], i + 1)
                        ch.link(nc.vector.tensor_scalar(acc[:, j], raw[:, j, 0:T], cwt[:, 0:1], cwt[:, 5:6], ALU.mult, ALU.add))
                        for tap in range(1, 5):
                            op = nc.vector.scalar_tensor_tensor(out=acc[:, j], in0=raw[:, j, tap:tap + T], scalar=cwt[:, tap:tap + 1],
                                                                in1=acc[:, j], op0=ALU.mult, op1=ALU.add)
                            if tap < 4:
                                ch.link(op)
                        op.then_inc(s_cv[j], 1)
                        dve.wait_ge(s_cv[j], i + 2)
                    ch.leave(4)

    def mlstm_gates(self, up):
        nc, ps = self.nc, self.ps
        s_gb, s_v, s_nf, s_e, s_l = (self.sem(n) for n in ("gate_b_loaded", "gates_dve", "neg_abs_f", "exp_f", "ln_f"))
        s_lf, s_b, s_bc = self.sem("log_f_ready"), self.sem("b_product"), self.sem("b_copied")
        s_rows, s_rowc, s_m, s_mc = self.sem("rows_turned"), self.sem("rows_copied"), self.sem("m_rows_ready"), self.sem("m_columns_turned")
        s_mb, s_mb2, s_f, s_fin = self.sem("m_copied"), self.sem("m_end_spread"), self.sem("factors_in"), self.sem("factors_out")
        s_rdy = self.sem("M_rows_ready")
        s_brow, s_late, s_lcp = self.sem("b_ada_row_loaded"), self.sem("late_product"), self.sem("late_copied")
        s_lw = [self.sem(f"w_ada_late_loaded{j}") for j in range(2)]
        w_ada = self.i["w_ada"].rearrange("(p k) n -> p k n", k=KD)
        modf = self.mod[:].rearrange("p a d -> p (a d)")
        self.acol = self.sb("a_col", [P, 2, TT, H], ctx=up)
        self.mext = self.sb("m_prev", [P, 2, TT + 2, H], ctx=up)
        self.wg = self.sb("wg", [P, 2, TT, H], ctx=up)
        self.dec = self.sb("decay", [P, 2, TT, H], ctx=up)
        self.emm = self.sb("exp_neg_m", [P, 2, TT, H], ctx=up)
        self.Mrow = self.sb("M_rows", [H, 2, T], ctx=up)
        with ExitStack() as x, nc.Block() as block:
            gb = self.sb("gate_b", [P, 16], ctx=x)
            g2 = self.sb("g_if", [P, 2, 2, TT, H], ctx=x)
            nf = self.sb("nf", [P, 2, TT, H], ctx=x)
            lf = self.sb("lf", [P, 2, TT, H], ctx=x)
            bcol = self.sb("b_col", [P, 2, TT, H], ctx=x)
            mcol = self.sb("m_col", [P, 2, 2, TT, H], ctx=x)
            mend = self.sb("m_end", [P, 2, 2, TT, H], ctx=x)
            rows = self.sb("rows", [H, 3, T], ctx=x)
            mrow = self.sb("m_rows", [H, 2, T], ctx=x)
            brow = self.sb("b_ada_row", [1, GATED * 512], ctx=x)
            flat = lambda a: a.rearrange("p d c h -> p (d c h)")
            gt5 = self.gt[:].rearrange("p c (d y h) -> p y d c h", d=2, y=2)

            @block.sync
            def _(sp):
                sp.dma_start(gb[:], self.i["gate_b"].partition_broadcast(P)).then_inc(s_gb, 16)
                for n in range(GATED):
                    if n > 1:
                        sp.wait_ge(s_late, n - 1)
                    at = (EARLY + n) * 512
                    sp.dma_start(self.w_ada_sb[:, n % 2], w_ada[:, :, at:at + 512]).then_inc(s_lw[n % 2], 16)
                    if n == 0:
                        sp.dma_start(brow[:], self.i["b_ada"][EARLY * 512:(EARLY + GATED) * 512].rearrange("(a n) -> a n", a=1)).then_inc(s_brow, 16)

            @block.vector
            def _(dve):
                ch = Chain(dve, s_v)
                v = nc.vector
                dve.wait_ge(s_gb, 16)
                gb5 = gb[:].rearrange("p (d y h) -> p y d h", d=2, y=2)
                for y in range(2):
                    for d in range(2):
                        ch.link(v.tensor_tensor(g2[:, y, d], gt5[:, y, d], gb5[:, y, d].unsqueeze(1).to_broadcast([P, TT, H]), ALU.add))
                f = flat(g2[:, 1])
                v.scalar_tensor_tensor(out=flat(nf[:]), in0=f, scalar=-1.0, in1=f, op0=ALU.mult, op1=ALU.min).then_inc(s_nf, 1)
                dve.wait_ge(s_l, 1)
                v.scalar_tensor_tensor(out=flat(lf[:]), in0=f, scalar=0.0, in1=flat(nf[:]), op0=ALU.min, op1=ALU.subtract).then_inc(s_lf, 1)
                dve.wait_ge(s_b, 1)
                v.tensor_copy(flat(bcol[:]), ps[:, 0, 0:64]).then_inc(s_bc, 1)
                dve.wait_ge(s_bc, 1)
                ch.link(v.tensor_tensor(flat(self.acol[:]), flat(g2[:, 0]), flat(bcol[:]), ALU.subtract))
                for d in range(2):
                    dve.wait_ge(s_rows, d + 1)
                    v.tensor_copy(rows[:], ps[0:H, 1:7, :].rearrange("p (q a) n -> p q (a n)", q=3)).then_inc(s_rowc, 1)
                    dve.wait_ge(s_rowc, d + 1)
                    if d == 0:
                        op = v.tensor_tensor_scan(mrow[:, 0, :], rows[:, 0, :], rows[:, 1, :], 0.0, ALU.add, ALU.max)
                    else:
                        op = v.tensor_tensor_scan(mrow[:, 1, :][:, ::-1], rows[:, 0, :][:, ::-1], rows[:, 1, :][:, ::-1], 0.0, ALU.add, ALU.max)
                    op.then_inc(s_m, 1)
                    dve.wait_ge(s_m, d + 1)
                    v.tensor_tensor(self.Mrow[:, d, :], mrow[:, d, :], rows[:, 2, :], ALU.subtract).then_inc(s_rdy, 1)
                    dve.wait_ge(s_rdy, d + 1)
                dve.wait_ge(s_mc, 1)
                ch.link(v.tensor_copy(flat(mcol[:, 0]), ps[:, 0, 0:64]))
                v.tensor_tensor(flat(mcol[:, 1]), flat(mcol[:, 0]), flat(bcol[:]), ALU.subtract).then_inc(s_mb, 1)
                dve.wait_ge(s_mb2, 1)
                ch.link(v.tensor_copy(mend[:].rearrange("p d q c h -> p (d q c h)"), ps[:, 1, 0:128]))
                ch.link(v.memset(self.mext[:], 0.0))
                ch.link(v.tensor_copy(self.mext[:, 0, 2:TT + 1, :], mend[:, 0, 0, 0:TT - 1, :]))
                ch.link(v.tensor_copy(self.mext[:, 1, 1:TT, :], mend[:, 1, 0, 1:TT, :]))
                for d in range(2):
                    ch.link(v.tensor_tensor(self.wg[:, d], self.acol[:, d], mend[:, d, 1], ALU.subtract))
                    op = v.tensor_tensor(self.dec[:, d], self.mext[:, d, 1:TT + 1, :], mend[:, d, 1], ALU.subtract)
                    if d == 0:
                        ch.link(op)
                op.then_inc(s_f, 1)

            @block.scalar
            def _(act):
                def late(n):
                    act.wait_ge(s_late, n + 1)
                    nc.scalar.activation(modf[:, (EARLY + n) * 512:(EARLY + n + 1) * 512], ps[:, 7, :], ACT.Identity,
                                         bias=0.0 if (EARLY + n) // 2 == 3 else 1.0).then_inc(s_lcp, 1)

                act.wait_ge(s_nf, 1)
                nc.scalar.activation(flat(nf[:]), flat(nf[:]), ACT.Exp).then_inc(s_e, 1)
                act.wait_ge(s_e, 1)
                nc.scalar.activation(flat(nf[:]), flat(nf[:]), ACT.Ln, bias=1.0).then_inc(s_l, 1)
                for n in range(3):
                    late(n)
                act.wait_ge(s_mb, 1)
                nc.scalar.activation(flat(self.emm[:]), flat(mcol[:, 0]), ACT.Exp, scale=-1.0).then_inc(s_fin, 1)
                for n in range(3, GATED):
                    late(n)
                act.wait_ge(s_f, 1)
                nc.scalar.activation(flat(self.wg[:]), flat(self.wg[:]), ACT.Exp).then_inc(s_fin, 1)
                nc.scalar.activation(flat(self.dec[:]), flat(self.dec[:]), ACT.Exp).then_inc(s_fin, 1)

            @block.tensor
            def _(pe):
                done = 0

                def late(count):
                    nonlocal done
                    for n in range(done, done + count):
                        if n == 0:
                            pe.wait_ge(s_brow, 16)
                        else:
                            pe.wait_ge(s_lcp, n)
                        pe.wait_ge(s_lw[n % 2], 16 * (n // 2 + 1))
                        nc.tensor.matmul(ps[:, 7, :], self.c(C_ONE, parts=1), brow[:, n * 512:n * 512 + 512], start=True, stop=False)
                        for k in range(KD):
                            mm = nc.tensor.matmul(ps[:, 7, :], self.ca[:, k:k + 1].to_broadcast([P, P]), self.w_ada_sb[:, n % 2, k, :],
                                                  start=False, stop=k == KD - 1)
                        mm.then_inc(s_late, 1)
                    done += count

                late(1)
                pe.wait_ge(s_lf, 1)
                for d, u in enumerate((C_UFW, C_UBW)):
                    mm = nc.tensor.matmul(ps[:, 0, d * 32:d * 32 + 32], self.c(u), lf[:, d].rearrange("p c h -> p (c h)"), start=True, stop=True)
                mm.then_inc(s_b, 1)
                pe.wait_ge(s_bc, 1)
                for d in range(2):
                    if d:
                        late(1)
                        pe.wait_ge(s_rowc, d)
                    for q, src in enumerate((lf, g2[:, 0], bcol)):
                        for c in range(TT):
                            mm = nc.tensor.matmul(ps[0:H, 1 + 2 * q + c // 4, (c % 4) * P:(c % 4 + 1) * P], src[:, d, c, :], self.c(C_ID),
                                                  start=True, stop=True)
                    mm.then_inc(s_rows, 1)
                late(1)
                pe.wait_ge(s_m, 2)
                for d in range(2):
                    for c in range(TT):
                        mm = nc.tensor.matmul(ps[:, 0, (d * TT + c) * H:(d * TT + c + 1) * H], mrow[:, d, c * P:(c + 1) * P], self.cst[0:H, C_ID:C_ID + H],
                                              start=True, stop=True)
                mm.then_inc(s_mc, 1)
                late(1)
                pe.wait_ge(s_mb, 1)
                pe.wait_ge(s_rowc, 2)
                for d, e in enumerate((C_E127, C_E0)):
                    mm = nc.tensor.matmul(ps[:, 1, d * 64:d * 64 + 64], self.c(e), mcol[:, :, d].rearrange("p q c h -> p q (c h)"), start=True, stop=True)
                mm.then_inc(s_mb2, 1)

    def mlstm(self, up):
        nc, ps = self.nc, self.ps
        N = ("kc", "mb", "sc", "kt", "mask", "z", "w", "y", "a", "p", "q", "kw", "o", "cm", "cn", "h")
        S = {n: [self.sem(f"ml_{n}{d}") for d in range(2)] for n in N}
        s_v, s_c0 = self.sem("ml_dve"), self.sem("ml_state0")
        self.hdir = self.uT[:].rearrange("p (d a) (c n) -> p d (a c) n", d=2, c=2)
        with ExitStack() as x, nc.Block() as block:
            sb = lambda n, s: self.sb(n, s, ctx=x)
            kc, mm_, w, ab, p, q, kw = (sb(n, [P, 2, H, P]) for n in ("kc", "Mm", "W", "ab", "pT", "qs", "kw"))
            cst8 = sb("Caug", [P, 2, H, HD + 1])
            den = sb("den", [P, 2, H])
            hn = HD + 1
            chunk = lambda i, d: i if d == 0 else i * -1 + (TT - 1)

            @block.scalar
            def _(act):
                a = nc.scalar
                with act.Fori(0, TT) as i:
                    for d in range(2):
                        c = chunk(i, d)
                        act.wait_ge(S["kt"][d], i + 1)
                        a.copy(kc[:, d], self.qkT[:, 4:8, bass.ds(c * P, P)]).then_inc(S["kc"][d], 1)
                    for d in range(2):
                        act.wait_ge(S["z"][d], i + 1)
                        act.wait_ge(S["p"][d], i + 1)
                        a.activation(w[:, d], mm_[:, d], ACT.Exp).then_inc(S["w"][d], 1)
                        act.wait_ge(S["y"][d], i + 2)
                        a.activation(ab[:, d], ab[:, d], ACT.Exp).then_inc(S["a"][d], 1)

            @block.tensor
            def _(pe):
                t = nc.tensor
                for n in ("kt", "o", "cm"):
                    for d in range(2):
                        pe.sem_inc(S[n][d], 1)
                pe.wait_ge(s_c0, 1)
                with pe.Fori(0, TT) as i:
                    for d in range(2):
                        c = chunk(i, d)
                        other = i + 1 if d == 0 else i + 2
                        pe.wait_ge(S["y"][1 - d], other)
                        for h in range(H):
                            m = t.matmul(ps[:, 0, h * P:(h + 1) * P], self.cst[0:H, C_SEL + h * P:C_SEL + (h + 1) * P],
                                         self.Mrow[0:H, d, bass.ds(c * P, P)], start=True, stop=True)
                        m.then_inc(S["mb"][d], 1)
                        pe.wait_ge(S["kc"][d], i + 1)
                        pe.wait_ge(S["p"][1 - d], other)
                        for h in range(H):
                            m = t.matmul(ps[:, 1, h * P:(h + 1) * P], kc[:, d, h, :], self.qkT[:, h, bass.ds(c * P, P)], start=True, stop=True)
                        m.then_inc(S["sc"][d], 1)
                        pe.wait_ge(S["kw"][1 - d], other)
                        for h in range(H):
                            m = t.transpose(ps[:, 2, h * P:(h + 1) * P], kc[:, d, h, :], self.c(C_ID))
                        m.then_inc(S["kt"][d], 1)
                    for d in range(2):
                        c = chunk(i, d)
                        other = i + 1 if d == 0 else i + 2
                        pe.wait_ge(S["p"][d], i + 2)
                        pe.wait_ge(S["q"][d], i + 2)
                        pe.wait_ge(S["cn"][d], i + 1)
                        pe.wait_ge(S["h"][1 - d], other)
                        for h in range(H):
                            o = ps[:, 3 + h // 2, (h % 2) * hn:(h % 2 + 1) * hn]
                            t.matmul(o, p[:, d, h, :], self.vaug[:, bass.ds(c, 1), h, :].rearrange("p a e -> p (a e)"), start=True, stop=False)
                            m = t.matmul(o, q[:, d, h, :], cst8[:, d, h, :], start=False, stop=True)
                        m.then_inc(S["o"][d], 1)
                        pe.wait_ge(S["kw"][d], i + 2)
                        pe.wait_ge(S["cn"][1 - d], other)
                        for h in range(H):
                            m = t.matmul(ps[:, 5 + h // 2, (h % 2) * hn:(h % 2 + 1) * hn], kw[:, d, h, :],
                                         self.vaug[:, bass.ds(c, 1), h, :].rearrange("p a e -> p (a e)"), start=True, stop=True)
                        m.then_inc(S["cm"][d], 1)

            @block.vector
            def _(dve):
                v = nc.vector
                ch = Chain(dve, s_v)
                for d in range(2):
                    for n in ("p", "kw", "y", "q", "cn", "h"):
                        dve.sem_inc(S[n][d], 1)
                v.memset(cst8[:], 0.0).then_inc(s_c0, 1)
                dve.wait_ge(s_c0, 1)
                bc = lambda ap: ap.unsqueeze(2).to_broadcast([P, H, P])
                sq = lambda ap: ap.rearrange("p a h -> p (a h)")
                psM = ps[:, 0, :].rearrange("p (h t) -> p h t", h=H)
                psS = ps[:, 1, :].rearrange("p (h t) -> p h t", h=H)
                psK = ps[:, 2, :].rearrange("p (h t) -> p h t", h=H)
                with dve.Fori(0, TT) as i:
                    ch.enter(i, 10)
                    for d in range(2):
                        c = chunk(i, d)
                        mask = self.c((C_MFW, C_MBW)[d]).unsqueeze(1).to_broadcast([P, H, P])
                        dve.wait_ge(S["mb"][d], i + 1)
                        ch.link(v.tensor_tensor(mm_[:, d], psM, mask, ALU.add))
                        v.tensor_tensor(mm_[:, d], bc(sq(self.acol[:, d, bass.ds(c, 1), :])), mm_[:, d], ALU.subtract).then_inc(S["z"][d], 1)
                        v.tensor_tensor(ab[:, d], bc(sq(self.mext[:, d, bass.ds(c + 1, 1), :])), psM, ALU.subtract).then_inc(S["y"][d], 1)
                        dve.wait_ge(S["sc"][d], i + 1)
                        dve.wait_ge(S["w"][d], i + 1)
                        dve.wait_ge(S["o"][d], i + 1)
                        v.scalar_tensor_tensor(out=p[:, d], in0=psS, scalar=QSCALE, in1=w[:, d], op0=ALU.mult, op1=ALU.mult).then_inc(S["p"][d], 1)
                        dve.wait_ge(S["kt"][d], i + 2)
                        dve.wait_ge(S["cm"][d], i + 1)
                        v.tensor_tensor(kw[:, d], psK, bc(sq(self.wg[:, d, bass.ds(c, 1), :])), ALU.mult).then_inc(S["kw"][d], 1)
                        dve.wait_ge(S["a"][d], i + 1)
                        v.scalar_tensor_tensor(out=q[:, d], in0=self.qkT[:, 0:H, bass.ds(c * P, P)], scalar=QSCALE, in1=ab[:, d],
                                               op0=ALU.mult, op1=ALU.mult).then_inc(S["q"][d], 1)
                    for d in range(2):
                        c = chunk(i, d)
                        dve.wait_ge(S["o"][d], i + 2)
                        po = ps[:, 3:5, 0:2 * hn].rearrange("p b (h e) -> p b h e", h=2)
                        den4 = den[:, d].rearrange("p (b h a) -> p b h a", b=2, a=1)
                        em4 = self.emm[:, d, bass.ds(c, 1), :].rearrange("p a (b h) -> p b h a", b=2)
                        ch.link(v.scalar_tensor_tensor(out=den4, in0=po[:, :, :, HD:hn], scalar=-1.0, in1=em4, op0=ALU.mult, op1=ALU.max))
                        ch.link(v.tensor_tensor(den4, den4, po[:, :, :, HD:hn], ALU.max))
                        ch.link(v.reciprocal(den[:, d], den[:, d]))
                        v.tensor_tensor(self.hdir[:, d, bass.ds(c, 1), :].rearrange("p a (b h e) -> p (a b) h e", b=2, h=2),
                                        po[:, :, :, 0:HD], den4.to_broadcast([P, 2, 2, HD]), ALU.mult).then_inc(S["h"][d], 1)
                        dve.wait_ge(S["cm"][d], i + 2)
                        pc = ps[:, 5:7, 0:2 * hn].rearrange("p b (h e) -> p b h e", h=2)
                        dc = self.dec[:, d, bass.ds(c, 1), :].rearrange("p a (b h) -> p b h a", b=2)
                        c4 = cst8[:, d].rearrange("p (b h) e -> p b h e", b=2)
                        ch.link(v.tensor_tensor(c4, c4, dc.to_broadcast([P, 2, 2, hn]), ALU.mult))
                        v.tensor_tensor(c4, c4, pc, ALU.add).then_inc(S["cn"][d], 1)
                    ch.leave(TT)

    def mlstm_norm(self):
        nc, ps = self.nc, self.ps
        s_gm = self.sem("gate_gain_ready")
        s_g, s_v, s_var, s_std, s_sig, s_sq, s_cen = (self.sem(n) for n in ("mh_g_loaded", "mln_dve", "mln_var", "mln_std", "o_sigmoid", "mln_squared", "mln_centred"))
        G = TT * H
        s_brow, s_late = self.sem("b_ada_rest_loaded"), self.sem("rest_product")
        s_lw = [self.sem(f"w_ada_rest_loaded{j}") for j in range(2)]
        w_ada = self.i["w_ada"].rearrange("(p k) n -> p k n", k=KD)
        modf = self.mod[:].rearrange("p a d -> p (a d)")
        with ExitStack() as x, nc.Block() as block:
            brow = self.sb("b_ada_rest", [1, LATE * 512], ctx=x)
            w1 = self.sb("w_ada_rest", [P, KD, 512], ctx=x)
            w0 = self.vaug[:].rearrange("p t h e -> p (t h e)")[:, 0:KD * 512].rearrange("p (k n) -> p k n", k=KD)
            g = self.sb("mh_g", [P, H * HD], ctx=x)
            sq = self.qkT
            sm = self.sb("mln_sum", [P, G], ctx=x)
            grp = lambda ap: ap.rearrange("p t (h e) -> p (t h) e", h=H)
            hf, hb = grp(self.hdir[:, 0]), grp(self.hdir[:, 1])
            sqv = sq[:, 0:4].rearrange("p k (g e) -> p (k g) e", e=HD)
            bc = lambda ap: ap.unsqueeze(2).to_broadcast([P, G, HD])

            @block.sync
            def _(sp):
                sp.dma_start(brow[:], self.i["b_ada"][(EARLY + GATED) * 512:].rearrange("(a n) -> a n", a=1)).then_inc(s_brow, 16)
                for n in range(LATE):
                    if n > 1:
                        sp.wait_ge(s_late, n - 1)
                    at = (EARLY + GATED + n) * 512
                    sp.dma_start((w0, w1[:])[n % 2], w_ada[:, :, at:at + 512]).then_inc(s_lw[n % 2], 16)
                    if n == 1:
                        sp.dma_start(g[:], self.i["mh_norm_g"].partition_broadcast(P)).then_inc(s_g, 16)

            @block.tensor
            def _(pe):
                pe.wait_ge(s_brow, 16)
                for n in range(LATE):
                    pe.wait_ge(s_lw[n % 2], 16 * (n // 2 + 1))
                    nc.tensor.matmul(ps[:, n, :], self.c(C_ONE, parts=1), brow[:, n * 512:n * 512 + 512], start=True, stop=False)
                    for k in range(KD):
                        mm = nc.tensor.matmul(ps[:, n, :], self.ca[:, k:k + 1].to_broadcast([P, P]), (w0, w1[:])[n % 2][:, k, :],
                                              start=False, stop=k == KD - 1)
                    mm.then_inc(s_late, 1)

            @block.gpsimd
            def _(pool):
                pool.wait_ge(s_g, 16)
                pool.wait_ge(s_sig, 1)
                nc.gpsimd.tensor_tensor(self.hm[:], self.hm[:], g[:].unsqueeze(1).to_broadcast([P, TT, H * HD]), ALU.mult).then_inc(s_gm, 1)

            @block.scalar
            def _(act):
                def late(n):
                    act.wait_ge(s_late, n + 1)
                    m = EARLY + GATED + n
                    nc.scalar.activation(modf[:, m * 512:(m + 1) * 512], ps[:, n, :], ACT.Identity,
                                         bias=0.0 if m // 2 == 3 else 1.0)

                nc.scalar.activation(self.hm[:], self.hm[:], ACT.Sigmoid).then_inc(s_sig, 1)
                act.wait_ge(s_cen, 1)
                nc.scalar.activation(sqv, hf, ACT.Square).then_inc(s_sq, 1)
                late(0)
                act.wait_ge(s_var, 1)
                nc.scalar.activation(sm[:], sm[:], ACT.Sqrt).then_inc(s_std, 1)
                for n in range(1, LATE):
                    late(n)

            @block.vector
            def _(dve):
                v = nc.vector
                ch = Chain(dve, s_v)
                ch.link(v.tensor_tensor(hf, hf, hb, ALU.add))
                ch.link(v.tensor_reduce(sm[:], hf, AX, ALU.add))
                ch.link(v.tensor_scalar_mul(sm[:], sm[:], 1.0 / HD))
                v.tensor_tensor(hf, hf, bc(sm[:]), ALU.subtract).then_inc(s_cen, 1)
                dve.wait_ge(s_sq, 1)
                ch.link(v.tensor_reduce(sm[:], sqv, AX, ALU.add))
                v.tensor_scalar(sm[:], sm[:], 1.0 / HD, LN_EPS, ALU.mult, ALU.add).then_inc(s_var, 1)
                dve.wait_ge(s_std, 1)
                ch.link(v.reciprocal(sm[:], sm[:]))
                dve.wait_ge(s_cen, 1)
                ch.link(v.tensor_tensor(hf, hf, bc(sm[:]), ALU.mult))
                dve.wait_ge(s_gm, 1)
                ch.link(v.tensor_tensor(grp(self.hm[:]), grp(self.hm[:]), hf, ALU.mult))

    def attention(self):
        with ExitStack() as at:
            self.latent_projections(at)
            self.attend()

    def latent_projections(self, at):
        nc, ps = self.nc, self.ps
        s_w, s_gg, s_v = self.sem("w_lat_loaded"), self.sem("lat_g_loaded"), self.sem("lat_dve")
        s_n, s_kr, s_tr, s_cT, s_tre = (self.sem(n) for n in ("lat_normed", "kr_tile", "lat_transposed", "latT_ready", "krT_copied"))
        s_qn, s_kn, s_qr, s_va = (self.sem(n) for n in ("qn_product", "kn_product", "qr_product", "va_product"))
        s_qne, s_kne, s_qrot, s_vae, s_qrt, s_qrte = (self.sem(n) for n in ("qn_copied", "kn_copied", "qr_rotated", "va_copied", "qr_transposed", "qrT_copied"))
        self.qnT = self.sb("qnT", [P, TT + 1, H, P], ctx=at)
        self.qrT = self.sb("qrT", [P, TT + 1, 2, P], ctx=at)
        self.knT = self.sb("knT", [P, H, T], ctx=at)
        self.krT = self.sb("krT", [P, T], ctx=at)
        self.va = self.sb("va", [P, TT, H * HD], ctx=at)
        NL = QL // P + KVL // P
        with ExitStack() as x, nc.Block() as block:
            wof, nq, nkv = self.wo[:].rearrange("p k n -> p (k n)"), QL // P * H * (HD + RO), KVL // P * H * 2 * HD
            wq = wof[:, 0:nq].rearrange("p (k n) -> p k n", k=QL // P)
            wkv = wof[:, nq:nq + nkv].rearrange("p (k n) -> p k n", k=KVL // P)
            gg = self.sb("lat_g", [P, NL], ctx=x)
            tn = self.sb("lat_tile", [P, QL + KVL + 2 * RO], ctx=x)
            cT = self.sb("latT", [P, 2, NL, P], ctx=x)
            qr = self.sb("qr_tile", [P, H, RO], ctx=x)
            tmp = self.sb("qr_tmp", [P, H, 32], ctx=x)

            @block.sync
            def _(sp):
                sp.dma_start(wq, self.i["w_uq"].rearrange("(k p) n -> p k n", p=P)).then_inc(s_w, 16)
                sp.dma_start(wkv, self.i["w_ukv"].rearrange("(k p) n -> p k n", p=P)).then_inc(s_w, 16)
                with nc.allow_non_contiguous_dma("gains with a channel to a partition"):
                    sp.dma_start(gg[:, 0:QL // P], self.i["q_norm_g"].rearrange("(k p) -> p k", p=P)).then_inc(s_gg, 16)
                    sp.dma_start(gg[:, QL // P:NL], self.i["kv_norm_g"].rearrange("(k p) -> p k", p=P)).then_inc(s_gg, 16)

            @block.gpsimd
            def _(pool):
                nc.gpsimd.memset(self.qnT[:, TT:TT + 1], 0.0)
                nc.gpsimd.memset(self.qrT[:, TT:TT + 1], 0.0)

            @block.vector
            def _(dve):
                v = nc.vector
                ch = Chain(dve, s_v)
                for s in (s_kne, s_qrot):
                    dve.sem_inc(s, 1)
                def norm(t):
                    dve.wait_ge(s_tr, t + 1)
                    ch.link(v.tensor_tensor(tn[:, 0:QL].unsqueeze(1), self.cq[:, bass.ds(t, 1), :],
                                            self.rlat[:, 0, bass.ds(t, 1)].unsqueeze(2).to_broadcast([P, 1, QL]), ALU.mult))
                    v.tensor_tensor(tn[:, QL:QL + KVL].unsqueeze(1), self.ckv[:, bass.ds(t, 1), :],
                                    self.rlat[:, 1, bass.ds(t, 1)].unsqueeze(2).to_broadcast([P, 1, KVL]), ALU.mult).then_inc(s_n, 1)

                def rotate(t):
                    dve.wait_ge(s_kn, t + 1)
                    v.tensor_copy(self.knT[:, :, bass.ds(t * P, P)], ps[:, 3, :].rearrange("p (h t) -> p h t", h=H)).then_inc(s_kne, 1)
                    dve.wait_ge(s_qr, t + 1)
                    dve.wait_ge(s_qrt, t + 1)
                    pq = ps[:, 4, 0:H * RO].rearrange("p (h e) -> p h e", h=H)
                    x1, x2 = pq[:, :, 0:32], pq[:, :, 32:64]
                    sn = self.tab[:, 0, bass.ds(t, 1), :].to_broadcast([P, H, 32])
                    cs = self.tab[:, 1, bass.ds(t, 1), :].to_broadcast([P, H, 32])
                    ch.link(v.tensor_tensor(qr[:, :, 0:32], x1, cs, ALU.mult))
                    ch.link(v.tensor_tensor(tmp[:], x2, sn, ALU.mult))
                    ch.link(v.tensor_tensor(qr[:, :, 0:32], qr[:, :, 0:32], tmp[:], ALU.subtract))
                    ch.link(v.tensor_tensor(qr[:, :, 32:64], x2, cs, ALU.mult))
                    ch.link(v.tensor_tensor(tmp[:], x1, sn, ALU.mult))
                    v.tensor_tensor(qr[:, :, 32:64], qr[:, :, 32:64], tmp[:], ALU.add).then_inc(s_qrot, 1)

                norm(0)
                with dve.Fori(0, TT // 2 - 1) as i:
                    ch.enter(i, 12)
                    for j in range(2):
                        norm(i * 2 + j + 1)
                        rotate(i * 2 + j)
                    ch.leave(TT // 2 - 1)
                norm(TT - 1)
                rotate(TT - 2)
                rotate(TT - 1)

            @block.scalar
            def _(act):
                a = nc.scalar
                for s in (s_qne, s_vae, s_tre, s_qrte):
                    act.sem_inc(s, 1)
                act.wait_ge(s_gg, 32)
                def key_tile(t):
                    act.wait_ge(s_tr, t + 1)
                    a.copy(tn[:, QL + KVL:].rearrange("p (a b c) -> p a b c", a=1, b=2), self.kr2[:, bass.ds(t, 1)]).then_inc(s_kr, 1)

                def turned(t, j):
                    act.wait_ge(s_tr, t + 2)
                    for l in range(NL):
                        op = a.mul(cT[:, j, l, :], ps[:, l // 4, (l % 4) * P:(l % 4 + 1) * P], gg[:, l:l + 1])
                    op.then_inc(s_cT, 1)
                    a.copy(self.krT[:, bass.ds(t * P, P)], ps[:, NL // 4, (NL % 4) * P:(NL % 4 + 1) * P]).then_inc(s_tre, 1)

                def copies(t):
                    act.wait_ge(s_qn, t + 1)
                    a.copy(self.qnT[:, bass.ds(t, 1)], ps[:, 2, :].rearrange("p (a h t) -> p a h t", a=1, h=H)).then_inc(s_qne, 1)
                    act.wait_ge(s_va, t + 1)
                    a.copy(self.va[:, bass.ds(t, 1), :], ps[:, 5, :].rearrange("p (a n) -> p a n", a=1)).then_inc(s_vae, 1)
                    act.wait_ge(s_qrt, t + 2)
                    a.copy(self.qrT[:, bass.ds(t, 1)], ps[:, 6, 0:2 * P].rearrange("p (a b t) -> p a b t", a=1, b=2)).then_inc(s_qrte, 1)

                key_tile(0)
                turned(0, 0)
                with act.Fori(0, TT // 2 - 1) as i:
                    for j in range(2):
                        key_tile(i * 2 + j + 1)
                        turned(i * 2 + j + 1, 1 - j)
                        copies(i * 2 + j)
                key_tile(TT - 1)
                turned(TT - 1, 1)
                copies(TT - 2)
                copies(TT - 1)

            @block.tensor
            def _(pe):
                m_ = nc.tensor
                ident = self.c(C_ID)
                pe.sem_inc(s_tr, 1)
                pe.sem_inc(s_qrt, 1)
                pe.wait_ge(s_w, 32)
                nq = QL // P

                def turn(t):
                    pe.wait_ge(s_n, t + 1)
                    pe.wait_ge(s_kr, t + 1)
                    pe.wait_ge(s_tre, t + 1)
                    for j in range(NL + 1):
                        m = m_.transpose(ps[:, j // 4, (j % 4) * P:(j % 4 + 1) * P], tn[:, j * P:(j + 1) * P], ident)
                    m.then_inc(s_tr, 1)

                def products1(t, j):
                    pe.wait_ge(s_cT, t + 1)
                    pe.wait_ge(s_qrot, t + 1)
                    for k in range(nq):
                        m = m_.matmul(ps[:, 4, 0:H * RO], cT[:, j, k, :], wq[:, k, :].rearrange("p (h e) -> p h e", h=H)[:, :, HD:],
                                      start=k == 0, stop=k == nq - 1)
                    m.then_inc(s_qr, 1)
                    pe.wait_ge(s_kne, t + 1)
                    for h in range(H):
                        for k in range(KVL // P):
                            m = m_.matmul(ps[:, 3, h * P:(h + 1) * P], wkv[:, k, h * 256:h * 256 + P], cT[:, j, nq + k, :],
                                          start=k == 0, stop=k == KVL // P - 1)
                    m.then_inc(s_kn, 1)

                def products2(t, j):
                    pe.wait_ge(s_qne, t + 1)
                    for h in range(H):
                        for k in range(nq):
                            m = m_.matmul(ps[:, 2, h * P:(h + 1) * P], wq[:, k, h * 192:h * 192 + P], cT[:, j, k, :],
                                          start=k == 0, stop=k == nq - 1)
                    m.then_inc(s_qn, 1)
                    pe.wait_ge(s_vae, t + 1)
                    for k in range(KVL // P):
                        m = m_.matmul(ps[:, 5, :], cT[:, j, nq + k, :], wkv[:, k, :].rearrange("p (h e) -> p h e", h=H)[:, :, HD:],
                                      start=k == 0, stop=k == KVL // P - 1)
                    m.then_inc(s_va, 1)
                    pe.wait_ge(s_qrot, t + 2)
                    pe.wait_ge(s_qrte, t + 1)
                    for pair in range(2):
                        m = m_.transpose(ps[:, 6, pair * P:(pair + 1) * P], qr[:, 2 * pair:2 * pair + 2, :].rearrange("p h e -> p (h e)"), ident)
                    m.then_inc(s_qrt, 1)

                turn(0)
                with pe.Fori(0, TT // 2 - 1) as i:
                    for j in range(2):
                        products1(i * 2 + j, j)
                        turn(i * 2 + j + 1)
                        products2(i * 2 + j, j)
                products1(TT - 2, 0)
                turn(TT - 1)
                products2(TT - 2, 0)
                products1(TT - 1, 1)
                products2(TT - 1, 1)

    def attend(self):
        nc, ps = self.nc, self.ps
        s_q, s_S, s_nm, s_p, s_t, s_td, s_ta, s_o, s_oe, s_v, s_mx = (self.sem(n) for n in (
            "q_tile", "scores", "neg_max", "probs", "probs_turned", "pT_dve", "pT_act", "attn_out", "attn_copied", "att_dve", "maxed"))
        with ExitStack() as x, nc.Block() as block:
            qs = self.sb("qs_tile", [P, H, P], ctx=x)
            qrs = self.sb("qrs_tile", [P, 2, P], ctx=x)
            pb = self.sb("probs", [P, 2, T], ctx=x)
            pT = self.sb("probsT", [P, TT, P], ctx=x)
            mx = self.sb("mx", [P, 2], ctx=x)
            nm = self.sb("nm", [P, 2], ctx=x)
            rs = self.sb("rs", [P, 2], ctx=x)
            ri = self.sb("ri", [P, 2], ctx=x)

            @block.sync
            def _(sp):
                sp.dma_start(self.wo[:], self.i["w_out"].rearrange("(k p) n -> p k n", p=P)).then_inc(self.s_wo, 16)

            @block.tensor
            def _(pe):
                m_ = nc.tensor

                def scores(h):
                    b = 2 * (h % 2)
                    lo = RO * (h % 2)
                    for half in range(2):
                        sl = slice(half * 512, half * 512 + 512)
                        m_.matmul(ps[:, b + half, :], qs[:, h, :], self.knT[:, h, sl], start=True, stop=False)
                        m = m_.matmul(ps[:, b + half, :], qrs[lo:lo + RO, h // 2, :], self.krT[lo:lo + RO, sl], start=False, stop=True)
                    m.then_inc(s_S, 1)

                pe.wait_ge(s_q, 1)
                scores(0)
                scores(1)
                with pe.Fori(0, TT) as t:
                    for h in range(H):
                        n = t * H + h
                        pe.wait_ge(s_p, n + 1)
                        for k in range(TT):
                            m = m_.transpose(ps[:, 4 + k // 4, (k % 4) * P:(k % 4 + 1) * P], pb[:, h % 2, k * P:(k + 1) * P], self.c(C_ID))
                        m.then_inc(s_t, 1)
                        if h == H - 2:
                            pe.wait_ge(s_q, t + 2)
                        scores((h + 2) % H)
                        pe.wait_ge(s_td, n + 1)
                        pe.wait_ge(s_ta, n + 1)
                        pe.wait_ge(s_oe, n + 1)
                        for k in range(TT):
                            m = m_.matmul(ps[:, 6, 0:HD], pT[:, k, :], self.va[:, k, h * HD:(h + 1) * HD], start=k == 0, stop=k == TT - 1)
                        m.then_inc(s_o, 1)

            @block.scalar
            def _(act):
                a = nc.scalar
                a.copy(qs[:], self.qnT[:, 0])
                a.copy(qrs[:], self.qrT[:, 0]).then_inc(s_q, 1)
                with act.Fori(0, TT) as t:
                    for h in range(H):
                        n = t * H + h
                        act.wait_ge(s_nm, n + 1)
                        a.activation(pb[:, h % 2, :], ps[:, 2 * (h % 2):2 * (h % 2) + 2, :].rearrange("p a b -> p (a b)"), ACT.Exp,
                                     bias=nm[:, h % 2:h % 2 + 1], scale=ASCALE, accum_out=rs[:, h % 2:h % 2 + 1]).then_inc(s_p, 1)
                        if h == H - 2:
                            act.wait_ge(s_S, n + 2)
                            a.copy(qs[:], self.qnT[:, bass.ds(t + 1, 1)].rearrange("p a h t -> p (a h) t"))
                            a.copy(qrs[:], self.qrT[:, bass.ds(t + 1, 1)].rearrange("p a h t -> p (a h) t")).then_inc(s_q, 1)
                        act.wait_ge(s_t, n + 1)
                        a.copy(pT[:, 4:8, :], ps[:, 5, :].rearrange("p (k t) -> p k t", k=4)).then_inc(s_ta, 1)

            @block.vector
            def _(dve):
                v = nc.vector
                ch = Chain(dve, s_v)
                dve.sem_inc(s_oe, 1)

                def maximum(n, j):
                    dve.wait_ge(s_S, n + 1)
                    ch.link(v.tensor_reduce(mx[:, j:j + 1], ps[:, 2 * j:2 * j + 2, :].rearrange("p a b -> p (a b)"), AX, ALU.max))
                    v.tensor_scalar_mul(nm[:, j:j + 1], mx[:, j:j + 1], -ASCALE).then_inc(s_nm, 1)

                maximum(0, 0)
                with dve.Fori(0, TT) as t:
                    ch.enter(t, 2 * H)
                    for h in range(H):
                        n = t * H + h
                        j = h % 2
                        dve.wait_ge(s_t, n + 1)
                        v.tensor_copy(pT[:, 0:4, :], ps[:, 4, :].rearrange("p (k t) -> p k t", k=4)).then_inc(s_td, 1)
                        maximum(n + 1, 1 - j)
                        ch.link(v.reciprocal(ri[:, j:j + 1], rs[:, j:j + 1]))
                        dve.wait_ge(s_o, n + 1)
                        v.tensor_scalar(self.oa[:, bass.ds(t, 1), h * HD:(h + 1) * HD], ps[:, 6, 0:HD].unsqueeze(1), ri[:, j:j + 1], None,
                                        ALU.mult).then_inc(s_oe, 1)
                    ch.leave(TT)

    def output_projection(self):
        nc, ps, mod = self.nc, self.ps, self.mod
        s_x, s_w, s_row, s_v, s_osq, s_oms, s_ostd, s_oan = (self.sem(n) for n in (
            "x_all_loaded", "w_router_loaded", "rows_loaded", "op_dve", "oa_squared", "oa_var", "oa_std", "oa_normed"))
        s_hc, s_ht, s_hT, s_y, s_ye = (self.sem(n) for n in ("h_tile", "h_turned", "hT_ready", "y_product", "y_read"))
        s_v1, s_s1, s_v2, s_s2, s_u, s_ut, s_uT, s_l, s_le, s_st = (self.sem(n) for n in (
            "varA", "stdA", "varB", "stdB", "u2_ready", "u2_turned", "u2T_ready", "logits_product", "logits_copied", "u2_stored"))
        s_x1, s_x1st = self.sem("x1_ready"), self.sem("x1_stored")
        with ExitStack() as x, nc.Block() as block:
            sb = lambda n, s: self.sb(n, s, ctx=x)
            x1 = sb("x1", [P, TT, D])
            wo = self.wo
            wr = sb("w_router", [P, KD, NG + E])
            ag = sb("attn_g", [P, H * HD])
            g1 = sb("ln1_g", [P, D])
            b1 = sb("ln1_b", [P, D])
            ro = sb("oa_rstd", [P, TT])
            hT = sb("hT", [P, KD, P])
            z = sb("z", [P, D])
            u2 = sb("u2", [P, D])
            uT = sb("u2T", [P, KD, P])
            oc = sb("oc", [P, 1])
            st, mv, ve = sb("stB", [P, 2, 6]), sb("mvB", [P, 2]), sb("veB", [P, 2])
            hc = sb("h_cat", [P, D])
            sqh = sb("oa_sq", [P, H * HD])

            @block.sync
            def _(sp):
                sp.dma_start(ag[:], self.i["attn_norm_g"].partition_broadcast(P)).then_inc(s_row, 16)
                sp.dma_start(g1[:], self.i["ln1_g"].partition_broadcast(P)).then_inc(s_row, 16)
                sp.dma_start(b1[:], self.i["ln1_b"].partition_broadcast(P)).then_inc(s_row, 16)
                sp.dma_start(x1[:], self.i["x"].rearrange("(t p) d -> p t d", p=P)).then_inc(s_x, 16)
                with nc.allow_non_contiguous_dma("narrow router weights"):
                    sp.dma_start(wr[:, :, 0:NG], self.i["w_rg"].rearrange("(k p) n -> p k n", p=P)).then_inc(s_w, 16)
                    sp.dma_start(wr[:, :, NG:], self.i["w_re"].rearrange("(k p) n -> p k n", p=P)).then_inc(s_w, 16)
                sp.sem_inc(s_st, 16)
                with sp.Fori(0, TT) as t:
                    sp.wait_ge(s_x1, t + 1)
                    sp.dma_start(self.x1d.rearrange("(t p) d -> t p d", p=P)[bass.ds(t, 1)].rearrange("a p d -> p (a d)"),
                                 x1[:, bass.ds(t, 1), :].rearrange("p a d -> p (a d)")).then_inc(s_x1st, 16)
                    sp.wait_ge(s_u, t + 1)
                    sp.dma_start(self.u2d.rearrange("(t p) d -> t p d", p=P)[bass.ds(t, 1)].rearrange("a p d -> p (a d)"), u2[:]).then_inc(s_st, 16)
                sp.wait_ge(s_st, 16 * TT + 16)
                sp.wait_ge(s_x1st, 16 * TT)

            @block.scalar
            def _(act):
                a = nc.scalar
                for t in range(TT):
                    a.activation(sqh[:], self.oa[:, t, :], ACT.Square, accum_out=ro[:, t:t + 1]).then_inc(s_osq, 1)
                    act.wait_ge(s_osq, t + 1)
                act.wait_ge(s_oms, 1)
                a.activation(ro[:], ro[:], ACT.Sqrt).then_inc(s_ostd, 1)
                def side_by_side(t, first=False):
                    if not first:
                        act.wait_ge(s_ht, t)
                    act.wait_ge(s_oan, t + 1)
                    a.copy(hc[:, 0:512].rearrange("p (a n) -> p a n", a=1), self.hm[:, bass.ds(t, 1), :])
                    a.copy(hc[:, 512:].rearrange("p (a n) -> p a n", a=1), self.oa[:, bass.ds(t, 1), :]).then_inc(s_hc, 1)

                def turned(t):
                    act.wait_ge(s_ht, t + 1)
                    a.copy(hT[:].rearrange("p k t -> p (k t)"), ps[:, 0:2, :].rearrange("p a b -> p (a b)")).then_inc(s_hT, 1)

                def std1(t):
                    act.wait_ge(s_v1, t + 1)
                    a.activation(ve[:, 1:2], ve[:, 0:1], ACT.Sqrt).then_inc(s_s1, 1)

                def back(t):
                    act.wait_ge(s_v2, t + 1)
                    a.activation(ve[:, 1:2], ve[:, 0:1], ACT.Sqrt).then_inc(s_s2, 1)
                    act.wait_ge(s_ut, t + 1)
                    a.copy(uT[:].rearrange("p k t -> p (k t)"), ps[:, 4:6, :].rearrange("p a b -> p (a b)")).then_inc(s_uT, 1)
                    act.wait_ge(s_l, t + 1)
                    a.copy(self.lg[:, bass.ds(t, 1), :], ps[:, 6, 0:NG + E].rearrange("p (a n) -> p a n", a=1)).then_inc(s_le, 1)

                side_by_side(0, first=True)
                turned(0)
                side_by_side(1)
                with act.Fori(0, TT - 2) as t:
                    std1(t)
                    turned(t + 1)
                    side_by_side(t + 2)
                    back(t)
                std1(TT - 2)
                turned(TT - 1)
                back(TT - 2)
                std1(TT - 1)
                back(TT - 1)

            @block.tensor
            def _(pe):
                m_ = nc.tensor
                ident = self.c(C_ID)

                def front(t, first=False):
                    pe.wait_ge(s_hc, t + 1)
                    if not first:
                        pe.wait_ge(s_hT, t)
                    for k in range(KD):
                        m = m_.transpose(ps[:, k // 4, (k % 4) * P:(k % 4 + 1) * P], hc[:, k * P:(k + 1) * P], ident)
                    m.then_inc(s_ht, 1)
                    pe.wait_ge(s_hT, t + 1)
                    if not first:
                        pe.wait_ge(s_ye, t)
                    for half in range(2):
                        for k in range(KD):
                            m = m_.matmul(ps[:, 2 + half, :], hT[:, k, :], wo[:, k, half * 512:half * 512 + 512], start=k == 0, stop=k == KD - 1)
                    m.then_inc(s_y, 1)

                def back(t):
                    pe.wait_ge(s_u, t + 1)
                    pe.wait_ge(s_le, t + 1)
                    for k in range(KD):
                        m = m_.transpose(ps[:, 4 + k // 4, (k % 4) * P:(k % 4 + 1) * P], u2[:, k * P:(k + 1) * P], ident)
                    m.then_inc(s_ut, 1)
                    pe.wait_ge(s_uT, t + 1)
                    for k in range(KD):
                        m = m_.matmul(ps[:, 6, 0:NG + E], uT[:, k, :], wr[:, k, :], start=k == 0, stop=k == KD - 1)
                    m.then_inc(s_l, 1)

                pe.sem_inc(s_le, 1)
                pe.wait_ge(self.s_wo, 16)
                front(0, first=True)
                pe.wait_ge(s_w, 32)
                with pe.Fori(0, TT - 1) as t:
                    front(t + 1)
                    back(t)
                back(TT - 1)

            @block.vector
            def _(dve):
                v = nc.vector
                ch = Chain(dve, s_v)
                dve.wait_ge(s_osq, TT)
                v.tensor_scalar(ro[:], ro[:], 1.0 / (H * HD), RMS_EPS, ALU.mult, ALU.add).then_inc(s_oms, 1)
                dve.wait_ge(s_ostd, 1)
                ch.link(v.reciprocal(ro[:], ro[:]))
                dve.wait_ge(s_row, 48)
                for t in range(TT):
                    v.scalar_tensor_tensor(out=self.oa[:, t, :], in0=self.oa[:, t, :], scalar=ro[:, t:t + 1], in1=ag[:], op0=ALU.mult, op1=ALU.mult).then_inc(s_oan, 1)
                dve.wait_ge(s_x, 16)
                one = lambda ap: ap.unsqueeze(1)

                def normed(src, s_var, s_std, t, gain, shift, out, free=None):
                    ch.link(v.bn_stats(st[:, 0, :], src[:, 0:512]))
                    ch.link(v.bn_stats(st[:, 1, :], src[:, 512:1024]))
                    v.tensor_copy(oc[:], self.cst[:, 0:1])
                    ch.link(v.bn_aggr(mv[:], st[:].rearrange("p a b -> p (a b)")))
                    v.tensor_scalar_add(ve[:, 0:1], mv[:, 1:2], LN_EPS).then_inc(s_var, 1)
                    dve.wait_ge(s_std, t + 1)
                    ch.link(v.reciprocal(ve[:, 1:2], ve[:, 1:2]))
                    ch.link(v.scalar_tensor_tensor(out=z[:], in0=src, scalar=mv[:, 0:1], in1=gain, op0=ALU.subtract, op1=ALU.mult))
                    if free:
                        free()
                    return v.scalar_tensor_tensor(out=out, in0=z[:], scalar=ve[:, 1:2], in1=shift, op0=ALU.mult, op1=ALU.add)

                with dve.Fori(0, TT) as t:
                    ch.enter(t, 12)
                    dve.wait_ge(s_y, t + 1)
                    v.tensor_tensor(z[:], ps[:, 2:4, :].rearrange("p a b -> p (a b)"), mod[:, 2, :], ALU.mult).then_inc(s_ye, 1)
                    dve.wait_ge(s_ye, t + 1)
                    ch.link(v.scalar_tensor_tensor(out=one(z[:]), in0=x1[:, bass.ds(t, 1), :], scalar=ALPHA, in1=one(z[:]), op0=ALU.mult, op1=ALU.add))
                    ch.link(normed(z[:], s_v1, s_s1, t, g1[:], b1[:], z[:]))
                    v.tensor_scalar_mul(x1[:, bass.ds(t, 1), :], one(z[:]), 1.0).then_inc(s_x1, 1)
                    dve.wait_ge(s_x1, t + 1)

                    def u2_free():
                        dve.wait_ge(s_le, t + 1)
                        dve.wait_ge(s_st, t * 16 + 16)

                    normed(z[:], s_v2, s_s2, t, mod[:, 4, :], mod[:, 3, :], u2[:], u2_free).then_inc(s_u, 1)
                    dve.wait_ge(s_u, t + 1)
                    ch.leave(TT)

    def routing(self, ctx):
        nc, ps = self.nc, self.ps
        s_b, s_v, s_d, s_e, s_d2, s_e2, s_A, s_rank, s_pos, s_fill, s_init, s_ids, s_sc, s_asg = (self.sem(n) for n in (
            "router_b", "rt_dve", "g_shifted", "g_exp", "e_gap", "e_exp", "assigned", "ranked", "positions_ready", "fill_ready",
            "slotmap_cleared", "ids_ready", "scattered", "asg_loaded"))
        self.wts = self.sb("pair_weights", [P, 2, TT], ctx=ctx)
        self.asg = self.sb("block_asg", [P, NB], I32, ctx=ctx)
        self.tok = self.sb("block_tok", [P, NB], I32, ctx=ctx)
        self.tbl = self.sb("block_table", [1, 6, NB], I32, ctx=ctx)
        with ExitStack() as x, nc.Block() as block:
            sb = lambda n, s, dt=F32: self.sb(n, s, dt, ctx=x)
            br = sb("b_router", [P, NG + E])
            gx = sb("g_work", [P, 3, TT, NG])
            gm, gs, gw = sb("g_max", [P, TT]), sb("g_sel", [P, TT]), sb("g_w", [P, TT])
            em, eq = sb("e_masked", [P, TT, E]), sb("e_eq", [P, TT, E])
            oh = sb("one_hot", [P, 2, TT, E])
            A = sb("assigned", [P, TT, E])
            mk = sb("e_top", [P, 2, TT])
            sel = sb("e_sel", [P, TT])
            eg = sb("e_gap", [P, TT])
            cnt, nbk, bend, bst = sb("cnt", [P, E]), sb("nbk", [P, E]), sb("bend", [P, E]), sb("bst", [P, E])
            ci = sb("cnt_i", [P, E], I32)
            zero = sb("zero_e", [P, E])
            pos = sb("pos", [P, 2, TT])
            posi = sb("pos_i32", [P, 2, TT], I32)
            ids = sb("ids", [P, 2, TT], I32)
            fill = sb("fill", [P, NB], I32)
            cmp_ = sb("cmp", [1, NB, NB])
            tf = sb("table_f", [1, 6, NB])
            zn = sb("zero_n", [1, NB])

            @block.sync
            def _(sp):
                sp.dma_start(br[:, 0:NG], self.i["b_rg"].partition_broadcast(P)).then_inc(s_b, 16)
                sp.dma_start(br[:, NG:], self.i["b_re"].partition_broadcast(P)).then_inc(s_b, 16)
                sp.wait_ge(s_fill, 1)
                sp.dma_start(self.slotmap.rearrange("(p b) a -> p (b a)", p=P), fill[:]).then_inc(s_init, 16)
                sp.wait_ge(s_sc, 16 * 2 * TT)
                with nc.allow_non_contiguous_dma("slots of a block to the partitions"):
                    sp.dma_start(self.asg[:], self.slotmap.rearrange("(b p) a -> p (b a)", p=P)).then_inc(s_asg, 16)

            @block.gpsimd
            def _(pool):
                g = nc.gpsimd
                g.memset(fill[:], OOB).then_inc(s_fill, 1)
                g.iota(ids[:], pattern=[[1, 2], [2 * P, TT]], base=0, channel_multiplier=2).then_inc(s_ids, 1)
                pool.wait_ge(s_ids, 1)
                pool.wait_ge(s_init, 16)
                pool.wait_ge(s_pos, 1)
                for k in range(2):
                    for t in range(TT):
                        g.indirect_dma_start(out=self.slotmap, out_offset=bass.IndirectOffsetOnAxis(ap=posi[:, k, t:t + 1], axis=0),
                                             in_=ids[:, k, t:t + 1], in_offset=None).then_inc(s_sc, 16)

            @block.scalar
            def _(act):
                act.wait_ge(s_d, 1)
                nc.scalar.activation(gx[:, 1], gx[:, 1], ACT.Exp).then_inc(s_e, 1)
                act.wait_ge(s_d2, 1)
                nc.scalar.activation(eg[:], eg[:], ACT.Exp).then_inc(s_e2, 1)

            @block.tensor
            def _(pe):
                pe.wait_ge(s_A, 1)
                for t in range(TT):
                    for j in range(t + 1):
                        m = nc.tensor.matmul(ps[:, 0, t * E:(t + 1) * E], self.c(C_ONE if j < t else C_US), A[:, j, :], start=j == 0, stop=j == t)
                for j in range(TT):
                    m = nc.tensor.matmul(ps[:, 1, 0:E], self.c(C_ONE), A[:, j, :], start=j == 0, stop=j == TT - 1)
                m.then_inc(s_rank, 1)

            @block.vector
            def _(dve):
                v = nc.vector
                ch = Chain(dve, s_v)
                lk = ch.link
                b3 = lambda ap, n: ap.unsqueeze(2).to_broadcast([P, TT, n])
                im4 = self.c(C_IM99, NG).unsqueeze(1).to_broadcast([P, TT, NG])
                im32 = self.c(C_IM99, E).unsqueeze(1).to_broadcast([P, TT, E])
                dve.wait_ge(s_b, 32)
                lk(v.tensor_tensor(self.lg[:], self.lg[:], br[:].unsqueeze(1).to_broadcast([P, TT, NG + E]), ALU.add))
                g4, e32 = self.lg[:, :, 0:NG], self.lg[:, :, NG:]
                lk(v.tensor_reduce(gm[:], g4, AX, ALU.max))
                lk(v.tensor_tensor(gx[:, 0], g4, b3(gm[:], NG), ALU.is_equal))
                lk(v.tensor_tensor(gx[:, 0], gx[:, 0], im4, ALU.mult))
                lk(v.tensor_reduce(gs[:], gx[:, 0], AX, ALU.min))
                lk(v.tensor_tensor(gx[:, 0], im4, b3(gs[:], NG), ALU.is_equal))
                v.tensor_tensor(gx[:, 1], g4, b3(gm[:], NG), ALU.subtract).then_inc(s_d, 1)
                dve.wait_ge(s_e, 1)
                lk(v.tensor_reduce(gw[:], gx[:, 1], AX, ALU.add))
                lk(v.reciprocal(gw[:], gw[:]))
                lk(v.tensor_scalar(gx[:, 2], gx[:, 0], BIG, -BIG, ALU.mult, ALU.add))
                lk(v.tensor_tensor(em[:].rearrange("p t (g e) -> p t g e", g=NG), e32.rearrange("p t (g e) -> p t g e", g=NG),
                                   gx[:, 2].unsqueeze(3).to_broadcast([P, TT, NG, EG]), ALU.add))
                for k in range(2):
                    lk(v.tensor_reduce(mk[:, k], em[:], AX, ALU.max))
                    lk(v.tensor_tensor(eq[:], em[:], b3(mk[:, k], E), ALU.is_equal))
                    lk(v.tensor_tensor(eq[:], eq[:], im32, ALU.mult))
                    lk(v.tensor_reduce(sel[:], eq[:], AX, ALU.min))
                    lk(v.tensor_tensor(oh[:, k], im32, b3(sel[:], E), ALU.is_equal))
                    if k == 0:
                        lk(v.scalar_tensor_tensor(out=em[:], in0=oh[:, 0], scalar=-100 * BIG, in1=em[:], op0=ALU.mult, op1=ALU.add))
                v.tensor_tensor(A[:], oh[:, 0], oh[:, 1], ALU.add).then_inc(s_A, 1)
                v.tensor_tensor(eg[:], mk[:, 1], mk[:, 0], ALU.subtract).then_inc(s_d2, 1)
                lk(v.memset(zero[:], 0.0))
                lk(v.memset(zn[:], 0.0))
                dve.wait_ge(s_e2, 1)
                lk(v.tensor_scalar_add(sel[:], eg[:], 1.0))
                lk(v.reciprocal(sel[:], sel[:]))
                lk(v.tensor_tensor(self.wts[:, 0], sel[:], gw[:], ALU.mult))
                lk(v.tensor_tensor(self.wts[:, 1], eg[:], self.wts[:, 0], ALU.mult))
                dve.wait_ge(s_rank, 1)
                lk(v.tensor_scalar_add(ci[:], ps[:, 1, 0:E], float(P - 1)))
                lk(v.tensor_scalar(ci[:], ci[:], 7, None, ALU.arith_shift_right))
                lk(v.tensor_copy(nbk[:], ci[:]))
                lk(v.tensor_tensor_scan(bend[:], nbk[:], zero[:], 0.0, ALU.add, ALU.add))
                lk(v.tensor_tensor(bst[:], bend[:], nbk[:], ALU.subtract))
                lk(v.tensor_scalar_mul(bst[:], bst[:], float(P)))
                lk(v.tensor_tensor(em[:], ps[:, 0, 0:TT * E].rearrange("p (t e) -> p t e", e=E), bst[:].unsqueeze(1).to_broadcast([P, TT, E]), ALU.add))
                for k in range(2):
                    lk(v.tensor_tensor(oh[:, k], oh[:, k], em[:], ALU.mult))
                    lk(v.tensor_reduce(pos[:, k], oh[:, k], AX, ALU.add))
                v.tensor_copy(posi[:], pos[:]).then_inc(s_pos, 1)
                io = self.cst[0:1, C_IOTA:C_IOTA + NB]
                lk(v.tensor_tensor(cmp_[:, :, 0:E], bend[0:1, :].unsqueeze(1).to_broadcast([1, NB, E]), io.unsqueeze(2).to_broadcast([1, NB, E]), ALU.is_le))
                lk(v.tensor_reduce(tf[:, 0], cmp_[:, :, 0:E], AX, ALU.add))
                lk(v.tensor_tensor(tf[:, 3, 1:NB], tf[:, 0, 1:NB], tf[:, 0, 0:NB - 1], ALU.not_equal))
                lk(v.memset(tf[:, 3, 0:1], 1.0))
                lk(v.tensor_tensor_scan(tf[:, 1], tf[:, 3], zn[:], 0.0, ALU.add, ALU.add))
                lk(v.tensor_scalar_add(zn[:], tf[:, 1], -2.0))
                lk(v.tensor_tensor(cmp_[:], tf[:, 1].unsqueeze(1).to_broadcast([1, NB, NB]), zn[:].unsqueeze(2).to_broadcast([1, NB, NB]), ALU.is_le))
                lk(v.tensor_reduce(tf[:, 2], cmp_[:], AX, ALU.add))
                lk(v.tensor_scalar_add(tf[:, 2], tf[:, 2], 1.0))
                lk(v.tensor_scalar_mul(tf[:, 5], tf[:, 1], 16.0))
                lk(v.tensor_scalar_min(tf[:, 0], tf[:, 0], float(E - 1)))
                lk(v.tensor_scalar_add(tf[:, 4], zn[:], 0.0))
                lk(v.tensor_copy(tf[:, 4, 0:1], bend[0:1, E - 1:E]))
                lk(v.tensor_copy(self.tbl[:], tf[:]))
                dve.wait_ge(s_asg, 16)
                lk(v.tensor_scalar(self.tok[:], self.asg[:], 1, None, ALU.arith_shift_right))

    def experts(self):
        nc, ps = self.nc, self.ps
        s_w = [self.sem(f"{n}_loaded") for n in ("w_gate", "w_up", "w_down")]
        s_x0, s_xg, s_xt, s_xT, s_G, s_U, s_sg, s_h, s_ht, s_hT, s_Y, s_yd, s_ya, s_out = (self.sem(n) for n in (
            "slots_cleared", "slots_gathered", "x_turned", "xT_copied", "gate_product", "up_product", "gate_silu", "h_ready", "hid_turned", "hidT_ready",
            "down_product", "y_copied_dve", "y_copied_act", "y_scattered"))
        s_yfree = self.sem("y_slots_free")
        wg_d = self.i["w_gate"].rearrange("e (k p) f -> e p k f", p=P)
        wu_d = self.i["w_up"].rearrange("e (k p) f -> e p k f", p=P)
        wd_d = self.i["w_down"].rearrange("e (k p) f -> e p k f", p=P)
        with ExitStack() as x, nc.Block() as block:
            sb = lambda n, s, dt=F32: self.sb(n, s, dt, ctx=x)
            wg, wu = sb("w_gate_sb", [P, 2, KD, FE]), sb("w_up_sb", [P, 2, KD, FE])
            wd = sb("w_down_sb", [P, 2, KF, D])
            xg = sb("x_slots", [P, D])
            xT = sb("x_slotsT", [P, KD, P])
            sg, h = sb("silu_g", [P, FE]), sb("hid", [P, FE])
            hT = sb("hidT", [P, KF, P])
            ys = sb("y_slots", [P, D])
            s_used = (s_G, s_U, s_Y)
            count = lambda eng: eng.value_load(self.tbl[0:1, 4, 0:1], min_val=1, max_val=NB - 1)
            entry = lambda eng, row, b, hi: eng.value_load(self.tbl[0:1, row, bass.ds(b, 1)], min_val=0, max_val=hi)

            @block.sync
            def _(sp):
                n = count(sp)
                with sp.Fori(0, NB) as b:
                    with sp.If(b < n):
                        new = entry(sp, 3, b, 1)
                        with sp.If(new > 0):
                            e = entry(sp, 0, b, E - 1)
                            w = entry(sp, 1, b, E)
                            landed = entry(sp, 5, b, 16 * E)
                            through = entry(sp, 2, b, NB + 1)
                            for j, (src, dst) in enumerate(((wg_d, wg), (wu_d, wu), (wd_d, wd))):
                                sp.wait_ge(s_w[j], landed)
                                sp.wait_ge(s_used[j], through)
                                buf = (w + 2 * (j + 1)) % 2
                                sp.dma_start(dst[:, bass.ds(buf, 1)].rearrange("p a k f -> p (a k) f"),
                                             src[bass.ds(e, 1)].rearrange("a p k f -> p (a k) f")).then_inc(s_w[j], 16)

                sp.dma_start(self.g2[:], self.i["ln2_g"].partition_broadcast(P)).then_inc(self.s_again, 16)
                sp.dma_start(self.b2[:], self.i["ln2_b"].partition_broadcast(P)).then_inc(self.s_again, 16)
                sp.dma_start(self.x1b[:], self.x1d.rearrange("(t p) d -> p t d", p=P)).then_inc(self.s_again, 16)

            @block.gpsimd
            def _(pool):
                g = nc.gpsimd
                n = count(pool)
                tok_end, asg_end = pool.to_reg(T - 1), pool.to_reg(2 * T - 1)

                def gather(b):
                    g.indirect_dma_start(out=xg[:], out_offset=None, in_=self.u2d,
                                         in_offset=bass.IndirectOffsetOnAxis(ap=self.tok[:, b:b + 1], axis=0),
                                         bounds_check=tok_end, oob_is_err=False).then_inc(s_xg, 16)

                def scatter(b):
                    pool.wait_ge(s_yd, b + 2)
                    pool.wait_ge(s_ya, b + 2)
                    g.indirect_dma_start(out=self.ybuf, out_offset=bass.IndirectOffsetOnAxis(ap=self.asg[:, b:b + 1], axis=0),
                                         in_=ys[:], in_offset=None, bounds_check=asg_end, oob_is_err=False).then_inc(s_out, 16)
                    pool.wait_ge(s_out, 16 * (b + 1))
                    pool.sem_inc(s_yfree, 1)

                pool.sem_inc(s_yfree, 1)
                g.memset(xg[:], 0.0).then_inc(s_x0, 1)
                pool.wait_ge(s_x0, 1)
                gather(0)
                for b in range(NB):
                    with pool.If(n > b):
                        pool.wait_ge(s_xt, b + 1)
                        gather(b + 1 if b + 1 < NB else b)
                    if b > 0:
                        with pool.If(n > b - 1):
                            scatter(b - 1)

            @block.tensor
            def _(pe):
                m_ = nc.tensor
                ident = self.c(C_ID)

                def turn():
                    for k in range(KD):
                        m = m_.transpose(ps[:, k // 4, (k % 4) * P:(k % 4 + 1) * P], xg[:, k * P:(k + 1) * P], ident)
                    m.then_inc(s_xt, 1)

                n = count(pe)
                for s in (s_G, s_U, s_Y, s_ht):
                    pe.sem_inc(s, 1)
                for s in s_w:
                    pe.sem_inc(s, 16)
                pe.wait_ge(s_xg, 16)
                turn()
                with pe.Fori(0, NB) as b:
                    with pe.If(b < n):
                        w = entry(pe, 1, b, E)
                        buf = w % 2
                        pe.wait_ge(s_xT, b + 1)
                        for dst, wt, s, s_done, bank in ((s_sg, wg, s_w[0], s_G, 2), (s_h, wu, s_w[1], s_U, 3)):
                            pe.wait_ge(dst, b + 1)
                            pe.wait_ge(s, w * 16 + 16)
                            for k in range(KD):
                                m = m_.matmul(ps[:, bank, :], xT[:, k, :], wt[:, bass.ds(buf, 1), k, :].rearrange("p a f -> p (a f)"),
                                              start=k == 0, stop=k == KD - 1)
                            m.then_inc(s_done, 1)
                        pe.wait_ge(s_xg, b * 16 + 32)
                        turn()
                        pe.wait_ge(s_h, b + 2)
                        for k in range(KF):
                            m = m_.transpose(ps[:, 4, k * P:(k + 1) * P], h[:, k * P:(k + 1) * P], ident)
                        m.then_inc(s_ht, 1)
                        pe.wait_ge(s_hT, b + 1)
                        pe.wait_ge(s_yd, b + 1)
                        pe.wait_ge(s_ya, b + 1)
                        pe.wait_ge(s_w[2], w * 16 + 16)
                        for half in range(2):
                            for k in range(KF):
                                m = m_.matmul(ps[:, 5 + half, :], hT[:, k, :],
                                              wd[:, bass.ds(buf, 1), k, half * 512:half * 512 + 512].rearrange("p a f -> p (a f)"),
                                              start=k == 0, stop=k == KF - 1)
                        m.then_inc(s_Y, 1)

            @block.scalar
            def _(act):
                a = nc.scalar
                n = count(act)
                act.sem_inc(s_sg, 1)
                act.sem_inc(s_ya, 1)
                act.wait_ge(s_xt, 1)
                a.copy(xT[:].rearrange("p k t -> p (k t)"), ps[:, 0:2, :].rearrange("p a b -> p (a b)")).then_inc(s_xT, 1)
                with act.Fori(0, NB) as b:
                    with act.If(b < n):
                        act.wait_ge(s_G, b + 2)
                        act.wait_ge(s_h, b + 1)
                        a.activation(sg[:], ps[:, 2, :], ACT.Silu).then_inc(s_sg, 1)
                        act.wait_ge(s_xt, b + 2)
                        a.copy(xT[:].rearrange("p k t -> p (k t)"), ps[:, 0:2, :].rearrange("p a b -> p (a b)")).then_inc(s_xT, 1)
                        act.wait_ge(s_Y, b + 2)
                        act.wait_ge(s_yfree, b + 1)
                        a.copy(ys[:, 512:], ps[:, 6, :]).then_inc(s_ya, 1)
                act.wait_ge(s_yfree, n + 1)
                a.copy(sg[:, 0:1], ys[:, 0:1])

            @block.vector
            def _(dve):
                v = nc.vector
                n = count(dve)
                dve.sem_inc(s_h, 1)
                dve.sem_inc(s_yd, 1)
                with dve.Fori(0, NB) as b:
                    with dve.If(b < n):
                        dve.wait_ge(s_U, b + 2)
                        dve.wait_ge(s_sg, b + 2)
                        dve.wait_ge(s_ht, b + 1)
                        v.tensor_tensor(h[:], sg[:], ps[:, 3, :], ALU.mult).then_inc(s_h, 1)
                        dve.wait_ge(s_ht, b + 2)
                        v.tensor_copy(hT[:].rearrange("p k t -> p (k t)"), ps[:, 4, :]).then_inc(s_hT, 1)
                        dve.wait_ge(s_Y, b + 2)
                        dve.wait_ge(s_yfree, b + 1)
                        v.tensor_copy(ys[:, 0:512], ps[:, 5, :]).then_inc(s_yd, 1)

    def combine(self):
        nc, mod = self.nc, self.mod
        B = 4
        s_y = [self.sem(f"pair_loaded{j}") for j in range(B)]
        s_sum = self.sem("rows_added")
        s_v, s_var, s_std, s_o = (self.sem(n) for n in ("cb_dve", "varC", "stdC", "out_ready"))
        s_y0, s_fac, s_nrm = self.sem("first_row_weighted"), self.sem("norm_factors"), self.sem("normed")
        s_st = [self.sem(f"out_stored{j}") for j in range(B)]
        yb = self.ybuf.rearrange("(t p k) d -> t p k d", p=P, k=2)
        with ExitStack() as x, nc.Block() as block:
            sb = lambda n, s: self.sb(n, s, ctx=x)
            yt = sb("y_pair", [P, B, 2, D])
            x1, g2, b2 = self.x1b, self.g2, self.b2
            z = sb("z2", [P, B, D])
            st, mv, ve = sb("stC", [P, 2, 6]), sb("mvC", [P, 2]), sb("veC", [P, 2, 3])

            def normed(act, t):
                act.wait_ge(s_fac, t + 1)
                nc.scalar.activation(z[:, t % B], z[:, t % B], ACT.Identity, bias=ve[:, t % 2, 2:3], scale=ve[:, t % 2, 1:2]).then_inc(s_nrm, 1)

            @block.sync
            def _(sp):
                def load(t):
                    sp.dma_start(yt[:, t % B], yb[t]).then_inc(s_y[t % B], 16)

                load(0)
                for t in range(1, B):
                    load(t)
                for t in range(TT):
                    if t + B < TT:
                        sp.wait_ge(s_sum, t + 1)
                        load(t + B)
                    sp.wait_ge(s_o, t + 1)
                    sp.dma_start(self.out[t * P:(t + 1) * P, :], z[:, t % B, :]).then_inc(s_st[t % B], 16)
                for j in range(B):
                    sp.wait_ge(s_st[j], 16 * TT // B)

            @block.scalar
            def _(act):
                a = nc.scalar
                for t in range(TT):
                    b, j = t % B, t % 2
                    act.wait_ge(s_y[b], 16 * (t // B) + 16)
                    if t >= B:
                        act.wait_ge(s_st[b], 16 * (t // B))
                    a.mul(z[:, b], yt[:, b, 0, :], self.wts[:, 0, t:t + 1]).then_inc(s_y0, 1)
                    if t > 0:
                        normed(act, t - 1)
                    act.wait_ge(s_var, t + 1)
                    a.activation(ve[:, j, 1:2], ve[:, j, 0:1], ACT.Sqrt).then_inc(s_std, 1)
                normed(act, TT - 1)

            @block.vector
            def _(dve):
                v = nc.vector
                ch = Chain(dve, s_v)
                def rows(t):
                    b, j = t % B, t % 2
                    zt = z[:, b]
                    dve.wait_ge(s_y0, t + 1)
                    ch.link(v.scalar_tensor_tensor(out=zt, in0=yt[:, b, 1, :], scalar=self.wts[:, 1, t:t + 1], in1=zt, op0=ALU.mult, op1=ALU.add))
                    ch.link(v.tensor_tensor(zt, zt, mod[:, 5, :], ALU.mult))
                    v.scalar_tensor_tensor(out=zt, in0=x1[:, t, :], scalar=ALPHA, in1=zt, op0=ALU.mult, op1=ALU.add).then_inc(s_sum, 1)
                    dve.wait_ge(s_sum, t + 1)
                    ch.link(v.bn_stats(st[:, 0, :], zt[:, 0:512]))
                    ch.link(v.bn_stats(st[:, 1, :], zt[:, 512:1024]))
                    ch.link(v.bn_aggr(mv[:], st[:].rearrange("p a b -> p (a b)")))
                    v.tensor_scalar_add(ve[:, j, 0:1], mv[:, 1:2], LN_EPS).then_inc(s_var, 1)
                    dve.wait_ge(s_std, t + 1)
                    ch.link(v.reciprocal(ve[:, j, 1:2], ve[:, j, 1:2]))
                    v.scalar_tensor_tensor(out=ve[:, j, 2:3], in0=mv[:, 0:1], scalar=-1.0, in1=ve[:, j, 1:2], op0=ALU.mult, op1=ALU.mult).then_inc(s_fac, 1)
                    dve.wait_ge(s_fac, t + 1)

                def gained(t):
                    dve.wait_ge(s_nrm, t + 1)
                    ch.link(v.tensor_tensor(z[:, t % B], z[:, t % B], g2[:], ALU.mult))
                    v.tensor_tensor(z[:, t % B], z[:, t % B], b2[:], ALU.add).then_inc(s_o, 1)

                dve.wait_ge(self.s_again, 48)
                rows(0)
                for t in range(1, TT):
                    rows(t)
                    gained(t - 1)
                gained(TT - 1)



SHAPES = {
    "x": (T, D), "c": (D,), "positions": (T,), "w_ada": (D, 6 * D), "b_ada": (6 * D,), "w_in": (D, 2768), "conv_w": (5, D), "conv_b": (D,),
    "gate_b": (16,), "mh_norm_g": (512,), "q_norm_g": (QL,), "kv_norm_g": (KVL,), "w_uq": (QL, 768), "w_ukv": (KVL, 1024), "attn_norm_g": (512,),
    "w_out": (D, D), "ln1_g": (D,), "ln1_b": (D,), "w_rg": (D, NG), "b_rg": (NG,), "w_re": (D, E), "b_re": (E,),
    "w_gate": (E, D, FE), "w_up": (E, D, FE), "w_down": (E, FE, D), "ln2_g": (D,), "ln2_b": (D,),
}


def kernel(**inputs):
    import concourse.bacc as bacc
    from concourse.bass_utils import run_bass_kernel_spmd

    nc = bacc.Bacc("TRN2", target_bir_lowering=False, num_devices=1)
    arrays = {f"in_{n}": np.ascontiguousarray(inputs[n]).reshape(s) for n, s in SHAPES.items()}
    arrays["in_consts"] = constants()
    ins = {n[3:]: nc.dram_tensor(n, a.shape, mybir.dt.from_np(a.dtype), kind="ExternalInput").ap() for n, a in arrays.items()}
    out = nc.dram_tensor("out_rows", (T, D), F32, kind="ExternalOutput").ap()
    Kernel(nc, ins, out).build()
    r = run_bass_kernel_spmd(nc, [arrays], core_ids=[0])
    return r.results[0]["out_rows"].reshape(1, T, D)
```
